# Optimizing a Trainium2 kernel written in Bass

```python
import jax, jax.numpy as jnp
from jax import lax
import numpy as np
import math

D_MODEL = 2048
BATCH = 1
SEQ = 256
DEPTH = 1

CHUNK = 64
Q_BLOCK = 2 * CHUNK
MIX_WIDTH = D_MODEL
ATTN_WIDTH = MIX_WIDTH // 2
ATTN_HEADS = 8
ATTN_HEAD_DIM = ATTN_WIDTH // ATTN_HEADS
LRU_WIDTH = MIX_WIDTH - ATTN_WIDTH
LRU_BLOCKS = 8
LRU_BLOCK_DIM = LRU_WIDTH // LRU_BLOCKS
CONV_WIDTH = 4
LRU_C = 8.0
OFF_Q = 0
OFF_K = OFF_Q + ATTN_WIDTH
OFF_V = OFF_K + ATTN_WIDTH
OFF_F = OFF_V + ATTN_WIDTH
OFF_LX = OFF_F + ATTN_HEADS
OFF_LY = OFF_LX + LRU_WIDTH
IN_COLS = OFF_LY + LRU_WIDTH
PEER_HEADS = 8
PEER_N_KEYS = 128
PEER_N_EXPERTS = PEER_N_KEYS * PEER_N_KEYS
PEER_QUERY_DIM = 256
PEER_HALF = PEER_QUERY_DIM // 2
PEER_TOPK = 16
PEER_TOKEN_BLOCK = 128
N_ADA = 6
EPS = 1e-6


def _rmsnorm(x, g):
    xf = x.astype(jnp.float32)
    y = xf * lax.rsqrt(jnp.mean(xf * xf, axis=-1, keepdims=True) + EPS)
    return y.astype(x.dtype) * g

def _forgetting_attention(q, k, v, log_f):
    n_blocks = q.shape[2] // Q_BLOCK
    cum = jnp.cumsum(log_f, axis=-1)
    scale = ATTN_HEAD_DIM ** -0.5
    outs = []
    for blk in range(n_blocks):
        start = blk * Q_BLOCK
        end = start + Q_BLOCK
        qb = q[:, :, start:end]
        kb = k[:, :, :end]
        vb = v[:, :, :end]
        logits = jnp.einsum('bhqd,bhkd->bhqk', qb, kb).astype(jnp.float32) * scale
        logits = logits + cum[:, :, start:end, None] - cum[:, :, None, :end]
        mask = jnp.arange(end)[None, :] <= (start + jnp.arange(Q_BLOCK))[:, None]
        logits = jnp.where(mask, logits, -jnp.inf)
        p = jax.nn.softmax(logits, axis=-1)
        outs.append(jnp.einsum('bhqk,bhkd->bhqd', p.astype(v.dtype), vb))
    return jnp.concatenate(outs, axis=2)

def _causal_depthwise_conv(x, w, b):
    y = lax.conv_general_dilated(
        x, w[:, None, :], window_strides=(1,), padding=[(CONV_WIDTH - 1, 0)],
        dimension_numbers=('NWC', 'WIO', 'NWC'), feature_group_count=x.shape[-1])
    return y + b

def _rg_lru(xc, w_a, b_a, w_x, b_x, lam):
    B, S, _ = xc.shape
    xb = xc.reshape(B, S, LRU_BLOCKS, LRU_BLOCK_DIM)
    r = jax.nn.sigmoid(jnp.einsum('bsni,nij->bsnj', xb, w_a).reshape(B, S, LRU_WIDTH) + b_a)
    i = jax.nn.sigmoid(jnp.einsum('bsni,nij->bsnj', xb, w_x).reshape(B, S, LRU_WIDTH) + b_x)
    log_a = -LRU_C * r.astype(jnp.float32) * jax.nn.softplus(-lam.astype(jnp.float32))
    a = jnp.exp(log_a)
    bterm = jnp.sqrt(-jnp.expm1(2.0 * log_a)) * (i * xc).astype(jnp.float32)

    def combine(lhs, rhs):
        a1, b1 = lhs
        a2, b2 = rhs
        return a1 * a2, a2 * b1 + b2

    _, h = lax.associative_scan(combine, (a, bterm), axis=1)
    return h.astype(xc.dtype)

def _hybrid_mixer(h, w_in, b_f, conv_w, conv_b, lru_w_a, lru_b_a, lru_w_x, lru_b_x,
                  lru_lambda, g_attn_out, g_lru_out, w_out):
    B, S, _ = h.shape
    proj = h @ w_in

    def heads(t):
        return t.reshape(B, S, ATTN_HEADS, ATTN_HEAD_DIM).transpose(0, 2, 1, 3)

    q = heads(proj[..., OFF_Q:OFF_K])
    k = heads(proj[..., OFF_K:OFF_V])
    v = heads(proj[..., OFF_V:OFF_F])
    f_logit = (proj[..., OFF_F:OFF_LX] + b_f).astype(jnp.float32)
    log_f = jax.nn.log_sigmoid(f_logit).transpose(0, 2, 1)
    attn = _forgetting_attention(q, k, v, log_f)
    attn = attn.transpose(0, 2, 1, 3).reshape(B, S, ATTN_WIDTH)

    lx = proj[..., OFF_LX:OFF_LY]
    ly = proj[..., OFF_LY:IN_COLS]
    xc = _causal_depthwise_conv(lx, conv_w, conv_b)
    lru = _rg_lru(xc, lru_w_a, lru_b_a, lru_w_x, lru_b_x, lru_lambda) * jax.nn.gelu(ly)

    merged = jnp.concatenate([_rmsnorm(attn, g_attn_out), _rmsnorm(lru, g_lru_out)], axis=-1)
    return merged @ w_out

def _peer(h, w_q, k1, k2, u, vt):
    B, S, D = h.shape
    q = (h @ w_q).reshape(B, S, PEER_HEADS, 2, PEER_HALF)
    s1 = jnp.einsum('bshd,hnd->bshn', q[..., 0, :], k1).astype(jnp.float32)
    s2 = jnp.einsum('bshd,hnd->bshn', q[..., 1, :], k2).astype(jnp.float32)
    v1, i1 = lax.top_k(s1, PEER_TOPK)
    v2, i2 = lax.top_k(s2, PEER_TOPK)
    cand = (v1[..., :, None] + v2[..., None, :]).reshape(B, S, PEER_HEADS, PEER_TOPK * PEER_TOPK)
    vs, ic = lax.top_k(cand, PEER_TOPK)
    e = (jnp.take_along_axis(i1, ic // PEER_TOPK, axis=-1) * PEER_N_KEYS
         + jnp.take_along_axis(i2, ic % PEER_TOPK, axis=-1))
    w = jax.nn.softmax(vs, axis=-1).astype(h.dtype)

    nb = (B * S) // PEER_TOKEN_BLOCK
    hb = h.reshape(nb, PEER_TOKEN_BLOCK, D)
    eb = e.reshape(nb, PEER_TOKEN_BLOCK, PEER_HEADS, PEER_TOPK)
    wb = w.reshape(nb, PEER_TOKEN_BLOCK, PEER_HEADS, PEER_TOPK)

    def expert_block(args):
        hx, ex, wx = args
        ug = jnp.take(u, ex, axis=0)
        act = jax.nn.gelu(jnp.einsum('thkd,td->thk', ug, hx)) * wx
        vg = jnp.take(vt, ex, axis=0)
        return jnp.einsum('thk,thkd->td', act, vg)

    y = lax.map(expert_block, (hb, eb, wb))
    return y.reshape(B, S, D)

def first_inputs(seed: int = 0) -> dict:
    key = jax.random.key(seed)
    ks = jax.random.split(key, 26)
    f32 = jnp.float32
    L, D = DEPTH, D_MODEL

    def nrm(k, shape, scale):
        return jax.random.normal(k, shape, f32) * scale

    a0 = jax.random.uniform(ks[12], (L, LRU_WIDTH), f32, 0.9, 0.999) ** (1.0 / LRU_C)
    return {
        'x': nrm(ks[0], (BATCH, SEQ, D), 1.0),
        'c': nrm(ks[1], (BATCH, D), 1.0),
        'w_ada': nrm(ks[2], (L, D, N_ADA * D), 0.5 * D ** -0.5),
        'b_ada': nrm(ks[3], (L, N_ADA * D), 0.01),
        'g_mix': 1.0 + nrm(ks[4], (L, D), 0.05),
        'w_in': nrm(ks[5], (L, D, IN_COLS), D ** -0.5),
        'b_f': jax.random.uniform(ks[6], (L, ATTN_HEADS), f32, 1.0, 4.0),
        'conv_w': nrm(ks[7], (L, CONV_WIDTH, LRU_WIDTH), CONV_WIDTH ** -0.5),
        'conv_b': nrm(ks[8], (L, LRU_WIDTH), 0.01),
        'lru_w_a': nrm(ks[9], (L, LRU_BLOCKS, LRU_BLOCK_DIM, LRU_BLOCK_DIM), LRU_BLOCK_DIM ** -0.5),
        'lru_b_a': nrm(ks[10], (L, LRU_WIDTH), 0.01),
        'lru_w_x': nrm(ks[11], (L, LRU_BLOCKS, LRU_BLOCK_DIM, LRU_BLOCK_DIM), LRU_BLOCK_DIM ** -0.5),
        'lru_b_x': nrm(ks[13], (L, LRU_WIDTH), 0.01),
        'lru_lambda': jnp.log(a0) - jnp.log1p(-a0),
        'g_attn_out': 1.0 + nrm(ks[14], (L, ATTN_WIDTH), 0.05),
        'g_lru_out': 1.0 + nrm(ks[15], (L, LRU_WIDTH), 0.05),
        'w_out': nrm(ks[16], (L, MIX_WIDTH, D), MIX_WIDTH ** -0.5),
        'g_ffn': 1.0 + nrm(ks[17], (L, D), 0.05),
        'peer_w_q': nrm(ks[18], (L, D, PEER_HEADS * PEER_QUERY_DIM), D ** -0.5),
        'peer_k1': nrm(ks[19], (L, PEER_HEADS, PEER_N_KEYS, PEER_HALF), PEER_HALF ** -0.5),
        'peer_k2': nrm(ks[20], (L, PEER_HEADS, PEER_N_KEYS, PEER_HALF), PEER_HALF ** -0.5),
        'peer_u': nrm(ks[21], (L, PEER_N_EXPERTS, D), D ** -0.5),
        'peer_v': nrm(ks[22], (L, PEER_N_EXPERTS, D), 1.0),
        'g_final': 1.0 + nrm(ks[23], (D,), 0.05),
    }

def first_block(x, c, w_ada, b_ada, g_mix, w_in, b_f, conv_w, conv_b, lru_w_a, lru_b_a,
              lru_w_x, lru_b_x, lru_lambda, g_attn_out, g_lru_out, w_out, g_ffn,
              peer_w_q, peer_k1, peer_k2, peer_u, peer_v, g_final):
    sc = jax.nn.silu(c)
    for l in range(DEPTH):
        mod = sc @ w_ada[l] + b_ada[l]
        sh1, sc1, ga1, sh2, sc2, ga2 = jnp.split(mod, N_ADA, axis=-1)
        h = _rmsnorm(x, g_mix[l]) * (1.0 + sc1[:, None, :]) + sh1[:, None, :]
        mix = _hybrid_mixer(h, w_in[l], b_f[l], conv_w[l], conv_b[l], lru_w_a[l], lru_b_a[l],
                            lru_w_x[l], lru_b_x[l], lru_lambda[l], g_attn_out[l],
                            g_lru_out[l], w_out[l])
        x = x + ga1[:, None, :] * mix
        h = _rmsnorm(x, g_ffn[l]) * (1.0 + sc2[:, None, :]) + sh2[:, None, :]
        x = x + ga2[:, None, :] * _peer(h, peer_w_q[l], peer_k1[l], peer_k2[l], peer_u[l], peer_v[l])
    return _rmsnorm(x, g_final)


DEPTH_2 = 2

N_A = DEPTH_2 // 2
N_B = DEPTH_2 - N_A
SSM_WIDTH = D_MODEL
SSM_GROUP = 16
SSM_GROUPS = SSM_WIDTH // SSM_GROUP
SSM_STATE = 64
N_HEADS = 16
N_KV = 4
HPG = N_HEADS // N_KV
HEAD_DIM = D_MODEL // N_HEADS
ATT_WIDTH = N_HEADS * HEAD_DIM
N_BRANCH = 3
CMP_LEN = 32
CMP_STRIDE = 16
SEL_LEN = 64
SEL_TOPK = 16
WINDOW = 512
WIN_QBLOCK = 128
SEL_QCHUNK = 32
SEL_BONUS = 1e3
NEG = -1e30


def rmsnorm(x, g):
    xf = x.astype(jnp.float32)
    y = xf * lax.rsqrt(jnp.mean(xf * xf, axis=-1, keepdims=True) + EPS)
    return (y * g.astype(jnp.float32)).astype(x.dtype)

def modulate(h, shift, scale):
    return h * (1.0 + scale[:, None, :]) + shift[:, None, :]

def masked_softmax(s, mask):
    s = jnp.where(mask, s.astype(jnp.float32), NEG)
    p = jax.nn.softmax(s, axis=-1)
    return jnp.where(mask, p, 0.0)

def s5_discretize(lam_re, lam_im, log_step, b_re, b_im):
    dt = jnp.exp(log_step.astype(jnp.float32))[:, None]
    lr, li = lam_re.astype(jnp.float32), lam_im.astype(jnp.float32)
    mag = jnp.exp(lr * dt)
    a_re, a_im = mag * jnp.cos(li * dt), mag * jnp.sin(li * dt)
    den = lr * lr + li * li
    coef_re = ((a_re - 1.0) * lr + a_im * li) / den
    coef_im = (a_im * lr - (a_re - 1.0) * li) / den
    br, bi = b_re.astype(jnp.float32), b_im.astype(jnp.float32)
    bb_re = coef_re[..., None] * br - coef_im[..., None] * bi
    bb_im = coef_re[..., None] * bi + coef_im[..., None] * br
    return a_re, a_im, bb_re, bb_im

def _ssm_combine(left, right):
    ar_i, ai_i, br_i, bi_i = left
    ar_j, ai_j, br_j, bi_j = right
    return (ar_j * ar_i - ai_j * ai_i,
            ar_j * ai_i + ai_j * ar_i,
            ar_j * br_i - ai_j * bi_i + br_j,
            ar_j * bi_i + ai_j * br_i + bi_j)

def _scan_one(a_re, a_im, bu_re, bu_im):
    out = lax.associative_scan(_ssm_combine, (a_re, a_im, bu_re, bu_im), axis=0)
    return out[2], out[3]

def s5_mixer(h, w_in, lam_re, lam_im, log_step, b_re, b_im, c_re, c_im, d_skip, w_glu, b_glu, w_out):
    B_, L, _ = h.shape
    u, z = jnp.split(h @ w_in, 2, axis=-1)
    ug = u.reshape(B_, L, SSM_GROUPS, SSM_GROUP).astype(jnp.float32)
    a_re, a_im, bb_re, bb_im = s5_discretize(lam_re, lam_im, log_step, b_re, b_im)
    bu_re = jnp.einsum('blgc,gnc->blgn', ug, bb_re)
    bu_im = jnp.einsum('blgc,gnc->blgn', ug, bb_im)
    shp = (L, SSM_GROUPS, SSM_STATE)
    x_re, x_im = jax.vmap(_scan_one, in_axes=(None, None, 0, 0))(
        jnp.broadcast_to(a_re, shp), jnp.broadcast_to(a_im, shp), bu_re, bu_im)
    y = (jnp.einsum('blgn,gcn->blgc', x_re, c_re.astype(jnp.float32))
         - jnp.einsum('blgn,gcn->blgc', x_im, c_im.astype(jnp.float32)))
    y = y + d_skip.astype(jnp.float32).reshape(SSM_GROUPS, SSM_GROUP) * ug
    y = jax.nn.gelu(y.reshape(B_, L, SSM_WIDTH).astype(h.dtype))
    y = y * jax.nn.sigmoid(y @ w_glu + b_glu)
    return (y * jax.nn.silu(z)) @ w_out

def compress_blocks(t, blk_idx, pe, w1, b1, w2, b2):
    blocks = t[:, blk_idx] + pe[None, None, :, None, :]
    B_, n = blocks.shape[:2]
    flat = jnp.moveaxis(blocks, 3, 2).reshape(B_, n, N_KV, CMP_LEN * HEAD_DIM)
    return jax.nn.gelu(flat @ w1 + b1) @ w2 + b2

def nsa_shared_kv(h_kv, w_kv, cmp_pe, cmp_w1, cmp_b1, cmp_w2, cmp_b2):
    B_, L, _ = h_kv.shape
    kv = (h_kv @ w_kv).reshape(B_, L, 2 * N_BRANCH, N_KV, HEAD_DIM)
    n_cmp = (L - CMP_LEN) // CMP_STRIDE + 1
    blk_idx = np.arange(n_cmp)[:, None] * CMP_STRIDE + np.arange(CMP_LEN)[None, :]
    kc = compress_blocks(kv[:, :, 0], blk_idx, cmp_pe[0], cmp_w1[0], cmp_b1[0], cmp_w2[0], cmp_b2[0])
    vc = compress_blocks(kv[:, :, 1], blk_idx, cmp_pe[1], cmp_w1[1], cmp_b1[1], cmp_w2[1], cmp_b2[1])
    return kc, vc, kv[:, :, 2], kv[:, :, 3], kv[:, :, 4], kv[:, :, 5]

def cmp_attention(q, kc, vc, pos):
    n_cmp = kc.shape[1]
    s = jnp.einsum('blghd,bngd->bghln', q, kc)
    blk_end = jnp.arange(n_cmp) * CMP_STRIDE + CMP_LEN - 1
    mask = blk_end[None, :] <= pos[:, None]
    p = masked_softmax(s, mask)
    o = jnp.einsum('bghln,bngd->blghd', p.astype(vc.dtype), vc)
    return o, p.sum(axis=2)

def selection_overlap(n_cmp, n_slc):
    c0 = np.arange(n_cmp)[:, None] * CMP_STRIDE
    s0 = np.arange(n_slc)[None, :] * SEL_LEN
    ov = np.clip(np.minimum(c0 + CMP_LEN, s0 + SEL_LEN) - np.maximum(c0, s0), 0, None)
    return (ov / CMP_STRIDE).astype(np.float32)

def select_blocks(p_cmp, pos):
    n_cmp = p_cmp.shape[-1]
    n_slc = pos.shape[0] // SEL_LEN
    p_slc = jnp.einsum('bgln,ns->bgls', p_cmp, jnp.asarray(selection_overlap(n_cmp, n_slc)))
    blk = jnp.arange(n_slc)[None, :]
    cur = (pos // SEL_LEN)[:, None]
    valid = blk <= cur
    forced = ((blk == 0) | (blk == cur) | (blk == cur - 1)).astype(jnp.float32)
    score = jnp.where(valid, p_slc + SEL_BONUS * forced, -SEL_BONUS)
    top, idx = lax.top_k(score, min(SEL_TOPK, n_slc))
    return idx, top > -0.5 * SEL_BONUS

def selected_attention(q, ks, vs, idx, ok):
    B_, L = q.shape[:2]
    n_slc = L // SEL_LEN
    n_ch = L // SEL_QCHUNK
    kb = jnp.moveaxis(ks.reshape(B_, n_slc, SEL_LEN, N_KV, HEAD_DIM), 3, 1)
    vb = jnp.moveaxis(vs.reshape(B_, n_slc, SEL_LEN, N_KV, HEAD_DIM), 3, 1)
    q_ch = jnp.moveaxis(q.reshape(B_, n_ch, SEL_QCHUNK, N_KV, HPG, HEAD_DIM), 1, 0)
    idx_ch = jnp.moveaxis(idx.reshape(B_, N_KV, n_ch, SEL_QCHUNK, -1), 2, 0)
    ok_ch = jnp.moveaxis(ok.reshape(B_, N_KV, n_ch, SEL_QCHUNK, -1), 2, 0)
    gather = jax.vmap(jax.vmap(lambda blocks, ix: blocks[ix]))
    offs = jnp.arange(SEL_LEN)

    def chunk(args):
        ci, qc, ic, oc = args
        t = ci * SEL_QCHUNK + jnp.arange(SEL_QCHUNK)
        kg = gather(kb, ic)
        vg = gather(vb, ic)
        s = jnp.einsum('bqghd,bgqksd->bgqhks', qc, kg)
        kpos = ic[..., None] * SEL_LEN + offs
        mask = (oc[..., None] & (kpos <= t[None, None, :, None, None]))[:, :, :, None]
        p = masked_softmax(s.reshape(*s.shape[:4], -1), mask.reshape(*mask.shape[:4], -1))
        p = p.reshape(s.shape).astype(vg.dtype)
        return jnp.einsum('bgqhks,bgqksd->bqghd', p, vg)

    o = lax.map(chunk, (jnp.arange(n_ch), q_ch, idx_ch, ok_ch))
    return jnp.moveaxis(o, 0, 1).reshape(B_, L, N_KV, HPG, HEAD_DIM)

def window_attention(q, kw, vw):
    B_, L = q.shape[:2]
    nb = L // WIN_QBLOCK
    span = WIN_QBLOCK + WINDOW
    pad = ((0, 0), (WINDOW, 0), (0, 0), (0, 0))
    kp, vp = jnp.pad(kw, pad), jnp.pad(vw, pad)
    q_blk = jnp.moveaxis(q.reshape(B_, nb, WIN_QBLOCK, N_KV, HPG, HEAD_DIM), 1, 0)
    koff = np.arange(span) - WINDOW
    rel = np.arange(WIN_QBLOCK)[:, None] - koff[None, :]
    band = (rel >= 0) & (rel < WINDOW)

    def block(args):
        bi, qb = args
        start = bi * WIN_QBLOCK
        kb = lax.dynamic_slice_in_dim(kp, start, span, axis=1)
        vb = lax.dynamic_slice_in_dim(vp, start, span, axis=1)
        mask = band & ((start + koff) >= 0)[None, :]
        s = jnp.einsum('bqghd,bkgd->bghqk', qb, kb)
        p = masked_softmax(s, mask).astype(vb.dtype)
        return jnp.einsum('bghqk,bkgd->bqghd', p, vb)

    o = lax.map(block, (jnp.arange(nb), q_blk))
    return jnp.moveaxis(o, 0, 1).reshape(B_, L, N_KV, HPG, HEAD_DIM)

def nsa_mixer(h, w_qg, w_o, kc, vc, ks, vs, kw, vw):
    B_, L, _ = h.shape
    proj = h @ w_qg
    q = proj[..., :ATT_WIDTH].reshape(B_, L, N_KV, HPG, HEAD_DIM) * (HEAD_DIM ** -0.5)
    g_end = ATT_WIDTH + N_BRANCH * N_HEADS
    gates = jax.nn.sigmoid(proj[..., ATT_WIDTH:g_end].astype(jnp.float32)).astype(h.dtype)
    gates = gates.reshape(B_, L, N_BRANCH, N_KV, HPG, 1)
    z = proj[..., g_end:].reshape(B_, L, N_BRANCH, N_KV, HPG, HEAD_DIM)
    pos = jnp.arange(L)
    o_cmp, p_cmp = cmp_attention(q, kc, vc, pos)
    idx, ok = select_blocks(p_cmp, pos)
    o_sel = selected_attention(q, ks, vs, idx, ok)
    o_win = window_attention(q, kw, vw)
    o_br = jnp.stack([o_cmp, o_sel, o_win], axis=2)
    o = jnp.sum(gates * jax.nn.silu(z) * o_br, axis=2)
    return o.reshape(B_, L, ATT_WIDTH) @ w_o

def second_inputs(seed: int = 0) -> dict:
    key = jax.random.key(seed)
    keys = list(jax.random.split(key, 40))

    def nrm(shape, s):
        return s * jax.random.normal(keys.pop(), shape, jnp.float32)

    D, E, G, N = D_MODEL, SSM_WIDTH, SSM_GROUPS, SSM_STATE
    qg_cols = ATT_WIDTH + N_BRANCH * N_HEADS + N_BRANCH * ATT_WIDTH
    lam_im0 = jnp.pi * jnp.arange(N, dtype=jnp.float32)
    return {
        "x": nrm((BATCH, SEQ, D), 1.0),
        "c": nrm((BATCH, D), 1.0),
        "norm_g": 1.0 + nrm((DEPTH_2, D), 0.02),
        "mod_w": nrm((DEPTH_2, D, 3 * D), 0.5 * D ** -0.5),
        "mod_b": nrm((DEPTH_2, 3 * D), 0.01),
        "ssm_w_in": nrm((N_A, D, 2 * E), D ** -0.5),
        "ssm_lam_re": -0.5 + nrm((N_A, G, N), 0.01),
        "ssm_lam_im": lam_im0 + nrm((N_A, G, N), 0.01),
        "ssm_log_step": jax.random.uniform(keys.pop(), (N_A, G), jnp.float32, math.log(1e-3), math.log(1e-1)),
        "ssm_b_re": nrm((N_A, G, N, SSM_GROUP), (2 * SSM_GROUP) ** -0.5),
        "ssm_b_im": nrm((N_A, G, N, SSM_GROUP), (2 * SSM_GROUP) ** -0.5),
        "ssm_c_re": nrm((N_A, G, SSM_GROUP, N), 0.5),
        "ssm_c_im": nrm((N_A, G, SSM_GROUP, N), 0.5),
        "ssm_d": nrm((N_A, E), 1.0),
        "ssm_w_glu": nrm((N_A, E, E), E ** -0.5),
        "ssm_b_glu": nrm((N_A, E), 0.01),
        "ssm_w_out": nrm((N_A, E, D), E ** -0.5),
        "kv_norm_g": 1.0 + nrm((D,), 0.02),
        "kv_mod_w": nrm((D, 2 * D), 0.5 * D ** -0.5),
        "kv_mod_b": nrm((2 * D,), 0.01),
        "w_kv": nrm((D, 2 * N_BRANCH * N_KV * HEAD_DIM), D ** -0.5),
        "cmp_pe": nrm((2, CMP_LEN, HEAD_DIM), 0.02),
        "cmp_w1": nrm((2, CMP_LEN * HEAD_DIM, HEAD_DIM), (CMP_LEN * HEAD_DIM) ** -0.5),
        "cmp_b1": nrm((2, HEAD_DIM), 0.01),
        "cmp_w2": nrm((2, HEAD_DIM, HEAD_DIM), HEAD_DIM ** -0.5),
        "cmp_b2": nrm((2, HEAD_DIM), 0.01),
        "nsa_w_qg": nrm((N_B, D, qg_cols), D ** -0.5),
        "nsa_w_o": nrm((N_B, ATT_WIDTH, D), ATT_WIDTH ** -0.5),
        "final_norm_g": 1.0 + nrm((D,), 0.02),
    }

def second_block(x, c, norm_g, mod_w, mod_b, ssm_w_in, ssm_lam_re, ssm_lam_im, ssm_log_step,
              ssm_b_re, ssm_b_im, ssm_c_re, ssm_c_im, ssm_d, ssm_w_glu, ssm_b_glu, ssm_w_out,
              kv_norm_g, kv_mod_w, kv_mod_b, w_kv, cmp_pe, cmp_w1, cmp_b1, cmp_w2, cmp_b2,
              nsa_w_qg, nsa_w_o, final_norm_g):
    c_act = jax.nn.silu(c)
    shared = None
    for layer in range(DEPTH_2):
        if layer == N_A:
            kv_shift, kv_scale = jnp.split(c_act @ kv_mod_w + kv_mod_b, 2, axis=-1)
            h_kv = modulate(rmsnorm(x, kv_norm_g), kv_shift, kv_scale)
            shared = nsa_shared_kv(h_kv, w_kv, cmp_pe, cmp_w1, cmp_b1, cmp_w2, cmp_b2)
        shift, scale, gate = jnp.split(c_act @ mod_w[layer] + mod_b[layer], 3, axis=-1)
        h = modulate(rmsnorm(x, norm_g[layer]), shift, scale)
        if layer < N_A:
            out = s5_mixer(h, ssm_w_in[layer], ssm_lam_re[layer], ssm_lam_im[layer],
                           ssm_log_step[layer], ssm_b_re[layer], ssm_b_im[layer],
                           ssm_c_re[layer], ssm_c_im[layer], ssm_d[layer],
                           ssm_w_glu[layer], ssm_b_glu[layer], ssm_w_out[layer])
        else:
            j = layer - N_A
            out = nsa_mixer(h, nsa_w_qg[j], nsa_w_o[j], *shared)
        x = x + gate[:, None, :] * out
    return rmsnorm(x, final_norm_g)


def setup_inputs(seed=0):
    out = dict(first_inputs(seed))
    for name, value in second_inputs(seed + 1).items():
        if name != "x":
            out[name + "_2"] = value
    return out


def reference(
    x, c, w_ada, b_ada, g_mix, w_in, b_f, conv_w, conv_b, lru_w_a, lru_b_a, lru_w_x, lru_b_x,
    lru_lambda, g_attn_out, g_lru_out, w_out, g_ffn, peer_w_q, peer_k1, peer_k2, peer_u, peer_v,
    g_final, c_2, norm_g_2, mod_w_2, mod_b_2, ssm_w_in_2, ssm_lam_re_2, ssm_lam_im_2,
    ssm_log_step_2, ssm_b_re_2, ssm_b_im_2, ssm_c_re_2, ssm_c_im_2, ssm_d_2, ssm_w_glu_2,
    ssm_b_glu_2, ssm_w_out_2, kv_norm_g_2, kv_mod_w_2, kv_mod_b_2, w_kv_2, cmp_pe_2, cmp_w1_2,
    cmp_b1_2, cmp_w2_2, cmp_b2_2, nsa_w_qg_2, nsa_w_o_2, final_norm_g_2,
):
    x = first_block(
        x, c, w_ada, b_ada, g_mix, w_in, b_f, conv_w, conv_b, lru_w_a, lru_b_a, lru_w_x,
        lru_b_x, lru_lambda, g_attn_out, g_lru_out, w_out, g_ffn, peer_w_q, peer_k1, peer_k2,
        peer_u, peer_v, g_final,
    )
    return second_block(
        x, c_2, norm_g_2, mod_w_2, mod_b_2, ssm_w_in_2, ssm_lam_re_2, ssm_lam_im_2,
        ssm_log_step_2, ssm_b_re_2, ssm_b_im_2, ssm_c_re_2, ssm_c_im_2, ssm_d_2, ssm_w_glu_2,
        ssm_b_glu_2, ssm_w_out_2, kv_norm_g_2, kv_mod_w_2, kv_mod_b_2, w_kv_2, cmp_pe_2,
        cmp_w1_2, cmp_b1_2, cmp_w2_2, cmp_b2_2, nsa_w_qg_2, nsa_w_o_2, final_norm_g_2,
    )


_drawn_inputs = setup_inputs


def setup_inputs(seed=0):
    import zlib

    import numpy as np

    out = dict(_drawn_inputs(seed))
    spreads = {}
    factors = {'conv_b': 3.9,
     'lru_b_a': 8.0,
     'lru_b_x': 8.0,
     'g_attn_out': 2.811,
     'norm_g_2': 8.0,
     'mod_b_2': 8.0,
     'ssm_lam_re_2': 8.0,
     'ssm_b_re_2': 2.834,
     'ssm_b_im_2': 2.784,
     'ssm_c_re_2': 2.868,
     'ssm_c_im_2': 2.815,
     'ssm_b_glu_2': 8.0,
     'kv_norm_g_2': 8.0,
     'kv_mod_b_2': 8.0,
     'cmp_pe_2': 23.472,
     'cmp_b1_2': 39.889,
     'cmp_b2_2': 64.0,
     'final_norm_g_2': 8.179}
    for name, (base, spread) in spreads.items():
        noise = np.random.default_rng([zlib.crc32(name.encode()), seed]).standard_normal(out[name].shape)
        drawn = base * np.exp(spread * noise) if base else spread * noise
        out[name] = __import__('jax').numpy.asarray(drawn.astype(out[name].dtype))
    for name, factor in factors.items():
        out[name] = (out[name] * factor).astype(out[name].dtype)
    return out
```

```python
import concourse.bass as bass
from concourse import mybir
from contextlib import ExitStack
import numpy as np

F32 = mybir.dt.float32
U32 = mybir.dt.uint32
I32 = mybir.dt.int32
ALU = mybir.AluOpType
ACT = mybir.ActivationFunctionType
AX = mybir.AxisListType.X

P = 128
T = 256
D = 2048
KT = D // P
R = 8
HEADS = 8
SCALE = float(P) ** -0.5
EPS = 1e-6
NEG = -1e30
LOW = -3.0e38
LRU_C = 8.0
TOPK = 16
SLOTS = HEADS * TOPK
NQ = 4
QW = P // NQ
KV = 4
HPG = 4
NCMP = (T - 32) // 16 + 1
CMP_L = 32
PAIRS = 64
MAGIC = 12582912.0
TWO_PI = 6.283185
HALF_PI = 1.5707963

STREAM = [("shift_scale", 32), ("heads", 64), ("ada_rest", 40), ("w_out", 16), ("topk", 64),
          ("spread", 32), ("peer", 256), ("between", 16), ("ssm", 64), ("glu", 16), ("ssm_out", 16),
          ("kv", 24), ("nsa", 64), ("w_o", 16)]
BASE = {}
for _name, _n in STREAM:
    BASE[_name] = sum(n for m, n in STREAM if m in BASE)

VEC = [("c", 16), ("c2", 16), ("b_ada", 96), ("b_mod2", 128), ("g_mix", 16), ("g_ffn", 16),
       ("g_final", 16), ("g_merge", 16), ("g_l0", 16), ("g_l1", 16), ("g_kv", 16), ("g_final2", 16),
       ("conv_w", 32), ("conv_b", 8), ("lru_b_a", 8), ("lru_b_x", 8), ("lru_lambda", 8), ("ssm_d", 16),
       ("b_glu", 16), ("cmp_b1", 2), ("cmp_b2", 2), ("cmp_pe", 64), ("lam_re", 64), ("lam_im", 64)]
VOFF = {}
for _name, _n in VEC:
    VOFF[_name] = sum(n for m, n in VEC if m in VOFF)
NVEC = sum(n for _, n in VEC)


def build(nc, a, debug=None):
    ctx = ExitStack()
    with ctx:
        def sb(name, shape, dt=F32):
            return ctx.enter_context(nc.sbuf_tensor(name, shape, dt))

        def sem(name):
            return ctx.enter_context(nc.semaphore(name))

        ring = sb("ring", [P, R, KT, P])
        x = sb("x", [P, KT, T])
        H = sb("H", [P, KT, T])
        vec = sb("vec", [P, NVEC])
        mod = sb("mod", [P, 224])
        gain = sb("gain", [P, 8, KT])
        cond = sb("cond", [P, 2, KT])
        cst = sb("cst", [P, 2])
        ident = sb("ident", [P, P])
        ones = sb("ones", [P, T])
        iota = sb("iota", [P, P])
        iota_t = sb("iota_t", [P, T])
        causal = sb("causal", [P, P])
        cmp_neg = sb("cmp_neg", [P, 2, NCMP])
        cmp_one = sb("cmp_one", [P, 2, NCMP])
        in16 = sb("in16", [P, 8])
        par16 = sb("par16", [P, 2])
        in64 = sb("in64", [P, 2])
        itmp = sb("itmp", [P, T], I32)
        var = sb("var", [P, 2, T])
        sd = sb("sd", [P, 2, T])
        rstd = sb("rstd", [P, 2, T])
        NA = 24704
        arena = sb("arena", [P, NA])
        banks = [ctx.enter_context(nc.psum_tensor(f"bank{i}", [P, 512], F32)) for i in range(4)]
        ps_mod = ctx.enter_context(nc.psum_tensor("ps_mod", [P, 512], F32))
        WA = ctx.enter_context(nc.psum_tensor("work_a", [P, 512], F32))
        WB = ctx.enter_context(nc.psum_tensor("work_b", [P, 512], F32))
        WC = ctx.enter_context(nc.psum_tensor("work_c", [P, 512], F32))

        def V(name, n=None):
            o = VOFF[name]
            return vec[:, o:o + (n or dict(VEC)[name])]

        class Region:
            def __init__(self, at=0):
                self.at = at

            def __call__(self, *shape, parts=P, dt=None):
                n = int(np.prod(shape))
                v = arena[0:parts, self.at:self.at + n]
                self.at += n
                assert self.at <= NA, self.at
                if dt is not None:
                    v = v.bitcast(dt)
                if len(shape) == 1:
                    return v
                names = "abcdef"[:len(shape)]
                return v.rearrange(f"p ({' '.join(names)}) -> p {' '.join(names)}",
                                   **{k: s for k, s in zip(names[1:], shape[1:])})

        r = Region()
        M = r(KT, T)
        Qh, Kh, VTh = r(T), r(T), r(T)
        LX = r(T + 4)
        LY = r(T)
        Vr = r(2, P)
        Pr = r(3, P)
        PT = r(3, P)
        xc, rg, ig, ut, at_, t1, t2, gx = [r(T) for _ in range(8)]
        gate_w = r(2, P)
        w_f = r(KT, 8)
        rowmax, rowsum, rowrec = r(2), r(2), r(2)
        sp8, lam_t = r(2, 8), r(3, 8)
        fl = r(6, T, parts=8)
        cm = r(2, T, parts=8)
        SQ = Region(17000)(KT, T)
        b_f = sb("b_f", [8, 1])

        r = Region()
        cols = r(3, T)
        Wd = r(2, QW, T)
        G = r(8, T)
        GL = r(4, T)
        hotA = r(2, 8, P)
        hotB = r(2, 8, QW)
        r = Region(3 * T)
        k12 = r(2, HEADS, P)
        Qp = r(2, T)
        S4 = r(4, P)
        v1f, v2f = r(TOPK), r(TOPK)
        i1u, i2u = r(TOPK, dt=U32), r(TOPK, dt=U32)
        i1f, i2f = r(TOPK), r(TOPK)
        cand = r(TOPK, TOPK)
        vs = r(TOPK)
        ic, ich, icl = r(TOPK, dt=U32), r(TOPK, dt=U32), r(TOPK, dt=U32)
        chf, clf = r(TOPK), r(TOPK)
        hot1, hot2 = r(TOPK, TOPK), r(TOPK, TOPK)
        picked = r(3, 2, HEADS, TOPK)
        pmax, psum_, prec = r(2, HEADS), r(2, HEADS), r(2, HEADS)

        r = Region()
        Y = r(KT, T)
        SZ = r(KT, T)
        BB = r(2, KT, 64)
        CC = r(3, PAIRS, 16)
        theta = r(PAIRS + 4)
        mag = r(PAIRS)
        ssm_at = r.at
        Bst = r(2, 2, 2, 64)
        Cst = r(2, 3, 4, 2, 16)
        Us = r(2, T)
        tab = r(2, 2, 2, T)
        ph, rn = r(2, T), r(2, T)
        P1, P2, Wr = r(2, T), r(2, T), r(2, T)
        Z = r(2, 2, T)
        Q1, Q2 = r(2, 2, T), r(2, 2, T)
        glt = Region(r.at)(2, T)
        r = Region()
        bl = r(2, KT, 64)
        bst_ = r(KT)
        br_ = r(2, KT, 64)
        pst = r(PAIRS)
        pe_ = [r(PAIRS) for _ in range(3)]
        r = Region(ssm_at)
        e = [r(KT, 64) for _ in range(7)]

        r = Region()
        KVT = r(6 * KV, T)
        VR = r(KV, 2, 2, P)
        VCr = r(KV, P, parts=16)
        KC, VCt = r(KV, NCMP), r(KV, NCMP)
        wg = r(KT, 48)
        GT = r(2, 48)
        nsa_at = r.at
        W1 = r(2, CMP_L, P)
        W2 = r(2, P)
        GC = r(KV * NCMP)
        b1e = r(2)
        SQ_end = r.at
        r = Region(nsa_at)
        O = r(KT, T)
        Qg = r(HPG, T)
        Vg = r(2, 2, P)
        VCg = r(P, parts=16)
        Pn = r(2, 3, P)
        Pc = r(2, NCMP)
        PTn = r(2, 3, P)
        PTc = r(2, P, parts=16)
        SZn = r(2, 3, T)
        ot = r(3, T)
        mx, sm, rc = r(6), r(6), r(6)

        slot_loaded = [sem(f"slot{i}_loaded") for i in range(R)]
        chunk_used = sem("chunk_used")
        bank_free = [sem(f"bank{i}_free") for i in range(4)]
        stage_end = sem("stage_end")
        params = sem("params_loaded")
        x_loaded = sem("x_loaded")
        S = {}

        def s(name):
            if name not in S:
                S[name] = sem(name)
            return S[name]

        for name in ("consts_ready cond_ready mod_ready norm_src squares_ready sums_ready var_ready sd_ready "
                     "scaled_ready h_ready f_in_psum f_ready f_abs log1p_ready cum_ready gatew_loaded qk_ready "
                     "vt_ready cm_ready scores_ready negmax_ready exps_ready probs_ready xc_ready gates_in_psum "
                     "lru_u_ready lru_t_ready lru_sq_ready ly_ready lru_done vrows_in_psum vrows_ready "
                     "pt_in_psum pt_ready attn_in_psum attn_ready merged_ready k_loaded peerq_ready s_in_psum "
                     "s_ready s_free vs_ready vs_exp picked_ready cols_in_psum cols_ready hot_ready hot_used "
                     "wd_copied gelu_ready g_ready ssm_loaded disc_a disc_b disc_c disc_d "
                     "disc_done masks_built u_ready bu_in_psum bu_read phase_ready frac_ready table_ready "
                     "z_ready q_ready y_pair gelu_free glu_free y_read y_gelu sig_ready glu_done "
                     "w1_loaded kv_ready vr_in_psum vr_ready cmp1_in_psum b1e_ready cmp_gelu cmp2_in_psum "
                     "kc_ready vc_in_psum vc_ready gt_in_psum gt_ready vg_ready q_ready2 sn_in_psum negmax2 "
                     "exps2 probs2 ptn_in_psum ptn_ready on_in_psum sz_ready combined out_ready stored").split():
            s(name)

        block = ctx.enter_context(nc.Block())

        def meet(eng, state):
            eng.drain().then_inc(stage_end, 1)
            state[0] += 4
            eng.wait_ge(stage_end, state[0])

        def norm_groups(g):
            return [(j, 0 if g == 1 or j < 2 else 1) for j in range(4)]


        GRANTED = dict(pe=('gates_in_psum', 's_in_psum', 'on_in_psum'), act=('attn_ready', 'pt_ready', 'lru_u_ready'),
                       dve=('lru_done', 's_ready', 'g_ready', 'combined'))

        NORMS = dict(mix=0, merged=1, ffn=2, final=3, l0=4, l1=5, final2=6)

        @block.sync
        def _(sp):
            def load(i, slot, stage, src, first=False):
                if not first:
                    sp.wait_ge(chunk_used, BASE[stage] + 8 * i + slot - 7)
                sp.dma_start(ring[:, slot], src).then_inc(slot_loaded[slot], 16)

            def plain(stage, src, at, n):
                with sp.Fori(0, n // 8) as i:
                    for slot in range(8):
                        load(i, slot, stage, src[at + 8 * i + slot])

            sp.dma_start(x[:], a["x"]).then_inc(x_loaded, 16)
            for slot in range(8):
                load(0, slot, "shift_scale", a["w_ada"][slot], first=True)
            with sp.Fori(1, 4) as i:
                for slot in range(8):
                    load(i, slot, "shift_scale", a["w_ada"][8 * i + slot])
            with sp.Fori(0, HEADS) as i:
                sp.wait_ge(s("gates_in_psum"), i + 1)
                sp.dma_start(gate_w, a["gate_w"][i]).then_inc(s("gatew_loaded"), 16)
                for slot in range(5):
                    load(i, slot, "heads", a["w_in"][5 * i + slot])
                for slot in range(3):
                    load(i, 5 + slot, "heads", a["w_ada"][32 + 3 * i + slot])
            plain("ada_rest", a["w_ada"], 56, 40)
            plain("w_out", a["w_out"], 0, 16)
            with sp.Fori(0, HEADS) as i:
                for slot in range(2):
                    load(i, slot, "topk", a["w_q"][2 * i + slot])
                for slot in range(6):
                    load(i, 2 + slot, "topk", a["w_mod2"][6 * i + slot])
            plain("spread", a["w_mod2"], 48, 32)
            with sp.Fori(0, 16) as g:
                for slot in range(8):
                    load(2 * g, slot, "peer", a["peer_u"][8 * g + slot])
                for slot in range(8):
                    load(2 * g + 1, slot, "peer", a["peer_v"][8 * g + slot])
            plain("between", a["w_mod2"], 80, 16)
            with sp.Fori(0, 8) as i:
                for t in range(2):
                    load(i, 4 * t, "ssm", a["ssm_in"][2 * i + t])
                    load(i, 4 * t + 1, "ssm", a["ssm_in"][KT + 2 * i + t])
                    for m in range(2):
                        load(i, 4 * t + 2 + m, "ssm", a["w_mod2"][96 + 4 * i + 2 * t + m])
            plain("glu", a["w_glu"], 0, 16)
            plain("ssm_out", a["ssm_out"], 0, 16)
            plain("kv", a["w_kv"], 0, 24)
            plain("nsa", a["w_qz"], 0, 64)
            plain("w_o", a["w_o"], 0, 16)
            sp.wait_ge(s("out_ready"), 1)
            sp.dma_start(a["out"], H[:]).then_inc(s("stored"), 16)
            sp.wait_ge(s("stored"), 16)

        @block.tensor
        def _(pe):
            mm = nc.tensor.matmul
            met = [0]
            uses = [0, 0, 0, 0]

            def chunk(stage, i, slot):
                pe.wait_ge(slot_loaded[slot % 8], 16 * (BASE[stage] // 8 + i + 1))
                return ring[:, slot % 8]

            def project(stage, i, slot, rhs, out, bank, need=None):
                w = chunk(stage, i, slot)
                if need is not None:
                    pe.wait_ge(bank_free[bank], need + 1)
                for k in range(KT):
                    last = mm(out, w[:, k, :], rhs[:, k, :], start=(k == 0), stop=(k == KT - 1))
                last.then_inc(chunk_used, 1)

            def vector_chunk(stage, i, slot, which, col):
                w = chunk(stage, i, slot)
                for k in range(KT):
                    last = mm(ps_mod[:, bass.ds(col, 1)] if not isinstance(col, int) else ps_mod[:, col:col + 1],
                              w[:, k, :], cond[:, which, k:k + 1], start=(k == 0), stop=(k == KT - 1))
                last.then_inc(chunk_used, 1)

            def norm_sums(name, groups=1):
                n = NORMS[name]
                for j, g in norm_groups(groups):
                    pe.wait_ge(s("squares_ready"), 4 * n + j + 1)
                    for k in range(4):
                        t = 4 * j + k
                        last = mm(WA[:, g * T:(g + 1) * T], ones[:, 0:P], SQ[:, t, :],
                                  start=(t % (KT // groups) == 0), stop=(t % (KT // groups) == KT // groups - 1))
                last.then_inc(s("sums_ready"), 1)

            def plain(stage, n, rhs):
                with pe.Fori(0, n // 8) as i:
                    for slot in range(8):
                        b = slot % 4
                        project(stage, i, slot, rhs, banks[b][:, 0:T], b, uses[b] + 2 * i + slot // 4)
                for b in range(4):
                    uses[b] += n // 4

            for name in GRANTED['pe']:
                pe.sem_inc(s(name), 1)
            pe.wait_ge(s("consts_ready"), 1)
            norm_sums("mix")
            pe.wait_ge(s("cond_ready"), 1)
            with pe.Fori(0, 4) as i:
                for slot in range(8):
                    vector_chunk("shift_scale", i, slot, 0, 8 * i + slot)
            pe.wait_ge(s("h_ready"), KT)
            for k in range(KT):
                last = mm(WB[0:8, 0:T], w_f[:, k, :], H[:, k, :], start=(k == 0), stop=(k == KT - 1))
            last.then_inc(s("f_in_psum"), 1)
            pe.wait_ge(s("cum_ready"), 1)
            with pe.Fori(0, HEADS) as i:
                project("heads", i, 0, H, banks[0][:, 0:T], 0, i)
                project("heads", i, 1, H, banks[0][:, T:2 * T], 0)
                project("heads", i, 2, H, banks[1][:, 0:T], 1, i)
                project("heads", i, 3, H, banks[2][:, 0:T], 2, i)
                pe.wait_ge(s("qk_ready"), i + 1)
                pe.wait_ge(s("cm_ready"), i + 1)
                pe.wait_ge(s("attn_ready"), i + 1)
                for qt in range(2):
                    nk = P * (qt + 1)
                    out = WA[:, P * qt:P * qt + nk]
                    mm(out, Qh[:, P * qt:P * qt + P], Kh[:, 0:nk], start=True, stop=False)
                    mm(out, cm[:, 0, P * qt:P * qt + P], ones[0:8, 0:nk], start=False, stop=False)
                    mm(out, ones[0:8, 0:P], cm[:, 1, 0:nk], start=False, stop=False)
                    last = mm(out[:, P * qt:P * qt + P], ident[:], causal[:], start=False, stop=True)
                last.then_inc(s("scores_ready"), 1)
                project("heads", i, 4, H, banks[3][:, 0:T], 3, i)
                pe.wait_ge(s("vt_ready"), i + 1)
                pe.wait_ge(s("pt_ready"), i + 1)
                for kt in range(2):
                    last = nc.tensor.transpose(WB[:, P * kt:P * kt + P], VTh[:, P * kt:P * kt + P], ident[:])
                last.then_inc(s("vrows_in_psum"), 1)
                pe.wait_ge(s("xc_ready"), i + 1)
                pe.wait_ge(s("gatew_loaded"), 16 * (i + 1))
                pe.wait_ge(s("lru_u_ready"), i + 1)
                for g in range(2):
                    last = mm(WC[:, T * g:T * g + T], gate_w[:, g, :], xc, start=True, stop=True)
                last.then_inc(s("gates_in_psum"), 1)
                vector_chunk("heads", i, 5, 0, 32 + 3 * i)
                pe.wait_ge(s("probs_ready"), i + 1)
                pe.wait_ge(s("vrows_ready"), i + 1)
                for b in range(3):
                    last = nc.tensor.transpose(WB[:, P * b:P * b + P], Pr[:, b, :], ident[:])
                last.then_inc(s("pt_in_psum"), 1)
                vector_chunk("heads", i, 6, 0, 33 + 3 * i)
                pe.wait_ge(s("pt_ready"), i + 1 + 1)
                mm(WA[:, 0:P], Vr[:, 0, :], PT[:, 0, :], start=True, stop=True)
                mm(WA[:, P:T], Vr[:, 0, :], PT[:, 1, :], start=True, stop=False)
                mm(WA[:, P:T], Vr[:, 1, :], PT[:, 2, :], start=False, stop=True).then_inc(s("attn_in_psum"), 1)
                vector_chunk("heads", i, 7, 0, 34 + 3 * i)
            for b in range(4):
                uses[b] += HEADS
            meet(pe, met)
            with pe.Fori(0, 5) as i:
                for slot in range(8):
                    vector_chunk("ada_rest", i, slot, 0, 56 + 8 * i + slot)
            norm_sums("merged", 2)
            pe.wait_ge(s("h_ready"), 2 * KT)
            plain("w_out", 16, H)
            norm_sums("ffn")
            pe.wait_ge(s("h_ready"), 3 * KT)
            pe.wait_ge(s("k_loaded"), 16)
            with pe.Fori(0, HEADS) as i:
                project("topk", i, 0, H, banks[0][:, 0:T], 0, uses[0] + i)
                project("topk", i, 1, H, banks[1][:, 0:T], 1, uses[1] + i)
                for m in range(3):
                    vector_chunk("topk", i, 2 + m, 1, 96 + 6 * i + m)
                pe.wait_ge(s("peerq_ready"), i + 1)
                pe.wait_ge(s("s_ready"), i + 1)
                for tt in range(2):
                    for h in range(2):
                        q = 2 * tt + h
                        last = mm(WA[:, P * q:P * q + P], Qp[:, h, P * tt:P * tt + P], k12[:, h, i, :],
                                  start=True, stop=True)
                last.then_inc(s("s_in_psum"), 1)
                for m in range(3):
                    vector_chunk("topk", i, 5 + m, 1, 99 + 6 * i + m)
            uses[0] += HEADS
            uses[1] += HEADS
            pe.wait_ge(s("picked_ready"), 1)
            for w in range(3):
                for tt in range(2):
                    last = nc.tensor.transpose((WA, WB, WC)[w][:, P * tt:P * tt + P],
                                               picked[:, w, tt].rearrange("p h k -> p (h k)"), ident[:])
            last.then_inc(s("cols_in_psum"), 1)
            meet(pe, met)

            pe.sem_inc(s("hot_used"), 2)

            def spread_unit(unit, bank):
                pe.wait_ge(s("wd_copied"), unit + 1)
                for h in range(2):
                    pe.wait_ge(s("hot_ready"), 2 * unit + h + 1)
                    for j in range(8):
                        o = QW * (8 * h + j)
                        last = mm(bank[:, o:o + QW], hotA[:, h, j, :], hotB[:, h, j, :], start=True, stop=True)
                    last.then_inc(s("hot_used"), 1)

            with pe.Fori(0, 4) as i:
                for u in range(4):
                    spread_unit(4 * i + u, (WB, WC)[u % 2])
                    vector_chunk("spread", i, 2 * u, 1, 144 + 8 * i + 2 * u)
                    vector_chunk("spread", i, 2 * u + 1, 1, 145 + 8 * i + 2 * u)
            with pe.Fori(0, 16) as g:
                for slot in range(8):
                    b = slot % 4
                    project("peer", 2 * g, slot, H, banks[b][:, 0:T], b, uses[b] + 4 * g + slot // 4)
                    if slot in (1, 6):
                        u = 0 if slot == 1 else 1
                        spread_unit(4 * g + 16 + u, (WB, WC)[u])
                for slot in range(8):
                    b = slot % 4
                    w = chunk("peer", 2 * g + 1, slot).rearrange("p k n -> p (k n)").rearrange("p (k n) -> p k n", k=8)
                    pe.wait_ge(bank_free[b], uses[b] + 4 * g + 2 + slot // 4 + 1)
                    for dd in range(2):
                        for k in range(8):
                            if slot == 0 and dd == 0:
                                pe.wait_ge(s("g_ready"), 8 * g + k + 1 + 1)
                            last = mm(banks[b][:, T * dd:T * dd + T], w[:, k, P * dd:P * dd + P], G[:, k, :],
                                      start=(k == 0), stop=(k == 7))
                    last.then_inc(chunk_used, 1)
                    if slot in (1, 6):
                        u = 2 if slot == 1 else 3
                        spread_unit(4 * g + 16 + u, (WB, WC)[u % 2])
            for b in range(4):
                uses[b] += 64
            meet(pe, met)
            with pe.Fori(0, 2) as i:
                for slot in range(8):
                    vector_chunk("between", i, slot, 1, 176 + 8 * i + slot)
            meet(pe, met)
            norm_sums("final")
            norm_sums("l0")
            pe.wait_ge(s("h_ready"), 4 * KT)
            meet(pe, met)
            pe.sem_inc(s("bu_read"), 2)
            with pe.Fori(0, 8) as i:
                for t in range(2):
                    tile = 2 * i + t
                    project("ssm", i, 4 * t, H, banks[2 * t][:, 0:T], 2 * t, uses[2 * t] + i)
                    project("ssm", i, 4 * t + 1, H, banks[2 * t + 1][:, 0:T], 2 * t + 1, uses[2 * t + 1] + i)

                    def b_times_u(j):
                        pe.wait_ge(s("bu_read"), 4 * tile + j + 1)
                        for ri in range(2):
                            last = mm((WA, WB)[j % 2][:, T * ri:T * ri + T],
                                      Bst[32 * j:32 * j + 32, t, ri].rearrange("p a b -> p (a b)"),
                                      Us[32 * j:32 * j + 32, t, :], start=True, stop=True, tile_position=(32 * j, 0))
                        last.then_inc(s("bu_in_psum"), 1)

                    def c_times_x(j):
                        pe.wait_ge(s("q_ready"), 4 + 4 * tile + j + 1)
                        for n, (kind, src) in enumerate(((0, Q1[:, j % 2, 0]), (1, Q2[:, j % 2, 1]),
                                                         (2, Q2[:, j % 2, 0]), (2, Q1[:, j % 2, 1]))):
                            last = mm(WC[32 * j:32 * j + 32, 0:T],
                                      Cst[:, t, kind, j].rearrange("p a b -> p (a b)"), src,
                                      start=(n == 0), stop=(n == 3), tile_position=(0, 32 * j))
                        return last

                    pe.wait_ge(s("u_ready"), tile + 1)
                    pe.wait_ge(s("masks_built"), tile + 1)
                    b_times_u(0)
                    b_times_u(1)
                    vector_chunk("ssm", i, 4 * t + 2, 1, 192 + 4 * i + 2 * t)
                    pe.wait_ge(s("y_read"), tile + 2)
                    c_times_x(0).then_inc(s("y_pair"), 1)
                    b_times_u(2)
                    c_times_x(1).then_inc(s("y_pair"), 1)
                    b_times_u(3)
                    vector_chunk("ssm", i, 4 * t + 3, 1, 193 + 4 * i + 2 * t)
                    c_times_x(2).then_inc(s("y_pair"), 1)
                    c_times_x(3).then_inc(s("y_pair"), 1)
            for b in range(4):
                uses[b] += 8
            pe.wait_ge(s("y_gelu"), 1)
            plain("glu", 16, Y)
            pe.wait_ge(s("glu_done"), KT)
            plain("ssm_out", 16, H)
            meet(pe, met)
            norm_sums("l1")
            pe.wait_ge(s("h_ready"), 5 * KT)
            plain("kv", 24, H)
            pe.wait_ge(s("kv_ready"), 6 * KV)
            for g in range(KV):
                if g >= 2:
                    pe.wait_ge(s("vr_ready"), g - 1)
                for b in range(2):
                    for kt in range(2):
                        o = P * (2 * b + kt)
                        last = nc.tensor.transpose((WA, WB)[g % 2][:, o:o + P],
                                                   KVT[:, (3 + 2 * b) * KV + g, P * kt:P * kt + P], ident[:])
                last.then_inc(s("vr_in_psum"), 1)
            pe.wait_ge(s("w1_loaded"), 48)
            nb = KV * NCMP
            for b in range(2):
                for l in range(CMP_L):
                    mm(WC[:, 64 * b:64 * b + nb], W1[:, b, l, :],
                       KVT[:, b * KV:(b + 1) * KV, l:l + 16 * (NCMP - 1) + 1:16],
                       start=(l == 0), stop=(l == CMP_L - 1))
                for l in range(CMP_L):
                    last = mm(WC[:, 128 + b:129 + b], W1[:, b, l, :], V("cmp_pe")[:, CMP_L * b + l:CMP_L * b + l + 1],
                              start=(l == 0), stop=(l == CMP_L - 1))
            last.then_inc(s("cmp1_in_psum"), 1)
            for b in range(2):
                pe.wait_ge(s("cmp_gelu"), b + 1)
                mm(WC[:, 192 + 64 * b:192 + 64 * b + nb], W2[:, b, :], GC, start=True, stop=True)\
                    .then_inc(s("cmp2_in_psum"), 1)
                pe.wait_ge(s("kc_ready"), b + 1)
            pe.wait_ge(s("vr_ready"), KV)
            for g in range(KV):
                last = nc.tensor.transpose(WA[0:NCMP, P * g:P * g + P], VCt[:, g, :], ident[:])
            last.then_inc(s("vc_in_psum"), 1)
            pe.wait_ge(s("h_ready"), 6 * KT)
            for tt in range(2):
                for k in range(KT):
                    last = mm(WB[:, 64 * tt:64 * tt + 48], H[:, k, P * tt:P * tt + P], wg[:, k, :],
                              start=(k == 0), stop=(k == KT - 1))
            last.then_inc(s("gt_in_psum"), 1)
            meet(pe, met)
            with pe.Fori(0, KV) as g:
                for hh in range(HPG):
                    project("nsa", 2 * g, hh, H, banks[hh][:, 0:T], hh, uses[hh] + 4 * g)
                for hh in range(HPG):
                    n = 4 * g + hh
                    def z_chunk(br):
                        c = 4 + 3 * hh + br
                        b = c % 4
                        project("nsa", 2 * g + c // 8, c, H, banks[b][:, 0:T], b, uses[b] + 4 * g + c // 4)
                    pe.wait_ge(s("q_ready2"), n + 1)
                    pe.wait_ge(s("combined"), n + 1)
                    for br in range(2):
                        for qt in range(2):
                            nk = P * (qt + 1)
                            out = (WA, WB)[br][:, P * qt:P * qt + nk]
                            mm(out, Qg[:, hh, P * qt:P * qt + P], KVT[:, (2 + 2 * br) * KV + g, 0:nk],
                               start=True, stop=False)
                            last = mm(out[:, P * qt:P * qt + P], ident[:], causal[:], start=False, stop=True)
                    for qt in range(2):
                        out = WC[:, 16 * qt:16 * qt + NCMP]
                        mm(out, Qg[:, hh, P * qt:P * qt + P], KC[:, g, :], start=True, stop=False)
                        last = mm(out, ident[:], cmp_neg[:, qt, :], start=False, stop=True)
                    last.then_inc(s("sn_in_psum"), 1)
                    z_chunk(0)
                    pe.wait_ge(s("probs2"), n + 1)
                    for br in range(2):
                        for b in range(3):
                            nc.tensor.transpose((WA, WB)[br][:, P * b:P * b + P], Pn[:, br, b, :], ident[:])
                    for qt in range(2):
                        last = nc.tensor.transpose(WC[0:NCMP, P * qt:P * qt + P], Pc[:, qt, :], ident[:])
                    last.then_inc(s("ptn_in_psum"), 1)
                    z_chunk(1)
                    pe.wait_ge(s("ptn_ready"), n + 1)
                    pe.wait_ge(s("vg_ready"), g + 1)
                    for br in range(2):
                        w = (WA, WB)[br]
                        mm(w[:, 0:P], Vg[:, br, 0, :], PTn[:, br, 0, :], start=True, stop=True)
                        mm(w[:, P:T], Vg[:, br, 0, :], PTn[:, br, 1, :], start=True, stop=False)
                        mm(w[:, P:T], Vg[:, br, 1, :], PTn[:, br, 2, :], start=False, stop=True)
                    for qt in range(2):
                        last = mm(WC[:, P * qt:P * qt + P], VCg[0:NCMP, :], PTc[0:NCMP, qt, :], start=True, stop=True)
                    last.then_inc(s("on_in_psum"), 1)
                    z_chunk(2)
            for b in range(4):
                uses[b] += 16
            pe.wait_ge(s("combined"), KT + 1)
            plain("w_o", 16, O)
            meet(pe, met)
            norm_sums("final2")

        @block.scalar
        def _(act):
            A = nc.scalar.activation
            met = [0]

            def used(stage, i, slot):
                act.wait_ge(chunk_used, BASE[stage] + 8 * i + slot + 1)

            def norm_squares(name, src):
                n = NORMS[name]
                act.wait_ge(s("norm_src"), n + 1)
                for j in range(4):
                    A(SQ[:, 4 * j:4 * j + 4, :], src[:, 4 * j:4 * j + 4, :], ACT.Square).then_inc(s("squares_ready"), 1)

            def norm_sqrt(name):
                n = NORMS[name]
                act.wait_ge(s("var_ready"), n + 1)
                A(sd[:], var[:], ACT.Sqrt).then_inc(s("sd_ready"), 1)

            def norm_bias(call, bias):
                for k in range(KT):
                    act.wait_ge(s("scaled_ready"), KT * call + k + 1)
                    A(H[:, k, :], H[:, k, :], ACT.Identity, bias=bias[:, k:k + 1]).then_inc(s("h_ready"), 1)

            for name in GRANTED['act']:
                act.sem_inc(s(name), 1)
            for b in range(4):
                act.sem_inc(bank_free[b], 1)
            for name, dst in (("vec", vec[:]), ("w_f", w_f), ("b_f", b_f[:])):
                act.dma_start(dst, a[name]).then_inc(params, 16)
            act.wait_ge(x_loaded, 16)
            act.wait_ge(s("consts_ready"), 1)
            act.sem_inc(s("norm_src"), 1)
            norm_squares("mix", x)
            act.wait_ge(params, 48)
            A(cond[:, 0, :], V("c"), ACT.Silu)
            A(cond[:, 1, :], V("c2"), ACT.Silu).then_inc(s("cond_ready"), 1)
            A(lam_t[:, 0, :], V("lru_lambda"), ACT.Abs)
            act.drain()
            A(lam_t[:, 1, :], lam_t[:, 0, :], ACT.Exp, scale=-1.0)
            act.drain()
            A(lam_t[:, 2, :], lam_t[:, 1, :], ACT.Ln, bias=ones[:, 0:1])
            norm_sqrt("mix")
            norm_bias(0, mod[:, 0:16])
            act.wait_ge(s("f_ready"), 1)
            A(fl[:, 1, :], fl[:, 0, :], ACT.Abs)
            act.drain()
            A(fl[:, 2, :], fl[:, 1, :], ACT.Exp, scale=-1.0)
            act.drain()
            A(fl[:, 3, :], fl[:, 2, :], ACT.Ln, bias=ones[0:8, 0:1]).then_inc(s("log1p_ready"), 1)
            with act.Fori(0, HEADS) as i:
                used("heads", i, 1)
                A(Qh, banks[0][:, 0:T], ACT.Copy, scale=SCALE)
                A(Kh, banks[0][:, T:2 * T], ACT.Copy).then_inc(bank_free[0], 1)
                act.drain().then_inc(s("qk_ready"), 1)
                used("heads", i, 2)
                A(VTh, banks[1][:, 0:T], ACT.Copy).then_inc(bank_free[1], 1)
                act.drain().then_inc(s("vt_ready"), 1)
                act.wait_ge(s("negmax_ready"), i + 1)
                A(Pr[:, 0, :], WA[:, 0:P], ACT.Exp, bias=rowmax[:, 0:1], accum_out=rowsum[:, 0:1])
                A(Pr[:, 1:3, :].rearrange("p a b -> p (a b)"), WA[:, P:3 * P], ACT.Exp, bias=rowmax[:, 1:2],
                  accum_out=rowsum[:, 1:2])
                act.drain().then_inc(s("exps_ready"), 1)
                used("heads", i, 4)
                act.wait_ge(s("lru_done"), i + 1)
                A(LY, banks[3][:, 0:T], ACT.Gelu_apprx_tanh).then_inc(bank_free[3], 1)
                act.drain().then_inc(s("ly_ready"), 1)
                act.wait_ge(s("vrows_in_psum"), i + 1)
                A(Vr.rearrange("p a b -> p (a b)"), WB[:, 0:T], ACT.Copy).then_inc(s("vrows_ready"), 1)
                act.wait_ge(s("gates_in_psum"), i + 1 + 1)
                A(rg, WC[:, 0:T], ACT.Sigmoid, bias=V("lru_b_a")[:, bass.ds(i, 1)])
                A(ig, WC[:, T:2 * T], ACT.Sigmoid, bias=V("lru_b_x")[:, bass.ds(i, 1)])
                act.drain()
                A(ut, rg, ACT.Tanh, scale=sp8[:, 0, bass.ds(i, 1)])
                A(at_, rg, ACT.Exp, scale=sp8[:, 1, bass.ds(i, 1)])
                act.drain().then_inc(s("lru_u_ready"), 1)
                act.wait_ge(s("lru_t_ready"), i + 1)
                A(t2, t1, ACT.Sqrt, scale=2.0).then_inc(s("lru_sq_ready"), 1)
                act.wait_ge(s("pt_in_psum"), i + 1)
                A(PT.rearrange("p a b -> p (a b)"), WB[:, 0:3 * P], ACT.Copy).then_inc(s("pt_ready"), 1)
                act.wait_ge(s("attn_in_psum"), i + 1)
                A(M[:, bass.ds(i, 1), :], WA[:, 0:T], ACT.Copy).then_inc(s("attn_ready"), 1)
            meet(act, met)
            act.sem_inc(s("norm_src"), 1)
            norm_squares("merged", M)
            norm_sqrt("merged")
            norm_squares("ffn", x)
            act.dma_start(k12, a["k12"]).then_inc(s("k_loaded"), 16)
            norm_sqrt("ffn")
            norm_bias(1, mod[:, 48:64])
            with act.Fori(0, HEADS) as i:
                act.wait_ge(s("s_in_psum"), i + 1)
                for h in range(2):
                    used("topk", i, h)
                    A(Qp[:, h, :], banks[h][:, 0:T], ACT.Copy).then_inc(bank_free[h], 1)
                act.drain().then_inc(s("peerq_ready"), 1)
            act.wait_ge(s("vs_ready"), 1)
            A(picked[:, 2], picked[:, 2], ACT.Exp).then_inc(s("vs_exp"), 1)
            act.wait_ge(s("cols_in_psum"), 1)
            for w in range(3):
                A(cols[:, w, :], (WA, WB, WC)[w][:, 0:T], ACT.Copy)
            meet(act, met)
            act.sem_inc(s("wd_copied"), 2)

            def copy_unit(unit, bank, buf, tok):
                act.wait_ge(s("hot_used"), 2 * unit + 4)
                A(Wd[:, buf, :, bass.ds(tok, 16)],
                  bank[:].rearrange("p (t i) -> p i t", i=QW), ACT.Copy).then_inc(s("wd_copied"), 1)

            with act.Fori(0, 4) as i:
                for u in range(4):
                    copy_unit(4 * i + u, (WB, WC)[u % 2], 0, 64 * i + 16 * u)
            with act.Fori(0, 2) as o:
                for par in range(2):
                    act.wait_ge(s("g_ready"), 64 * o + 32 * par + 1)
                    with act.Fori(0, 4) as q:
                        g = 8 * o + 4 * par + q
                        for slot in range(8):
                            b = slot % 4
                            used("peer", 2 * g, slot)
                            act.wait_ge(s("gelu_free"), 8 * g + slot + 1)
                            A(GL[:, b, :], banks[b][:, 0:T], ACT.Gelu_apprx_tanh).then_inc(bank_free[b], 1)
                            act.drain().then_inc(s("gelu_ready"), 1)
                            if slot in (2, 7):
                                u = 0 if slot == 2 else 1
                                copy_unit(4 * g + 16 + u, (WB, WC)[u], 1 - par, 64 * q + 16 * u)
                        for u in (2, 3):
                            copy_unit(4 * g + 16 + u, (WB, WC)[u % 2], 1 - par, 64 * q + 16 * u)
            meet(act, met)
            for k in range(2):
                act.dma_start(pst[64 * k:64 * k + 64], a["step_pair"][k:k + 1, :].broadcast_to([64, PAIRS]))\
                    .then_inc(s("ssm_loaded"), 16)
            for k in range(8):
                act.dma_start(bl[16 * k:16 * k + 16], a["lam_tile"][k:k + 1].broadcast_to([16, 2, KT, 64]))\
                    .then_inc(s("ssm_loaded"), 16)
                act.dma_start(bst_[16 * k:16 * k + 16], a["step_tile"][k:k + 1, :].broadcast_to([16, KT]))\
                    .then_inc(s("ssm_loaded"), 16)
            act.dma_start(br_, a["ssm_b"]).then_inc(s("ssm_loaded"), 16)
            act.dma_start(CC[:, 0:3:2], a["ssm_c"]).then_inc(s("ssm_loaded"), 16)
            act.wait_ge(s("ssm_loaded"), 20 * 16)
            A(pst, pst, ACT.Exp)
            A(bst_, bst_, ACT.Exp)
            act.drain().then_inc(s("disc_a"), 1)
            act.wait_ge(s("disc_b"), 1)
            A(e[0], e[0], ACT.Exp)
            A(mag, pe_[0], ACT.Exp)
            A(e[3], e[1], ACT.Sin, scale=TWO_PI)
            A(e[2], e[1], ACT.Abs)
            act.drain()
            A(e[2], e[2], ACT.Sin, scale=-TWO_PI, bias=cst[:, 1:2])
            act.drain().then_inc(s("disc_c"), 1)
            act.wait_ge(s("disc_done"), 1)
            meet(act, met)
            act.sem_inc(s("norm_src"), 1)
            norm_squares("final", x)
            norm_sqrt("final")
            norm_squares("l0", x)
            norm_sqrt("l0")
            norm_bias(2, mod[:, 96:112])
            meet(act, met)

            def table(duo, col, need):
                for k in range(2):
                    A(ph[:, k, :], iota_t[:], ACT.Copy, scale=theta[:, bass.ds(col + k, 1)] if not isinstance(col, int) else theta[:, col + k:col + k + 1])
                act.drain()
                A(rn, ph, ACT.Copy, bias=MAGIC)
                act.drain()
                A(rn, rn, ACT.Copy, bias=-MAGIC).then_inc(s("phase_ready"), 1)
                act.wait_ge(s("frac_ready"), need[0])
                if need[1] is not None:
                    act.wait_ge(s("q_ready"), need[1])
                A(tab[:, duo, 1], ph, ACT.Sin, scale=TWO_PI)
                A(rn, ph, ACT.Abs)
                act.drain()
                A(tab[:, duo, 0], rn, ACT.Sin, scale=-TWO_PI, bias=cst[:, 1:2])
                act.drain().then_inc(s("table_ready"), 1)

            for duo in range(2):
                table(duo, 2 * duo, (duo + 1, None))
            with act.Fori(0, 8) as i:
                for t in range(2):
                    tile = 2 * i + t
                    used("ssm", i, 4 * t)
                    act.wait_ge(s("y_read"), tile + 1)
                    A(Us[:, t, :], banks[2 * t][:, 0:T], ACT.Copy).then_inc(bank_free[2 * t], 1)
                    act.drain().then_inc(s("u_ready"), 1)
                    used("ssm", i, 4 * t + 1)
                    A(SZ[:, bass.ds(tile, 1), :], banks[2 * t + 1][:, 0:T], ACT.Silu).then_inc(bank_free[2 * t + 1], 1)
                    for duo in range(2):
                        table(duo, 4 * tile + 4 + 2 * duo, (2 * tile + 2 + duo + 1, 4 + 4 * tile + 2 * duo + 2))
            act.wait_ge(s("y_read"), KT + 2)
            A(Y, Y, ACT.Gelu_apprx_tanh).then_inc(s("y_gelu"), 1)
            with act.Fori(0, 2) as i:
                for slot in range(8):
                    b = slot % 4
                    used("glu", i, slot)
                    act.wait_ge(s("glu_free"), 8 * i + slot + 1)
                    A(glt[:, slot % 2, :], banks[b][:, 0:T], ACT.Sigmoid, bias=V("b_glu")[:, bass.ds(8 * i + slot, 1)]).then_inc(bank_free[b], 1)
                    act.drain().then_inc(s("sig_ready"), 1)
            meet(act, met)
            act.sem_inc(s("norm_src"), 1)
            norm_squares("l1", x)
            norm_sqrt("l1")
            norm_bias(3, mod[:, 192:208])
            act.drain()
            for k in range(2):
                act.dma_start((W1, W2)[k], a[("cmp_w1", "cmp_w2")[k]]).then_inc(s("w1_loaded"), 16)
            act.dma_start(wg, a["w_gate"]).then_inc(s("w1_loaded"), 16)
            with act.Fori(0, 3) as i:
                for slot in range(8):
                    b = slot % 4
                    used("kv", i, slot)
                    A(KVT[:, bass.ds(8 * i + slot, 1), :], banks[b][:, 0:T], ACT.Copy).then_inc(bank_free[b], 1)
                    act.drain().then_inc(s("kv_ready"), 1)
            for g in range(KV):
                act.wait_ge(s("vr_in_psum"), g + 1)
                A(VR[:, g].rearrange("p a b c -> p (a b c)"), (WA, WB)[g % 2][:], ACT.Copy).then_inc(s("vr_ready"), 1)
            for b in range(2):
                act.wait_ge(s("b1e_ready"), 1)
                A(GC, WC[:, 64 * b:64 * b + KV * NCMP], ACT.Gelu_apprx_tanh, bias=b1e[:, b:b + 1])\
                    .then_inc(s("cmp_gelu"), 1)
                act.wait_ge(s("cmp2_in_psum"), b + 1)
                A((KC, VCt)[b].rearrange("p a b -> p (a b)"), WC[:, 192 + 64 * b:192 + 64 * b + KV * NCMP],
                  ACT.Identity, bias=V("cmp_b2")[:, b:b + 1])
                act.drain().then_inc(s("kc_ready"), 1)
            act.wait_ge(s("vc_in_psum"), 1)
            A(VCr[0:NCMP].rearrange("p a b -> p (a b)"), WA[0:NCMP, :], ACT.Copy)
            norm_bias(4, mod[:, 144:160])
            act.wait_ge(s("gt_in_psum"), 1)
            A(GT, WB[:, 0:128].rearrange("p (a b) -> p a b", a=2)[:, :, 0:48], ACT.Sigmoid)
            meet(act, met)
            with act.Fori(0, KV) as g:
                for hh in range(HPG):
                    used("nsa", 2 * g, hh)
                    A(Qg[:, hh, :], banks[hh][:, 0:T], ACT.Copy, scale=SCALE).then_inc(bank_free[hh], 1)
                    act.drain().then_inc(s("q_ready2"), 1)
                for hh in range(HPG):
                    n = 4 * g + hh
                    def z_silu(br):
                        c = 4 + 3 * hh + br
                        used("nsa", 2 * g, c)
                        A(SZn[:, hh % 2, br, :], banks[c % 4][:, 0:T], ACT.Silu).then_inc(bank_free[c % 4], 1)
                        act.drain().then_inc(s("sz_ready"), 1)
                    act.wait_ge(s("negmax2"), n + 1)
                    for br in range(2):
                        w = (WA, WB)[br]
                        A(Pn[:, br, 0, :], w[:, 0:P], ACT.Exp, bias=mx[:, 2 * br:2 * br + 1],
                          accum_out=sm[:, 2 * br:2 * br + 1])
                        A(Pn[:, br, 1:3, :].rearrange("p a b -> p (a b)"), w[:, P:3 * P], ACT.Exp,
                          bias=mx[:, 2 * br + 1:2 * br + 2], accum_out=sm[:, 2 * br + 1:2 * br + 2])
                    for qt in range(2):
                        A(Pc[:, qt, :], WC[:, 16 * qt:16 * qt + NCMP], ACT.Exp, bias=mx[:, 4 + qt:5 + qt],
                          accum_out=sm[:, 4 + qt:5 + qt])
                    act.drain().then_inc(s("exps2"), 1)
                    z_silu(0)
                    act.wait_ge(s("ptn_in_psum"), n + 1)
                    for br in range(2):
                        A(PTn[:, br].rearrange("p a b -> p (a b)"), (WA, WB)[br][:, 0:3 * P], ACT.Copy)
                    A(PTc[0:NCMP].rearrange("p a b -> p (a b)"), WC[0:NCMP, 0:T], ACT.Copy)
                    act.drain().then_inc(s("ptn_ready"), 1)
                    z_silu(1)
                    z_silu(2)
            act.wait_ge(s("combined"), KT + 1)
            meet(act, met)
            act.sem_inc(s("norm_src"), 1)
            norm_squares("final2", x)
            norm_sqrt("final2")

        @block.vector
        def _(dve):
            v = nc.vector
            met = [0]

            def used(stage, i, slot):
                dve.wait_ge(chunk_used, BASE[stage] + 8 * i + slot + 1)

            def norm_rstd(name, width):
                n = NORMS[name]
                dve.wait_ge(s("sums_ready"), n + 1)
                groups = 2 if name == "merged" else 1
                dve.drain()
                v.tensor_scalar(var[:, 0:groups], WA[:, 0:groups * T].rearrange("p (a b) -> p a b", b=T),
                                1.0 / width, EPS, ALU.mult, ALU.add)
                if groups == 1:
                    v.tensor_scalar(var[:, 1], WA[:, 0:T], 1.0 / width, EPS, ALU.mult, ALU.add)
                dve.drain().then_inc(s("var_ready"), 1)
                dve.wait_ge(s("sd_ready"), n + 1)
                v.reciprocal(rstd[:], sd[:])
                dve.drain()

            def norm_scale(dst, src, g, signal=None):
                for k in range(KT):
                    ins = v.scalar_tensor_tensor(dst[:, k, :], src[:, k, :], g[:, k:k + 1], rstd[:, k // 8, :],
                                                 ALU.mult, ALU.mult)
                    if signal:
                        ins.then_inc(s(signal), 1)
                dve.drain()

            def modulated_gain(n, g, scale):
                v.tensor_scalar(gain[:, n, :], scale, 1.0, None, ALU.add)
                dve.drain()
                v.tensor_tensor(gain[:, n, :], gain[:, n, :], g, ALU.mult)
                dve.drain()

            def take_mod(lo, hi, stage, chunks):
                dve.wait_ge(chunk_used, BASE[stage] + chunks)
                v.tensor_tensor(mod[:, lo:hi], ps_mod[:, lo:hi],
                                vec[:, VOFF["b_ada"] + lo:VOFF["b_ada"] + hi], ALU.add)
                dve.drain()

            for name in GRANTED['dve']:
                dve.sem_inc(s(name), 1)
            v.memset(cst[:, 0:1], -MAGIC)
            v.memset(cst[:, 1:2], HALF_PI)
            v.memset(LX[:, 0:3], 0.0)
            norm_rstd("mix", D)
            dve.wait_ge(params, 48)
            take_mod(0, 32, "shift_scale", 32)
            modulated_gain(0, V("g_mix"), mod[:, 16:32])
            norm_scale(H, x, gain[:, 0, :], "scaled_ready")
            v.tensor_scalar(sp8[:, 0, :], V("lru_lambda"), -1.0, 0.0, ALU.mult, ALU.max)
            dve.drain()
            v.tensor_tensor(sp8[:, 0, :], sp8[:, 0, :], lam_t[:, 2, :], ALU.add)
            dve.drain()
            v.tensor_scalar(sp8[:, 0, :], sp8[:, 0, :], LRU_C, None, ALU.mult)
            dve.drain()
            v.tensor_scalar(sp8[:, 1, :], sp8[:, 0, :], -1.0, None, ALU.mult)
            dve.wait_ge(s("f_in_psum"), 1)
            v.tensor_scalar(fl[:, 0, :], WB[0:8, 0:T], b_f[:, 0:1], None, ALU.add).then_inc(s("f_ready"), 1)
            dve.drain()
            v.tensor_scalar(fl[:, 4, :], fl[:, 0, :], 0.0, None, ALU.min)
            dve.wait_ge(s("log1p_ready"), 1)
            dve.drain()
            v.tensor_tensor(fl[:, 4, :], fl[:, 4, :], fl[:, 3, :], ALU.subtract)
            dve.drain()
            v.tensor_tensor_scan(fl[:, 5, :], ones[0:8, :], fl[:, 4, :], 0.0, ALU.mult, ALU.add)
            dve.drain().then_inc(s("cum_ready"), 1)
            conv_w = V("conv_w").rearrange("p (a b) -> p a b", b=4)
            with dve.Fori(0, HEADS) as i:
                v.tensor_scalar(cm[:, 0, :], fl[:, 5, :], ident[0:8, bass.ds(i, 1)], None, ALU.mult)
                dve.drain()
                v.tensor_scalar(cm[:, 1, :], cm[:, 0, :], -1.0, None, ALU.mult).then_inc(s("cm_ready"), 1)
                used("heads", i, 3)
                v.tensor_copy(LX[:, 3:3 + T], banks[2][:, 0:T]).then_inc(bank_free[2], 1)
                dve.drain()
                v.tensor_scalar(xc, LX[:, 0:T], conv_w[:, bass.ds(i, 1), 0], V("conv_b")[:, bass.ds(i, 1)],
                                ALU.mult, ALU.add)
                for w in range(1, 4):
                    dve.drain()
                    v.scalar_tensor_tensor(xc, LX[:, w:w + T], conv_w[:, bass.ds(i, 1), w], xc, ALU.mult, ALU.add)
                dve.drain().then_inc(s("xc_ready"), 1)
                dve.wait_ge(s("scores_ready"), i + 1)
                v.tensor_reduce(rowmax[:, 0:1], WA[:, 0:P], AX, ALU.max)
                v.tensor_reduce(rowmax[:, 1:2], WA[:, P:3 * P], AX, ALU.max)
                dve.drain()
                v.tensor_scalar(rowmax, rowmax, -1.0, None, ALU.mult).then_inc(s("negmax_ready"), 1)
                dve.wait_ge(s("exps_ready"), i + 1)
                v.reciprocal(rowrec, rowsum)
                dve.drain()
                v.tensor_scalar(Pr[:, 0, :], Pr[:, 0, :], rowrec[:, 0:1], None, ALU.mult)
                v.tensor_scalar(Pr[:, 1:3, :], Pr[:, 1:3, :], rowrec[:, 1:2], None, ALU.mult)
                dve.drain().then_inc(s("probs_ready"), 1)
                dve.wait_ge(s("lru_u_ready"), i + 1 + 1)
                v.tensor_tensor(gx, ig, xc, ALU.mult)
                v.tensor_scalar(t1, ut, 1.0, None, ALU.add)
                dve.drain()
                v.reciprocal(t1, t1)
                dve.drain()
                v.tensor_tensor(t1, t1, ut, ALU.mult).then_inc(s("lru_t_ready"), 1)
                dve.wait_ge(s("lru_sq_ready"), i + 1)
                v.tensor_tensor(gx, gx, t2, ALU.mult)
                dve.drain()
                v.tensor_tensor_scan(t1, at_, gx, 0.0, ALU.mult, ALU.add)
                dve.drain()
                dve.wait_ge(s("ly_ready"), i + 1)
                v.tensor_tensor(M[:, bass.ds(HEADS + i, 1), :], t1, LY, ALU.mult).then_inc(s("lru_done"), 1)
            meet(dve, met)
            norm_rstd("merged", D // 2)
            norm_scale(H, M, V("g_merge"), "h_ready")
            take_mod(32, 96, "ada_rest", 40)

            def residual(stage, i, slot, gate):
                used(stage, i, slot)
                m = 8 * i + slot
                v.scalar_tensor_tensor(x[:, bass.ds(m, 1), :], banks[slot % 4][:, 0:T], gate[:, bass.ds(m, 1)],
                                       x[:, bass.ds(m, 1), :], ALU.mult, ALU.add).then_inc(bank_free[slot % 4], 1)

            with dve.Fori(0, 2) as i:
                for slot in range(8):
                    residual("w_out", i, slot, mod[:, 32:48])
            dve.drain().then_inc(s("norm_src"), 1)
            modulated_gain(1, V("g_ffn"), mod[:, 64:80])
            norm_rstd("ffn", D)
            norm_scale(H, x, gain[:, 1, :], "scaled_ready")

            def top16(vals, idx, src):
                v.max(vals[:, 0:8], src)
                dve.drain()
                v.max_index(idx[:, 0:8], vals[:, 0:8], src)
                dve.drain()
                v.match_replace(src, vals[:, 0:8], src, LOW)
                dve.drain()
                v.max(vals[:, 8:16], src)
                dve.drain()
                v.max_index(idx[:, 8:16], vals[:, 8:16], src)

            iota16 = iota[:, 0:TOPK].unsqueeze(1).broadcast_to([P, TOPK, TOPK])
            with dve.Fori(0, HEADS) as i:
                dve.wait_ge(s("s_in_psum"), i + 1 + 1)
                v.tensor_copy(S4.rearrange("p a b -> p (a b)"), WA[:]).then_inc(s("s_ready"), 1)
                dve.drain()
                for tt in range(2):
                    top16(v1f, i1u, S4[:, 2 * tt, :])
                    top16(v2f, i2u, S4[:, 2 * tt + 1, :])
                    dve.drain()
                    v.tensor_copy(i1f, i1u)
                    v.tensor_copy(i2f, i2u)
                    v.tensor_tensor(cand, v1f.unsqueeze(2).broadcast_to([P, TOPK, TOPK]),
                                    v2f.unsqueeze(1).broadcast_to([P, TOPK, TOPK]), ALU.add)
                    dve.drain()
                    top16(vs, ic, cand.rearrange("p a b -> p (a b)"))
                    dve.drain()
                    v.tensor_scalar(ich, ic, 4, None, ALU.logical_shift_right)
                    v.tensor_scalar(icl, ic, 15, None, ALU.bitwise_and)
                    dve.drain()
                    v.tensor_copy(chf, ich)
                    v.tensor_copy(clf, icl)
                    dve.drain()
                    for cf, hot, idx, w in ((chf, hot1, i1f, 0), (clf, hot2, i2f, 1)):
                        v.tensor_tensor(hot, cf.unsqueeze(2).broadcast_to([P, TOPK, TOPK]), iota16, ALU.is_equal)
                        dve.drain()
                        v.tensor_tensor(hot, hot, idx.unsqueeze(1).broadcast_to([P, TOPK, TOPK]), ALU.mult)
                        dve.drain()
                        v.tensor_reduce(picked[:, w, tt, bass.ds(i, 1), :].rearrange("p a b -> p (a b)"), hot, AX, ALU.add)
                    v.tensor_copy(picked[:, 2, tt, bass.ds(i, 1), :].rearrange("p a b -> p (a b)"), vs)
                    dve.drain()
                dve.drain()
            v.tensor_copy(pmax, picked[:, 2, :, :, 0])
            dve.drain()
            for tt in range(2):
                v.tensor_tensor(picked[:, 2, tt], picked[:, 2, tt],
                                pmax[:, tt].unsqueeze(2).broadcast_to([P, HEADS, TOPK]), ALU.subtract)
            dve.drain().then_inc(s("vs_ready"), 1)
            dve.wait_ge(s("vs_exp"), 1)
            v.tensor_reduce(psum_, picked[:, 2], AX, ALU.add)
            dve.drain()
            v.reciprocal(prec, psum_)
            dve.drain()
            for tt in range(2):
                v.tensor_tensor(picked[:, 2, tt], picked[:, 2, tt],
                                prec[:, tt].unsqueeze(2).broadcast_to([P, HEADS, TOPK]), ALU.mult)
            dve.drain().then_inc(s("picked_ready"), 1)
            meet(dve, met)

            def one_hots(unit, tok):
                for h in range(2):
                    dve.wait_ge(s("hot_used"), 2 * unit + h + 1)
                    for j in range(8):
                        t = tok + 8 * h + j
                        v.tensor_scalar(hotA[:, h, j, :], iota[:], cols[:, 0, bass.ds(t, 1)],
                                        cols[:, 2, bass.ds(t, 1)], ALU.is_equal, ALU.mult)
                    v.tensor_tensor(hotB[:, h], iota[:, 0:QW].unsqueeze(1).broadcast_to([P, 8, QW]),
                                    cols[:, 1, bass.ds(tok + 8 * h, 8)].unsqueeze(2).broadcast_to([P, 8, QW]),
                                    ALU.is_equal)
                    dve.drain().then_inc(s("hot_ready"), 1)

            with dve.Fori(0, 4) as i:
                for u in range(4):
                    one_hots(4 * i + u, 64 * i + 16 * u)
            with dve.Fori(0, 2) as o:
                for par in range(2):
                    dve.wait_ge(s("wd_copied"), 2 + 16 + 32 * o + 16 * par)
                    v.tensor_scalar(cols[:, 1, :], cols[:, 1, :], float(QW), None, ALU.subtract)
                    dve.drain()
                    with dve.Fori(0, 4) as q:
                        g = 8 * o + 4 * par + q
                        one_hots(4 * g + 16, 64 * q)
                        for slot in range(8):
                            dve.wait_ge(s("gelu_ready"), 8 * g + slot + 1)
                            v.tensor_tensor(G[:, slot, :], GL[:, slot % 4, :],
                                            Wd[:, par, bass.ds(8 * q + slot, 1), :], ALU.mult).then_inc(s("g_ready"), 1)
                            dve.drain().then_inc(s("gelu_free"), 1)
                            if slot == 3:
                                one_hots(4 * g + 17, 64 * q + 16)
                        one_hots(4 * g + 18, 64 * q + 32)
                        for slot in range(8):
                            used("peer", 2 * g + 1, slot)
                            for dd in range(2):
                                m = 2 * slot + dd
                                v.scalar_tensor_tensor(x[:, m, :], banks[slot % 4][:, T * dd:T * dd + T],
                                                       mod[:, 80 + m:81 + m], x[:, m, :], ALU.mult, ALU.add)
                            dve.drain().then_inc(bank_free[slot % 4], 1)
                            if slot == 3:
                                one_hots(4 * g + 19, 64 * q + 48)
            meet(dve, met)
            take_mod(96, 192, "between", 16)
            dve.wait_ge(s("disc_a"), 1)
            lr, li = bl[:, 0], bl[:, 1]
            dt = bst_.unsqueeze(2).broadcast_to([P, KT, 64])
            v.tensor_tensor(e[0], lr, dt, ALU.mult)
            v.tensor_tensor(e[1], li, dt, ALU.mult)
            v.tensor_tensor(pe_[0], V("lam_re"), pst, ALU.mult)
            v.tensor_tensor(pe_[1], V("lam_im"), pst, ALU.mult)
            dve.drain()

            def to_turns(ang, tmp):
                v.tensor_scalar(ang, ang, 1.0 / (2 * np.pi), None, ALU.mult)
                dve.drain()
                v.tensor_scalar(tmp, ang, MAGIC, None, ALU.add)
                dve.drain()
                v.tensor_scalar(tmp, tmp, MAGIC, None, ALU.subtract)
                dve.drain()
                v.tensor_tensor(ang, ang, tmp, ALU.subtract)
                dve.drain()

            to_turns(e[1], e[2])
            to_turns(pe_[1], pe_[2])
            v.tensor_copy(theta[:, 0:PAIRS], pe_[1])
            v.memset(theta[:, PAIRS:PAIRS + 4], 0.0)
            dve.drain().then_inc(s("disc_b"), 1)
            v.tensor_tensor(e[4], lr, lr, ALU.mult)
            v.tensor_tensor(e[5], li, li, ALU.mult)
            dve.drain()
            v.tensor_tensor(e[4], e[4], e[5], ALU.add)
            dve.drain()
            v.reciprocal(e[4], e[4])
            dve.wait_ge(s("disc_c"), 1)
            v.tensor_tensor(e[2], e[0], e[2], ALU.mult)
            v.tensor_tensor(e[3], e[0], e[3], ALU.mult)
            dve.drain()
            v.tensor_scalar(e[2], e[2], 1.0, None, ALU.subtract)
            dve.drain()
            v.tensor_tensor(e[0], e[2], lr, ALU.mult)
            v.tensor_tensor(e[1], e[3], li, ALU.mult)
            v.tensor_tensor(e[5], e[3], lr, ALU.mult)
            v.tensor_tensor(e[6], e[2], li, ALU.mult)
            dve.drain()
            v.tensor_tensor(e[0], e[0], e[1], ALU.add)
            v.tensor_tensor(e[5], e[5], e[6], ALU.subtract)
            dve.drain()
            v.tensor_tensor(e[0], e[0], e[4], ALU.mult)
            v.tensor_tensor(e[5], e[5], e[4], ALU.mult)
            dve.drain()
            v.tensor_tensor(BB[:, 0], e[0], br_[:, 0], ALU.mult)
            v.tensor_tensor(e[1], e[5], br_[:, 1], ALU.mult)
            v.tensor_tensor(BB[:, 1], e[0], br_[:, 1], ALU.mult)
            v.tensor_tensor(e[2], e[5], br_[:, 0], ALU.mult)
            dve.drain()
            v.tensor_tensor(BB[:, 0], BB[:, 0], e[1], ALU.subtract)
            v.tensor_tensor(BB[:, 1], BB[:, 1], e[2], ALU.add)
            v.tensor_scalar(CC[:, 1], CC[:, 0], -1.0, None, ALU.mult)
            v.tensor_scalar(CC[:, 2], CC[:, 2], -1.0, None, ALU.mult)
            dve.drain().then_inc(s("disc_done"), 1)
            meet(dve, met)
            norm_rstd("final", D)
            norm_scale(x, x, V("g_final"))
            dve.drain().then_inc(s("norm_src"), 1)
            modulated_gain(2, V("g_l0"), mod[:, 112:128])
            norm_rstd("l0", D)
            norm_scale(H, x, gain[:, 2, :], "scaled_ready")
            meet(dve, met)
            with dve.Fori(0, 8) as i:
                for t in range(2):
                    tile = 2 * i + t
                    for j in range(4):
                        duo, k = j // 2, j % 2
                        bu = (WA, WB)[j % 2][:].rearrange("p (a b) -> p a b", a=2)
                        dve.wait_ge(s("table_ready"), 2 * tile + duo + 1)
                        dve.wait_ge(s("bu_in_psum"), 4 * tile + j + 1)
                        v.tensor_tensor(P1, bu, tab[:, duo, 0, k:k + 1, :].broadcast_to([P, 2, T]), ALU.mult)
                        v.tensor_tensor(P2, bu, tab[:, duo, 1, k:k + 1, :].broadcast_to([P, 2, T]), ALU.mult)
                        dve.drain().then_inc(s("bu_read"), 1)
                        v.tensor_tensor(Wr[:, 0, :], P1[:, 0, :], P2[:, 1, :], ALU.add)
                        v.tensor_tensor(Wr[:, 1, :], P1[:, 1, :], P2[:, 0, :], ALU.subtract)
                        dve.drain()
                        dve.wait_ge(s("q_ready"), 4 + 4 * tile + j - 1)
                        m = mag[:, bass.ds(4 * tile + j, 1)].broadcast_to([P, T])
                        for ri in range(2):
                            v.tensor_tensor_scan(Z[:, j % 2, ri, :], m, Wr[:, ri, :], 0.0, ALU.mult, ALU.add)
                        dve.drain().then_inc(s("z_ready"), 1)
                    dve.wait_ge(s("y_pair"), 4 * tile + 9)
                    v.scalar_tensor_tensor(Y[:, bass.ds(tile, 1), :], Us[:, t, :], V("ssm_d")[:, bass.ds(tile, 1)],
                                           WC[:, 0:T], ALU.mult, ALU.add)
                    dve.drain().then_inc(s("y_read"), 1)
            take_mod(192, 224, "ssm", 64)
            dve.sem_inc(s("glu_free"), 2)
            with dve.Fori(0, 2) as i:
                for slot in range(8):
                    m = 8 * i + slot
                    dve.wait_ge(s("sig_ready"), m + 1)
                    v.tensor_tensor(H[:, bass.ds(m, 1), :], glt[:, slot % 2, :], Y[:, bass.ds(m, 1), :], ALU.mult)
                    dve.drain().then_inc(s("glu_free"), 1)
                    v.tensor_tensor(H[:, bass.ds(m, 1), :], H[:, bass.ds(m, 1), :], SZ[:, bass.ds(m, 1), :], ALU.mult)\
                        .then_inc(s("glu_done"), 1)
            with dve.Fori(0, 2) as i:
                for slot in range(8):
                    residual("ssm_out", i, slot, mod[:, 128:144])
            meet(dve, met)
            modulated_gain(3, V("g_kv"), mod[:, 208:224])
            modulated_gain(4, V("g_l1"), mod[:, 160:176])
            norm_rstd("l1", D)
            norm_scale(H, x, gain[:, 3, :], "scaled_ready")
            dve.wait_ge(s("cmp1_in_psum"), 1)
            v.tensor_tensor(b1e, WC[:, 128:130], V("cmp_b1"), ALU.add).then_inc(s("b1e_ready"), 1)
            norm_scale(H, x, gain[:, 4, :], "scaled_ready")
            meet(dve, met)
            gates = GT.rearrange("p t (b n) -> p t b n", b=3)
            with dve.Fori(0, KV) as g:
                for hh in range(HPG):
                    n = 4 * g + hh
                    dve.wait_ge(s("sn_in_psum"), n + 1)
                    for br in range(2):
                        w = (WA, WB)[br]
                        v.tensor_reduce(mx[:, 2 * br:2 * br + 1], w[:, 0:P], AX, ALU.max)
                        v.tensor_reduce(mx[:, 2 * br + 1:2 * br + 2], w[:, P:3 * P], AX, ALU.max)
                    v.tensor_reduce(mx[:, 4:6], WC[:, 0:32].rearrange("p (a b) -> p a b", a=2)[:, :, 0:NCMP], AX, ALU.max)
                    dve.drain()
                    v.tensor_scalar(mx, mx, -1.0, None, ALU.mult).then_inc(s("negmax2"), 1)
                    dve.wait_ge(s("exps2"), n + 1)
                    v.reciprocal(rc, sm)
                    dve.drain()
                    for k, br in enumerate((1, 2, 0)):
                        v.tensor_tensor(rc[:, 2 * k:2 * k + 2], rc[:, 2 * k:2 * k + 2],
                                        gates[:, :, br, bass.ds(n, 1)].rearrange("p a b -> p (a b)"), ALU.mult)
                    dve.drain()
                    for br in range(2):
                        v.tensor_scalar(Pn[:, br, 0, :], Pn[:, br, 0, :], rc[:, 2 * br:2 * br + 1], None, ALU.mult)
                        v.tensor_scalar(Pn[:, br, 1:3, :], Pn[:, br, 1:3, :], rc[:, 2 * br + 1:2 * br + 2], None, ALU.mult)
                    for qt in range(2):
                        v.scalar_tensor_tensor(Pc[:, qt, :], Pc[:, qt, :], rc[:, 4 + qt:5 + qt], cmp_one[:, qt, :],
                                               ALU.mult, ALU.mult)
                    dve.drain().then_inc(s("probs2"), 1)
                    dve.wait_ge(s("sz_ready"), 3 * n + 3)
                    dve.wait_ge(s("on_in_psum"), n + 1 + 1)
                    v.tensor_tensor(ot[:, 0, :], WA[:, 0:T], SZn[:, hh % 2, 1, :], ALU.mult)
                    v.tensor_tensor(ot[:, 1, :], WB[:, 0:T], SZn[:, hh % 2, 2, :], ALU.mult)
                    v.tensor_tensor(ot[:, 2, :], WC[:, 0:T], SZn[:, hh % 2, 0, :], ALU.mult)
                    dve.drain()
                    v.tensor_tensor(ot[:, 0, :], ot[:, 0, :], ot[:, 1, :], ALU.add)
                    dve.drain()
                    v.tensor_tensor(O[:, bass.ds(n, 1), :], ot[:, 0, :], ot[:, 2, :], ALU.add)
                    dve.drain().then_inc(s("combined"), 1)
            with dve.Fori(0, 2) as i:
                for slot in range(8):
                    residual("w_o", i, slot, mod[:, 176:192])
            meet(dve, met)
            norm_rstd("final2", D)
            norm_scale(H, x, V("g_final2"))
            dve.drain().then_inc(s("out_ready"), 1)

        @block.gpsimd
        def _(pool):
            gp = nc.gpsimd
            met = [0]
            gp.memset(ones[:], 1.0)
            gp.iota(itmp[:], [[1, T]], base=0, channel_multiplier=0)
            pool.drain()
            gp.tensor_copy(iota_t[:], itmp[:])
            gp.tensor_copy(iota[:], itmp[:, 0:P])

            def select(out, src, base, pattern, cm_, op, fill):
                pool.drain()
                gp.affine_select(out=out, in_=src, compare_op=op, fill=fill, base=base, pattern=pattern,
                                 channel_multiplier=cm_)

            select(ident[:], ones[:, 0:P], 0, [[-1, P]], 1, ALU.is_equal, 0.0)
            gp.memset(causal[:], 0.0)
            select(causal[:], causal[:], 0, [[-1, P]], 1, ALU.is_ge, NEG)
            gp.memset(cmp_neg[:], 0.0)
            select(cmp_neg[:], cmp_neg[:], -31, [[P, 2], [-16, NCMP]], 1, ALU.is_ge, NEG)
            gp.memset(cmp_one[:], 1.0)
            select(cmp_one[:], cmp_one[:], -31, [[P, 2], [-16, NCMP]], 1, ALU.is_ge, 0.0)
            select(in16[:], ones[:, 0:8], 0, [[-16, 8]], 1, ALU.is_ge, 0.0)
            select(in16[:], in16[:], 15, [[16, 8]], -1, ALU.is_ge, 0.0)
            select(in64[:], ones[:, 0:2], 0, [[-64, 2]], 1, ALU.is_ge, 0.0)
            select(in64[:], in64[:], 63, [[64, 2]], -1, ALU.is_ge, 0.0)
            pool.drain()
            i16 = in16[:].rearrange("p (a b) -> p b a", b=2)
            gp.tensor_tensor(par16[:], i16[:, :, 0], i16[:, :, 1], ALU.add)
            for k in (2, 3):
                pool.drain()
                gp.tensor_tensor(par16[:], par16[:], i16[:, :, k], ALU.add)
            pool.drain().then_inc(s("consts_ready"), 1)
            meet(pool, met)
            meet(pool, met)
            pool.sem_inc(s("gelu_free"), 4)
            meet(pool, met)
            meet(pool, met)
            pool.sem_inc(s("q_ready"), 4)
            pool.sem_inc(s("y_pair"), 5)
            pool.sem_inc(s("y_read"), 2)
            meet(pool, met)

            def fraction(n):
                pool.wait_ge(s("phase_ready"), n + 1)
                gp.tensor_tensor(ph, ph, rn, ALU.subtract)
                pool.drain().then_inc(s("frac_ready"), 1)

            fraction(0)
            fraction(1)
            with pool.Fori(0, 8) as i:
                for t in range(2):
                    tile = 2 * i + t
                    pool.wait_ge(s("y_pair"), 4 * tile + 1)
                    for ri in range(2):
                        gp.tensor_tensor(Bst[:, t, ri], BB[:, ri, bass.ds(tile, 1), :].broadcast_to([P, 2, 64]),
                                         par16[:].unsqueeze(2).broadcast_to([P, 2, 64]), ALU.mult)
                    for kind in range(3):
                        gp.tensor_tensor(Cst[:, t, kind],
                                         CC[:, kind, bass.ds(4 * tile, 4), :].unsqueeze(2).broadcast_to([P, 4, 2, 16]),
                                         in64[:].unsqueeze(1).unsqueeze(3).broadcast_to([P, 4, 2, 16]), ALU.mult)
                    pool.drain().then_inc(s("masks_built"), 1)
                    for j in range(4):
                        duo, k = j // 2, j % 2
                        pool.wait_ge(s("z_ready"), 4 * tile + j + 1)
                        pool.wait_ge(s("y_pair"), 4 * tile + j + 4)
                        gp.tensor_tensor(Q1[:, j % 2], Z[:, j % 2], tab[:, duo, 0, k:k + 1, :].broadcast_to([P, 2, T]), ALU.mult)
                        gp.tensor_tensor(Q2[:, j % 2], Z[:, j % 2], tab[:, duo, 1, k:k + 1, :].broadcast_to([P, 2, T]), ALU.mult)
                        pool.drain().then_inc(s("q_ready"), 1)
                        if j % 2 == 1:
                            fraction(2 * tile + 2 + duo)
            meet(pool, met)
            meet(pool, met)
            with pool.Fori(0, KV) as g:
                pool.wait_ge(s("on_in_psum"), 4 * g + 1)
                gp.tensor_copy(Vg, VR[:, bass.ds(g, 1)].rearrange("p g a b c -> p (g a) b c"))
                gp.tensor_copy(VCg[0:NCMP], VCr[0:NCMP, bass.ds(g, 1), :].rearrange("p a b -> p (a b)"))
                pool.drain().then_inc(s("vg_ready"), 1)
            meet(pool, met)


def _tiles(w):
    return np.ascontiguousarray(w.reshape(KT, P, w.shape[1] // P, P).transpose(2, 1, 0, 3))


def _cols(v):
    return v.reshape(-1, P).T


def kernel(**inputs):
    import concourse.bacc as bacc
    from concourse.bass_utils import run_bass_kernel_spmd
    i = {k: np.asarray(v) for k, v in inputs.items()}
    w_in = i["w_in"][0]
    heads = [w_in[:, off + P * h:off + P * (h + 1)] for h in range(HEADS) for off in (0, 1024, 2048, 3080, 4104)]
    qg = i["nsa_w_qg_2"][0]
    qz = []
    for g in range(KV):
        qz += [qg[:, P * (HPG * g + h):P * (HPG * g + h + 1)] for h in range(HPG)]
        qz += [qg[:, 2096 + P * (16 * b + HPG * g + h):2096 + P * (16 * b + HPG * g + h + 1)]
               for h in range(HPG) for b in range(3)]
    vecs = dict(
        c=_cols(i["c"]), c2=_cols(i["c_2"]), b_ada=_cols(i["b_ada"]),
        b_mod2=np.concatenate([_cols(i["mod_b_2"]), _cols(i["kv_mod_b_2"])], axis=1),
        g_mix=_cols(i["g_mix"]), g_ffn=_cols(i["g_ffn"]), g_final=_cols(i["g_final"]),
        g_merge=np.concatenate([_cols(i["g_attn_out"]), _cols(i["g_lru_out"])], axis=1),
        g_l0=_cols(i["norm_g_2"][0]), g_l1=_cols(i["norm_g_2"][1]), g_kv=_cols(i["kv_norm_g_2"]),
        g_final2=_cols(i["final_norm_g_2"]),
        conv_w=i["conv_w"][0].reshape(4, HEADS, P).transpose(2, 1, 0).reshape(P, 32),
        conv_b=_cols(i["conv_b"]), lru_b_a=_cols(i["lru_b_a"]), lru_b_x=_cols(i["lru_b_x"]),
        lru_lambda=_cols(i["lru_lambda"]), ssm_d=_cols(i["ssm_d_2"]), b_glu=_cols(i["ssm_b_glu_2"]),
        cmp_b1=_cols(i["cmp_b1_2"]), cmp_b2=_cols(i["cmp_b2_2"]), cmp_pe=_cols(i["cmp_pe_2"]),
        lam_re=i["ssm_lam_re_2"].reshape(PAIRS, P).T, lam_im=i["ssm_lam_im_2"].reshape(PAIRS, P).T)
    arrays = dict(
        x=i["x"][0].reshape(T, KT, P).transpose(2, 1, 0),
        vec=np.concatenate([vecs[n] for n, _ in VEC], axis=1),
        w_f=w_in[:, 3072:3080].reshape(KT, P, 8).transpose(1, 0, 2),
        b_f=i["b_f"].reshape(8, 1),
        w_ada=_tiles(i["w_ada"][0]),
        w_in=_tiles(np.concatenate(heads, axis=1)),
        gate_w=np.stack([i["lru_w_a"][0], i["lru_w_x"][0]], axis=2).reshape(HEADS, P, 2, P),
        w_out=_tiles(i["w_out"][0]),
        w_q=_tiles(i["peer_w_q"][0]),
        k12=np.stack([i["peer_k1"][0], i["peer_k2"][0]]).transpose(3, 0, 1, 2),
        w_mod2=_tiles(np.concatenate([i["mod_w_2"][0], i["mod_w_2"][1], i["kv_mod_w_2"]], axis=1)),
        peer_u=i["peer_u"][0].reshape(P, P, KT, P).transpose(1, 3, 2, 0),
        peer_v=i["peer_v"][0].reshape(P, 16, 8, 8, 2 * P).transpose(1, 3, 0, 2, 4).reshape(P, P, KT, P),
        ssm_in=_tiles(i["ssm_w_in_2"][0]),
        step_pair=i["ssm_log_step_2"].reshape(PAIRS, 2).T,
        step_tile=i["ssm_log_step_2"].reshape(KT, 8).T,
        lam_tile=np.stack([i["ssm_lam_re_2"].reshape(KT, 8, 64), i["ssm_lam_im_2"].reshape(KT, 8, 64)]).transpose(2, 0, 1, 3),
        ssm_b=np.stack([i["ssm_b_re_2"], i["ssm_b_im_2"]]).reshape(2, KT, 8, 64, 16).transpose(2, 4, 0, 1, 3).reshape(P, 2, KT, 64),
        ssm_c=np.stack([i["ssm_c_re_2"], i["ssm_c_im_2"]]).reshape(2, PAIRS, 2, 16, 64).transpose(2, 4, 0, 1, 3).reshape(P, 2, PAIRS, 16),
        w_glu=_tiles(i["ssm_w_glu_2"][0]), ssm_out=_tiles(i["ssm_w_out_2"][0]),
        w_kv=_tiles(i["w_kv_2"]),
        cmp_w1=i["cmp_w1_2"].reshape(2, CMP_L, P, P).transpose(2, 0, 1, 3),
        cmp_w2=i["cmp_w2_2"].transpose(1, 0, 2),
        w_gate=qg[:, 2048:2096].reshape(KT, P, 48).transpose(1, 0, 2),
        w_qz=_tiles(np.concatenate(qz, axis=1)), w_o=_tiles(i["nsa_w_o_2"][0]))
    nc = bacc.Bacc("TRN2", target_bir_lowering=False, num_devices=1)
    feed, aps = {}, {}
    for name, value in arrays.items():
        feed["in_" + name] = np.ascontiguousarray(value)
        aps[name] = nc.dram_tensor("in_" + name, value.shape, mybir.dt.from_np(value.dtype), kind="ExternalInput").ap()
    aps["out"] = nc.dram_tensor("out_0", (P, KT, T), F32, kind="ExternalOutput").ap()
    build(nc, aps)
    res = run_bass_kernel_spmd(nc, [feed], core_ids=[0])
    return np.ascontiguousarray(res.results[0]["out_0"].transpose(2, 1, 0)).reshape(1, T, D)
```

```python
import concourse.bass as bass
from concourse import mybir
from contextlib import ExitStack
import numpy as np

F32 = mybir.dt.float32
F32R = mybir.dt.float32r
BF16 = mybir.dt.bfloat16
U32 = mybir.dt.uint32
I32 = mybir.dt.int32
ALU = mybir.AluOpType
ACT = mybir.ActivationFunctionType
AX = mybir.AxisListType.X

P = 128
T = 256
D = 2048
KT = D // P
R = 4
HEADS = 8
SCALE = float(P) ** -0.5
EPS = 1e-6
NEG = -1e30
LOW = -3.0e38
LRU_C = 8.0
TOPK = 16
SLOTS = HEADS * TOPK
NQ = 4
QW = P // NQ
KV = 4
HPG = 4
NCMP = (T - 32) // 16 + 1
CMP_L = 32
PAIRS = 64
MAGIC = 12582912.0
TWO_PI = 6.283185
HALF_PI = 1.5707963

STAGES = dict(shift_scale=(4, 8, 0, 2), heads=(8, HEADS, 5, 3), w_out=(20, 2, 8, 12), topk=(8, 4, 4, 0),
              peer=(24, 16, 16, 8), ssm=(4, 8, 4, 0), glu=(8, 2, 8, 0), ssm_out=(8, 2, 8, 0), kv=(8, 3, 8, 0),
              nsa=(16, KV, 16, 0), w_o=(8, 2, 8, 0))
STREAM = [(name, b * n) for name, (b, n, _, _) in STAGES.items()]
CHUNK0, GEMM0, VEC0 = {}, {}, {}
_c = _g = _v = 0
for _name, (_b, _n, _gb, _vb) in STAGES.items():
    CHUNK0[_name], GEMM0[_name], VEC0[_name] = _c, _g, _v
    _c, _g, _v = _c + _b * _n, _g + _gb * _n, _v + _vb * _n
DVE_K = 5


def use_of(stage, i, pos):
    return CHUNK0[stage] // R + (STAGES[stage][0] // R) * i + pos // R


def half_of(stage, i, gemm, half):
    return 2 * (GEMM0[stage] + STAGES[stage][2] * i + gemm) + half


def vec_of(stage, i, n):
    return VEC0[stage] + STAGES[stage][3] * i + n, min(STAGES[stage][3], 4)


VEC = [("c", 16), ("c2", 16), ("b_ada", 96), ("b_mod2", 128), ("g_mix", 16), ("g_ffn", 16),
       ("g_final", 16), ("g_merge", 16), ("g_l0", 16), ("g_l1", 16), ("g_kv", 16), ("g_final2", 16),
       ("conv_w", 32), ("conv_b", 8), ("lru_b_a", 8), ("lru_b_x", 8), ("lru_lambda", 8), ("ssm_d", 16),
       ("b_glu", 16), ("cmp_b1", 2), ("cmp_b2", 2), ("cmp_pe", 64), ("lam_re", 64), ("lam_im", 64)]
VOFF = {}
for _name, _n in VEC:
    VOFF[_name] = sum(n for m, n in VEC if m in VOFF)
NVEC = sum(n for _, n in VEC)


def build(nc, a, debug=None):
    ctx = ExitStack()
    with ctx:
        def sb(name, shape, dt=F32):
            return ctx.enter_context(nc.sbuf_tensor(name, shape, dt))

        def sem(name):
            return ctx.enter_context(nc.semaphore(name))

        ring = sb("ring", [P, R, KT, P])
        x = sb("x", [P, KT, T])
        Hhi = sb("Hhi", [P, KT, T], F32R)
        Hlo = sb("Hlo", [P, KT, T], F32R)
        Ghi = sb("Ghi", [P, 8, T], F32R)
        Glo = sb("Glo", [P, 8, T], F32R)
        whi = sb("whi", [P, 2, 8, P], F32R)
        wlo = sb("wlo", [P, 2, 8, P], F32R)
        vec = sb("vec", [P, NVEC])
        mod = sb("mod", [P, 224])
        gain = sb("gain", [P, 8, KT])
        cond = sb("cond", [P, 2, KT])
        cst = sb("cst", [P, 2])
        ident = sb("ident", [P, P])
        ones = sb("ones", [P, T])
        iota = sb("iota", [P, P])
        iota_t = sb("iota_t", [P, T])
        causal = sb("causal", [P, P])
        cmp_neg = sb("cmp_neg", [P, 2, NCMP])
        cmp_one = sb("cmp_one", [P, 2, NCMP])
        in16 = sb("in16", [P, 8])
        par16 = sb("par16", [P, 2])
        in64 = sb("in64", [P, 2])
        neg64 = sb("neg64", [P, 2])
        ident16 = sb("ident16", [P, P], BF16)
        causal16 = sb("causal16", [P, P], BF16)
        iota16b = sb("iota16b", [P, P], BF16)
        var = sb("var", [P, 2, T])
        sd = sb("sd", [P, 2, T])
        rstd = sb("rstd", [P, 2, T])
        NA = 20544
        arena = sb("arena", [P, NA])
        banks = [ctx.enter_context(nc.psum_tensor(f"bank{i}", [P, 512], F32)) for i in range(4)]
        ps_mod = ctx.enter_context(nc.psum_tensor("ps_mod", [P, 512], F32))
        WA = ctx.enter_context(nc.psum_tensor("work_a", [P, 512], F32))
        WB = ctx.enter_context(nc.psum_tensor("work_b", [P, 512], F32))
        WC = ctx.enter_context(nc.psum_tensor("work_c", [P, 512], F32))

        def V(name, n=None):
            o = VOFF[name]
            return vec[:, o:o + (n or dict(VEC)[name])]

        class Region:
            def __init__(self, at=0):
                self.at = at

            def __call__(self, *shape, parts=P, dt=None):
                n = int(np.prod(shape))
                v = arena[0:parts, self.at:self.at + n]
                self.at += n
                assert self.at <= NA, self.at
                if dt is not None:
                    v = v.bitcast(dt)
                if len(shape) == 1:
                    return v
                names = "abcdef"[:len(shape)]
                return v.rearrange(f"p ({' '.join(names)}) -> p {' '.join(names)}",
                                   **{k: s for k, s in zip(names[1:], shape[1:])})

        r = Region()
        M = r(KT, T)
        Qh, Kh, VTh = r(T), r(T), r(T)
        LX = r(T + 4)
        LY = r(T)
        Vr = r(2, P)
        Pr = r(3, P)
        PT = r(3, P)
        xc, rg, ig, ut, at_, t1, t2, gx = [r(T) for _ in range(8)]
        gate_w = r(2, P)
        w_f = Region(15808)(KT, 8)
        rowmax, rowsum, rowrec = r(2), r(2), r(2)
        sp8, lam_t = r(2, 8), r(3, 8)
        fl = r(6, T, parts=8)
        cm = r(2, T, parts=8)
        SQ = Region(15936)(KT, T)
        itmp = Region(15936)(T, dt=I32)
        b_f = sb("b_f", [8, 1])
        part = arena[:, NA - 4 * P:NA].rearrange("p (a b) -> p a b", a=4)

        r = Region()
        cols = r(5, T)
        Wd = r(2, QW, T)
        GL = r(2, T)
        hotA = arena[:, r.at:r.at + 1024].bitcast(BF16).rearrange("p (a b c) -> p a b c", a=2, b=8)
        r.at += 1024
        hotB = arena[:, r.at:r.at + 768].bitcast(BF16).rearrange("p (a b k c) -> p a b k c", a=2, b=8, k=3)
        r.at += 768
        assert r.at <= NA - 4 * P
        r = Region(5 * T)
        k12 = r(2, HEADS, P)
        Qp = r(2, T)
        S4 = r(4, P)
        v1f, v2f = r(TOPK), r(TOPK)
        i1u, i2u = r(TOPK, dt=U32), r(TOPK, dt=U32)
        i1f, i2f = r(TOPK), r(TOPK)
        cand = r(TOPK, TOPK)
        vs = r(TOPK)
        ic, ich, icl = r(TOPK, dt=U32), r(TOPK, dt=U32), r(TOPK, dt=U32)
        chf, clf = r(TOPK), r(TOPK)
        hot1, hot2 = r(TOPK, TOPK), r(TOPK, TOPK)
        picked = r(3, 2, HEADS, TOPK)
        pmax, psum_, prec = r(2, HEADS), r(2, HEADS), r(2, HEADS)

        r = Region()
        Y = r(KT, T)
        SZ = r(KT, T)
        BB = r(2, KT, 64)
        theta = r(PAIRS + 4)
        mag = r(PAIRS)
        disc = arena[:, 2 * KT * T:r.at]
        CC = r(2, PAIRS, 16)
        ssm_at = r.at
        Bst = r(2, 2, 2, 64)
        Cst = r(2, 2, 4, 2, 16)
        Us = r(2, T)
        tab = r(2, 2, 2, T)
        ph, rn, Wr = sd, rstd, var
        P1, P2 = r(2, T), r(2, T)
        Z = r(2, 2, T)
        Q1, Q2 = r(2, T), r(2, T)
        X = r(2, 2, T)
        glt = P1
        r = Region()
        bl = r(2, KT, 64)
        bst_ = r(KT)
        br_ = r(2, KT, 64)
        pst = r(PAIRS)
        pe_ = [r(PAIRS) for _ in range(3)]
        e = [r(KT, 64) for _ in range(3)]
        assert r.at <= 2 * KT * T
        r = Region(ssm_at - 2 * PAIRS * 16)
        e += [r(KT, 64) for _ in range(4)]
        assert r.at <= 15808

        r = Region()
        KVT = r(6 * KV, T)
        VR = r(KV, 2, 2, P)
        VCr = r(KV, P, parts=16)
        KC, VCt = r(KV, NCMP), r(KV, NCMP)
        wg = r(KT, 48)
        GT = r(2, 48)
        nsa_at = r.at
        W1 = r(CMP_L, P)
        W2 = r(2, P)
        GC = r(KV * NCMP)
        b1e = r(2)
        SQ_end = r.at
        r = Region(nsa_at)
        O = r(KT, T)
        Qg = r(HPG, T)
        Vg = r(2, 2, P)
        VCg = r(P, parts=16)
        Pn = r(2, 3, P)
        Pc = r(2, NCMP)
        PTn = r(2, 3, P)
        PTc = r(2, P, parts=16)
        SZn = r(2, 3, T)
        ot = r(3, T)
        mx, sm, rc = r(6), r(6), r(6)

        slot_loaded = [sem(f"slot{i}_loaded") for i in range(R)]
        slot_free = [sem(f"slot{i}_free") for i in range(R)]
        bank_free = [sem(f"bank{i}_free") for i in range(4)]
        stage_end = sem("stage_end")
        params = sem("params_loaded")
        x_loaded = sem("x_loaded")
        S = {}

        def s(name):
            if name not in S:
                S[name] = sem(name)
            return S[name]

        for name in ("consts_ready cond_ready mod_ready norm_src half_done hi_ready lo_dve lo_pool prod_ready part_ready part_used biased hhi_ready disc_e disc_f disc_g disc_saved lam_ready split_src disc_loaded w1b_used gtmp squares_ready sums_ready var_ready sd_ready "
                     "scaled_ready h_ready f_in_psum f_ready f_abs log1p_ready cum_ready gatew_loaded qk_ready "
                     "vt_ready cm_ready scores_ready negmax_ready exps_ready probs_ready xc_ready gates_in_psum "
                     "lru_u_ready lru_t_ready lru_sq_ready ly_ready lru_done vrows_in_psum vrows_ready "
                     "pt_in_psum pt_ready attn_in_psum attn_ready merged_ready k_loaded peerq_ready s_in_psum "
                     "s_ready s_free vs_ready vs_exp picked_ready cols_in_psum cols_ready hot_ready hot_used "
                     "wd_copied gelu_ready g_ready ssm_loaded disc_a disc_b disc_c disc_d "
                     "disc_done masks_built u_ready bu_in_psum bu_read phase_ready frac_ready table_ready "
                     "z_ready q_ready y_pair gelu_free glu_free y_read y_gelu sig_ready glu_done "
                     "w1_loaded kv_ready vr_in_psum vr_ready cmp1_in_psum b1e_ready cmp_gelu cmp2_in_psum "
                     "kc_ready vc_in_psum vc_ready gt_in_psum gt_ready vg_ready q_ready2 sn_in_psum negmax2 "
                     "exps2 probs2 ptn_in_psum ptn_ready on_in_psum sz_ready combined out_ready stored").split():
            s(name)

        block = ctx.enter_context(nc.Block())

        def meet(eng, state):
            eng.drain().then_inc(stage_end, 1)
            state[0] += 4
            eng.wait_ge(stage_end, state[0])

        def norm_groups(g):
            return [(j, 0 if g == 1 or j < 2 else 1) for j in range(4)]


        GRANTED = dict(pe=('gates_in_psum', 's_in_psum', 'on_in_psum'), act=('attn_ready', 'pt_ready', 'lru_u_ready'),
                       dve=('lru_done', 's_ready', 'g_ready', 'combined'))

        NORMS = dict(mix=0, merged=1, ffn=2, final=3, l0=4, l1=5, final2=6)

        POOL_VECS = dict(shift_scale=0, heads=2, w_out=9, peer=8)
        POOL_VEC0 = dict(shift_scale=0, heads=0, w_out=2 * HEADS, peer=2 * HEADS + 18)
        half_done = s("half_done")
        SPLITS = dict(mix=0, merged=1, ffn=2, l0=3, y=4, glu=5, kv=6, l1=7, o=8)

        def loaded(eng, stage, i, pos):
            eng.wait_ge(slot_loaded[pos % R], 16 * (use_of(stage, i, pos) + 1))

        def product(eng, stage, i, gemm):
            eng.wait_ge(half_done, half_of(stage, i, gemm, 1) + 3)

        def half_chunk(pos, half, by_column=False):
            if by_column:
                return ring[:, pos % R].rearrange("p k n -> p (k n)")\
                    .rearrange("p (k n) -> p k n", k=8)[:, :, P * half:P * half + P]
            return ring[:, pos % R, 8 * half:8 * half + 8, :]

        @block.sync
        def _(sp):
            def load(stage, i, pos, src, first=False):
                if not first:
                    sp.wait_ge(slot_free[pos % R], 2 * use_of(stage, i, pos))
                sp.dma_start(ring[:, pos % R], src).then_inc(slot_loaded[pos % R], 16)

            def plain(stage, src, at=0):
                body, n = STAGES[stage][0:2]
                with sp.Fori(0, n) as i:
                    for pos in range(body):
                        load(stage, i, pos, src[at + body * i + pos])

            sp.dma_start(x[:], a["x"]).then_inc(x_loaded, 16)
            for pos in range(4):
                load("shift_scale", 0, pos, a["w_ada"][pos], first=True)
            with sp.Fori(1, 8) as i:
                for pos in range(4):
                    load("shift_scale", i, pos, a["w_ada"][4 * i + pos])
            sp.wait_ge(stage_end, 4)
            with sp.Fori(0, HEADS) as i:
                for pos in range(5):
                    load("heads", i, pos, a["w_in"][5 * i + pos])
                sp.wait_ge(s("gates_in_psum"), i + 1)
                sp.dma_start(gate_w, a["gate_w"][i]).then_inc(s("gatew_loaded"), 16)
                for pos in range(3):
                    load("heads", i, 5 + pos, a["w_ada"][32 + 3 * i + pos])
            with sp.Fori(0, 2) as i:
                for m in range(4):
                    for k, pos in enumerate((0, 1, 2, 3, 4)):
                        src = a["w_out"][8 * i + 2 * m + k // 2] if k in (0, 2) else \
                            a["w_ada"][56 + 12 * i + 3 * m + (0, 0, 0, 1, 2)[k]]
                        load("w_out", i, 5 * m + pos, src)
            with sp.Fori(0, 4) as i:
                for h in range(2):
                    for k in range(2):
                        load("topk", i, 4 * h + k, a["w_q"][4 * i + 2 * h + k])
                    for k in range(2):
                        load("topk", i, 4 * h + 2 + k, a["w_ada"][80 + 4 * i + 2 * h + k])
            with sp.Fori(0, 16) as g:
                for half, name in enumerate(("peer_u", "peer_v")):
                    for m in range(4):
                        for k in range(2):
                            load("peer", g, 12 * half + 3 * m + k, a[name][8 * g + 2 * m + k])
                        load("peer", g, 12 * half + 3 * m + 2, a["w_mod2"][8 * g + 4 * half + m])
            with sp.Fori(0, 8) as i:
                for t in range(2):
                    load("ssm", i, 2 * t, a["ssm_in"][2 * i + t])
                    load("ssm", i, 2 * t + 1, a["ssm_in"][KT + 2 * i + t])
            plain("glu", a["w_glu"])
            plain("ssm_out", a["ssm_out"])
            plain("kv", a["w_kv"])
            plain("nsa", a["w_qz"])
            plain("w_o", a["w_o"])
            sp.wait_ge(s("out_ready"), 1)
            sp.dma_start(a["out"], SQ).then_inc(s("stored"), 16)
            sp.wait_ge(s("stored"), 16)

        @block.tensor
        def _(pe):
            mm = nc.tensor.matmul
            met = [0]
            uses = [0, 0, 0, 0]

            def gemm(stage, i, g, out, bank, need=None, rhs=(Hhi, Hlo)):
                if need is not None:
                    pe.wait_ge(bank_free[bank], need + 1)
                for half in range(2):
                    n = half_of(stage, i, g, half)
                    pe.wait_ge(s("hi_ready"), n + 1)
                    for k in range(8):
                        kk = 8 * half + k
                        mm(out, whi[:, half, k, :], rhs[0][:, kk, :], start=(kk == 0), stop=False)
                        mm(out, whi[:, half, k, :], rhs[1][:, kk, :], start=False, stop=False)
                    pe.wait_ge(s("lo_dve"), n + 1)
                    pe.wait_ge(s("lo_pool"), n + 1)
                    for k in range(8):
                        kk = 8 * half + k
                        last = mm(out, wlo[:, half, k, :], rhs[0][:, kk, :], start=False, stop=(kk == KT - 1))
                    last.then_inc(half_done, 1)

            def gemm_v(g, n_, bank, need):
                pe.wait_ge(bank_free[bank], need + 1)
                for dd in range(2):
                    n = half_of("peer", g, 8 + n_, dd)
                    out = banks[bank][:, T * dd:T * dd + T]
                    pe.wait_ge(s("hi_ready"), n + 1)
                    for k in range(8):
                        if n_ == 0 and dd == 0:
                            pe.wait_ge(s("g_ready"), 8 * g + k + 2)
                        mm(out, whi[:, dd, k, :], Ghi[:, k, :], start=(k == 0), stop=False)
                        mm(out, whi[:, dd, k, :], Glo[:, k, :], start=False, stop=False)
                    pe.wait_ge(s("lo_dve"), n + 1)
                    pe.wait_ge(s("lo_pool"), n + 1)
                    for k in range(8):
                        last = mm(out, wlo[:, dd, k, :], Ghi[:, k, :], start=False, stop=(k == 7))
                    last.then_inc(half_done, 1)

            def column(col):
                return ps_mod[:, bass.ds(col, 1)]

            def vec_on_tensor(stage, i, pos, which, col):
                loaded(pe, stage, i, pos)
                for k in range(KT):
                    last = mm(column(col), ring[:, pos % R, k, :], cond[:, which, k:k + 1],
                              start=(k == 0), stop=(k == KT - 1))
                last.then_inc(slot_free[pos % R], 2)

            def vec_fold(stage, i, n, col):
                v_, _ = vec_of(stage, i, n)
                pe.wait_ge(s("part_ready"), v_ + 1)
                mm(column(col), part[:, n % 4, :], ones[:, 0:1], start=True, stop=True).then_inc(s("part_used"), 1)

            def norm_sums(name, groups=1):
                n = NORMS[name]
                for j, g in norm_groups(groups):
                    pe.wait_ge(s("squares_ready"), 4 * n + j + 1)
                    for k in range(4):
                        t = 4 * j + k
                        last = mm(WA[:, g * T:(g + 1) * T], ones[:, 0:P], SQ[:, t, :],
                                  start=(t % (KT // groups) == 0), stop=(t % (KT // groups) == KT // groups - 1))
                last.then_inc(s("sums_ready"), 1)

            def split_done(name):
                pe.wait_ge(s("h_ready"), 4 * (SPLITS[name] + 1))

            def plain(stage):
                body, n = STAGES[stage][0:2]
                with pe.Fori(0, n) as i:
                    for g in range(body):
                        gemm(stage, i, g, banks[g % 4][:, 0:T], g % 4, uses[g % 4] + body // 4 * i + g // 4)
                for b in range(4):
                    uses[b] += body * n // 4

            for name in GRANTED["pe"]:
                pe.sem_inc(s(name), 1)
            pe.sem_inc(half_done, 2)
            pe.sem_inc(s("part_used"), 4)
            pe.wait_ge(s("consts_ready"), 1)
            norm_sums("mix")
            pe.wait_ge(s("cond_ready"), 1)
            with pe.Fori(0, 8) as i:
                vec_on_tensor("shift_scale", i, 0, 0, 4 * i)
                vec_on_tensor("shift_scale", i, 2, 0, 4 * i + 2)
                for n in range(2):
                    vec_fold("shift_scale", i, n, 4 * i + 1 + 2 * n)
            pe.drain().then_inc(s("mod_ready"), 1)
            meet(pe, met)
            split_done("mix")
            for k in range(KT):
                last = mm(WB[0:8, 0:T], w_f[:, k, :], SQ[:, k, :], start=(k == 0), stop=(k == KT - 1))
            last.then_inc(s("f_in_psum"), 1)
            pe.wait_ge(s("cum_ready"), 1)
            with pe.Fori(0, HEADS) as i:
                gemm("heads", i, 0, banks[0][:, 0:T], 0, i)
                gemm("heads", i, 1, banks[0][:, T:2 * T], 0)
                gemm("heads", i, 2, banks[1][:, 0:T], 1, i)
                gemm("heads", i, 3, banks[2][:, 0:T], 2, i)
                pe.wait_ge(s("qk_ready"), i + 1)
                pe.wait_ge(s("cm_ready"), i + 1)
                pe.wait_ge(s("attn_ready"), i + 1)
                for qt in range(2):
                    nk = P * (qt + 1)
                    out = WA[:, P * qt:P * qt + nk]
                    mm(out, Qh[:, P * qt:P * qt + P], Kh[:, 0:nk], start=True, stop=False)
                    mm(out, cm[:, 0, P * qt:P * qt + P], ones[0:8, 0:nk], start=False, stop=False)
                    mm(out, ones[0:8, 0:P], cm[:, 1, 0:nk], start=False, stop=False)
                    last = mm(out[:, P * qt:P * qt + P], ident16[:], causal16[:], start=False, stop=True)
                last.then_inc(s("scores_ready"), 1)
                gemm("heads", i, 4, banks[3][:, 0:T], 3, i)
                pe.wait_ge(s("vt_ready"), i + 1)
                pe.wait_ge(s("pt_ready"), i + 1)
                for kt in range(2):
                    last = nc.tensor.transpose(WB[:, P * kt:P * kt + P], VTh[:, P * kt:P * kt + P], ident[:])
                last.then_inc(s("vrows_in_psum"), 1)
                pe.wait_ge(s("xc_ready"), i + 1)
                pe.wait_ge(s("gatew_loaded"), 16 * (i + 1))
                pe.wait_ge(s("lru_u_ready"), i + 1)
                for g in range(2):
                    last = mm(WC[:, T * g:T * g + T], gate_w[:, g, :], xc, start=True, stop=True)
                last.then_inc(s("gates_in_psum"), 1)
                pe.wait_ge(s("probs_ready"), i + 1)
                pe.wait_ge(s("vrows_ready"), i + 1)
                for b in range(3):
                    last = nc.tensor.transpose(WB[:, P * b:P * b + P], Pr[:, b, :], ident[:])
                last.then_inc(s("pt_in_psum"), 1)
                vec_fold("heads", i, 0, 32 + 3 * i)
                pe.wait_ge(s("pt_ready"), i + 2)
                mm(WA[:, 0:P], Vr[:, 0, :], PT[:, 0, :], start=True, stop=True)
                mm(WA[:, P:T], Vr[:, 0, :], PT[:, 1, :], start=True, stop=False)
                mm(WA[:, P:T], Vr[:, 1, :], PT[:, 2, :], start=False, stop=True).then_inc(s("attn_in_psum"), 1)
                vec_fold("heads", i, 1, 33 + 3 * i)
                vec_fold("heads", i, 2, 34 + 3 * i)
            for b in range(4):
                uses[b] += HEADS
            meet(pe, met)
            norm_sums("merged", 2)
            split_done("merged")
            with pe.Fori(0, 2) as i:
                for g in range(8):
                    gemm("w_out", i, g, banks[g % 4][:, 0:T], g % 4, uses[g % 4] + 2 * i + g // 4)
                    if g % 2 == 1 and g > 1:
                        for k in range(3):
                            n = 3 * (g // 2 - 1) + k
                            vec_fold("w_out", i, n, 56 + 12 * i + n)
                for n in range(9, 12):
                    vec_fold("w_out", i, n, 56 + 12 * i + n)
            for b in range(4):
                uses[b] += 4
            meet(pe, met)
            norm_sums("ffn")
            split_done("ffn")
            pe.wait_ge(s("k_loaded"), 16)
            with pe.Fori(0, 4) as i:
                for h in range(2):
                    n = 2 * i + h
                    gemm("topk", i, 2 * h, banks[0][:, 0:T], 0, uses[0] + n)
                    gemm("topk", i, 2 * h + 1, banks[1][:, 0:T], 1, uses[1] + n)
                    vec_on_tensor("topk", i, 4 * h + 2, 0, 80 + 4 * i + 2 * h)
                    pe.wait_ge(s("peerq_ready"), n + 1)
                    pe.wait_ge(s("s_ready"), n + 1)
                    for tt in range(2):
                        for half in range(2):
                            q = 2 * tt + half
                            last = mm(WA[:, P * q:P * q + P], Qp[:, half, P * tt:P * tt + P], k12[:, half, n, :],
                                      start=True, stop=True)
                    last.then_inc(s("s_in_psum"), 1)
                    vec_on_tensor("topk", i, 4 * h + 3, 0, 81 + 4 * i + 2 * h)
            uses[0] += HEADS
            uses[1] += HEADS
            pe.drain().then_inc(s("mod_ready"), 1)
            pe.wait_ge(s("picked_ready"), 1)
            for w in range(3):
                for tt in range(2):
                    last = nc.tensor.transpose((WA, WB, WC)[w][:, P * tt:P * tt + P],
                                               picked[:, w, tt].rearrange("p h k -> p (h k)"), ident[:])
            last.then_inc(s("cols_in_psum"), 1)
            meet(pe, met)

            pe.sem_inc(s("hot_used"), 2)

            def spread_unit(unit, bank):
                pe.wait_ge(s("wd_copied"), unit + 1)
                for h in range(2):
                    pe.wait_ge(s("hot_ready"), 2 * unit + h + 1)
                    for j in range(8):
                        o = QW * (8 * h + j)
                        for k in range(3):
                            last = mm(bank[:, o:o + QW], hotA[:, h, j, :], hotB[:, h, j, k, :],
                                      start=(k == 0), stop=(k == 2))
                    last.then_inc(s("hot_used"), 1)

            with pe.Fori(0, 4) as i:
                for u in range(4):
                    spread_unit(4 * i + u, (WB, WC)[u % 2])
            with pe.Fori(0, 16) as g:
                def fold(n):
                    vec_fold("peer", g, n, 96 + 8 * g + n)
                for n in range(8):
                    gemm("peer", g, n, banks[n % 4][:, 0:T], n % 4, uses[n % 4] + 4 * g + n // 4)
                    if n == 3:
                        spread_unit(4 * g + 16, WB)
                    if n == 4:
                        fold(0)
                    if n == 6:
                        fold(1)
                    if n == 7:
                        spread_unit(4 * g + 17, WC)
                for n in range(8):
                    gemm_v(g, n, n % 4, uses[n % 4] + 4 * g + 2 + n // 4)
                    if n == 0:
                        fold(2)
                    if n in (2, 4, 6):
                        fold(2 + n // 2)
                    if n == 3:
                        spread_unit(4 * g + 18, WB)
                    if n == 6:
                        spread_unit(4 * g + 19, WC)
                fold(6)
                fold(7)
            for b in range(4):
                uses[b] += 64
            meet(pe, met)
            norm_sums("final")
            norm_sums("l0")
            split_done("l0")
            meet(pe, met)
            pe.sem_inc(s("bu_read"), 2)
            with pe.Fori(0, 8) as i:
                for t in range(2):
                    tile = 2 * i + t
                    gemm("ssm", i, 2 * t, banks[2 * t][:, 0:T], 2 * t, uses[2 * t] + i)

                    def b_times_u(j):
                        pe.wait_ge(s("bu_read"), 4 * tile + j + 1)
                        for ri in range(2):
                            last = mm((WA, WB)[j % 2][:, T * ri:T * ri + T],
                                      Bst[32 * j:32 * j + 32, t, ri].rearrange("p a b -> p (a b)"),
                                      Us[32 * j:32 * j + 32, t, :], start=True, stop=True, tile_position=(32 * j, 0))
                        last.then_inc(s("bu_in_psum"), 1)

                    def c_times_x(j):
                        pe.wait_ge(s("q_ready"), 4 + 4 * tile + j + 1)
                        for ri in range(2):
                            last = mm(WC[32 * j:32 * j + 32, 0:T], Cst[:, t, ri, j].rearrange("p a b -> p (a b)"),
                                      X[:, j % 2, ri, :], start=(ri == 0), stop=(ri == 1), tile_position=(0, 32 * j))
                        last.then_inc(s("y_pair"), 1)

                    pe.wait_ge(s("u_ready"), tile + 1)
                    pe.wait_ge(s("masks_built"), tile + 1)
                    b_times_u(0)
                    b_times_u(1)
                    gemm("ssm", i, 2 * t + 1, banks[2 * t + 1][:, 0:T], 2 * t + 1, uses[2 * t + 1] + i)
                    pe.wait_ge(s("y_read"), tile + 2)
                    c_times_x(0)
                    b_times_u(2)
                    c_times_x(1)
                    b_times_u(3)
                    c_times_x(2)
                    c_times_x(3)
            for b in range(4):
                uses[b] += 8
            split_done("y")
            plain("glu")
            split_done("glu")
            plain("ssm_out")
            meet(pe, met)
            norm_sums("l1")
            split_done("kv")
            plain("kv")
            pe.wait_ge(s("kv_ready"), 6 * KV)
            for g in range(KV):
                if g >= 2:
                    pe.wait_ge(s("vr_ready"), g - 1)
                for b in range(2):
                    for kt in range(2):
                        o = P * (2 * b + kt)
                        last = nc.tensor.transpose((WA, WB)[g % 2][:, o:o + P],
                                                   KVT[:, (3 + 2 * b) * KV + g, P * kt:P * kt + P], ident[:])
                last.then_inc(s("vr_in_psum"), 1)
            nb = KV * NCMP
            for b in range(2):
                pe.wait_ge(s("w1_loaded"), (48, 64)[b])
                for l in range(CMP_L):
                    mm(WC[:, 64 * b:64 * b + nb], W1[:, l, :],
                       KVT[:, b * KV:(b + 1) * KV, l:l + 16 * (NCMP - 1) + 1:16],
                       start=(l == 0), stop=(l == CMP_L - 1))
                for l in range(CMP_L):
                    last = mm(WC[:, 128 + b:129 + b], W1[:, l, :], V("cmp_pe")[:, CMP_L * b + l:CMP_L * b + l + 1],
                              start=(l == 0), stop=(l == CMP_L - 1))
                last.then_inc(s("w1b_used"), 1)
            for b in range(2):
                pe.wait_ge(s("cmp_gelu"), b + 1)
                mm(WC[:, 192 + 64 * b:192 + 64 * b + nb], W2[:, b, :], GC, start=True, stop=True)\
                    .then_inc(s("cmp2_in_psum"), 1)
                pe.wait_ge(s("kc_ready"), b + 1)
            pe.wait_ge(s("vr_ready"), KV)
            for g in range(KV):
                last = nc.tensor.transpose(WA[0:NCMP, P * g:P * g + P], VCt[:, g, :], ident[:])
            last.then_inc(s("vc_in_psum"), 1)
            split_done("l1")
            for tt in range(2):
                for k in range(KT):
                    last = mm(WB[:, 64 * tt:64 * tt + 48], SQ[:, k, P * tt:P * tt + P], wg[:, k, :],
                              start=(k == 0), stop=(k == KT - 1))
            last.then_inc(s("gt_in_psum"), 1)
            meet(pe, met)
            with pe.Fori(0, KV) as g:
                for hh in range(HPG):
                    gemm("nsa", g, hh, banks[hh][:, 0:T], hh, uses[hh] + 4 * g)
                for hh in range(HPG):
                    n = 4 * g + hh

                    def z_chunk(br):
                        c = 4 + 3 * hh + br
                        gemm("nsa", g, c, banks[c % 4][:, 0:T], c % 4, uses[c % 4] + 4 * g + c // 4)

                    pe.wait_ge(s("q_ready2"), n + 1)
                    pe.wait_ge(s("combined"), n + 1)
                    for br in range(2):
                        for qt in range(2):
                            nk = P * (qt + 1)
                            out = (WA, WB)[br][:, P * qt:P * qt + nk]
                            mm(out, Qg[:, hh, P * qt:P * qt + P], KVT[:, (2 + 2 * br) * KV + g, 0:nk],
                               start=True, stop=False)
                            last = mm(out[:, P * qt:P * qt + P], ident16[:], causal16[:], start=False, stop=True)
                    for qt in range(2):
                        out = WC[:, 16 * qt:16 * qt + NCMP]
                        mm(out, Qg[:, hh, P * qt:P * qt + P], KC[:, g, :], start=True, stop=False)
                        last = mm(out, ident[:], cmp_neg[:, qt, :], start=False, stop=True)
                    last.then_inc(s("sn_in_psum"), 1)
                    z_chunk(0)
                    pe.wait_ge(s("probs2"), n + 1)
                    for br in range(2):
                        for b in range(3):
                            nc.tensor.transpose((WA, WB)[br][:, P * b:P * b + P], Pn[:, br, b, :], ident[:])
                    for qt in range(2):
                        last = nc.tensor.transpose(WC[0:NCMP, P * qt:P * qt + P], Pc[:, qt, :], ident[:])
                    last.then_inc(s("ptn_in_psum"), 1)
                    z_chunk(1)
                    pe.wait_ge(s("ptn_ready"), n + 1)
                    pe.wait_ge(s("vg_ready"), g + 1)
                    for br in range(2):
                        w = (WA, WB)[br]
                        mm(w[:, 0:P], Vg[:, br, 0, :], PTn[:, br, 0, :], start=True, stop=True)
                        mm(w[:, P:T], Vg[:, br, 0, :], PTn[:, br, 1, :], start=True, stop=False)
                        mm(w[:, P:T], Vg[:, br, 1, :], PTn[:, br, 2, :], start=False, stop=True)
                    for qt in range(2):
                        last = mm(WC[:, P * qt:P * qt + P], VCg[0:NCMP, :], PTc[0:NCMP, qt, :], start=True, stop=True)
                    last.then_inc(s("on_in_psum"), 1)
                    z_chunk(2)
            for b in range(4):
                uses[b] += 16
            meet(pe, met)
            split_done("o")
            plain("w_o")
            meet(pe, met)
            norm_sums("final2")

        @block.scalar
        def _(act):
            A = nc.scalar.activation
            met = [0]

            def high(stage, i, g, pos, by_column=False):
                loaded(act, stage, i, pos)
                for half in range(2):
                    n = half_of(stage, i, g, half)
                    act.wait_ge(half_done, n + 1)
                    A(whi[:, half], half_chunk(pos, half, by_column), ACT.Copy).then_inc(s("hi_ready"), 1)

            def norm_squares(name, src):
                n = NORMS[name]
                act.wait_ge(s("norm_src"), n + 1)
                for j in range(4):
                    A(SQ[:, 4 * j:4 * j + 4, :], src[:, 4 * j:4 * j + 4, :], ACT.Square).then_inc(s("squares_ready"), 1)

            def norm_sqrt(name):
                n = NORMS[name]
                act.wait_ge(s("var_ready"), n + 1)
                A(sd[:], var[:], ACT.Sqrt).then_inc(s("sd_ready"), 1)

            def norm_bias(call, bias):
                for k in range(KT):
                    act.wait_ge(s("scaled_ready"), KT * call + k + 1)
                    A(SQ[:, k, :], SQ[:, k, :], ACT.Identity, bias=bias[:, k:k + 1]).then_inc(s("biased"), 1)

            for name in GRANTED["act"]:
                act.sem_inc(s(name), 1)
            for b in range(4):
                act.sem_inc(bank_free[b], 1)
            for name, dst in (("vec", vec[:]), ("w_f", w_f), ("b_f", b_f[:])):
                act.dma_start(dst, a[name]).then_inc(params, 16)
            for k in range(2):
                act.dma_start(pst[64 * k:64 * k + 64], a["step_pair"][k:k + 1, :].broadcast_to([64, PAIRS]))\
                    .then_inc(s("ssm_loaded"), 16)
            for k in range(8):
                act.dma_start(bl[16 * k:16 * k + 16], a["lam_tile"][k:k + 1].broadcast_to([16, 2, KT, 64]))\
                    .then_inc(s("ssm_loaded"), 16)
                act.dma_start(bst_[16 * k:16 * k + 16], a["step_tile"][k:k + 1, :].broadcast_to([16, KT]))\
                    .then_inc(s("ssm_loaded"), 16)
            act.dma_start(br_, a["ssm_b"]).then_inc(s("ssm_loaded"), 16)
            act.wait_ge(params, 48)
            A(cond[:, 0, :], V("c"), ACT.Silu)
            A(cond[:, 1, :], V("c2"), ACT.Silu).then_inc(s("cond_ready"), 1)
            act.wait_ge(x_loaded, 16)
            act.wait_ge(s("consts_ready"), 1)
            act.sem_inc(s("norm_src"), 1)
            norm_squares("mix", x)
            act.wait_ge(s("ssm_loaded"), 19 * 16)
            A(pst, pst, ACT.Exp)
            A(bst_, bst_, ACT.Exp)
            act.drain().then_inc(s("disc_a"), 1)
            norm_sqrt("mix")
            act.wait_ge(s("disc_b"), 1)
            A(e[0], e[0], ACT.Exp)
            A(mag, pe_[0], ACT.Exp)
            A(e[3], e[1], ACT.Sin, scale=TWO_PI)
            A(e[2], e[1], ACT.Abs)
            act.drain()
            A(e[2], e[2], ACT.Sin, scale=-TWO_PI, bias=cst[:, 1:2])
            act.drain().then_inc(s("disc_c"), 1)
            act.wait_ge(s("disc_done"), 1)
            act.dma_start(a["disc"], disc).then_inc(s("disc_saved"), 16)
            act.wait_ge(s("disc_saved"), 16)
            meet(act, met)
            A(lam_t[:, 0, :], V("lru_lambda"), ACT.Abs)
            act.drain()
            A(lam_t[:, 1, :], lam_t[:, 0, :], ACT.Exp, scale=-1.0)
            act.drain()
            A(lam_t[:, 2, :], lam_t[:, 1, :], ACT.Ln, bias=ones[:, 0:1]).then_inc(s("lam_ready"), 1)
            norm_bias(0, mod[:, 0:16])
            act.wait_ge(s("f_ready"), 1)
            A(fl[:, 1, :], fl[:, 0, :], ACT.Abs)
            act.drain()
            A(fl[:, 2, :], fl[:, 1, :], ACT.Exp, scale=-1.0)
            act.drain()
            A(fl[:, 3, :], fl[:, 2, :], ACT.Ln, bias=ones[0:8, 0:1]).then_inc(s("log1p_ready"), 1)
            with act.Fori(0, HEADS) as i:
                for g in range(3):
                    high("heads", i, g, g)
                product(act, "heads", i, 1)
                A(Qh, banks[0][:, 0:T], ACT.Copy, scale=SCALE)
                A(Kh, banks[0][:, T:2 * T], ACT.Copy).then_inc(bank_free[0], 1)
                act.drain().then_inc(s("qk_ready"), 1)
                high("heads", i, 3, 3)
                product(act, "heads", i, 2)
                A(VTh, banks[1][:, 0:T], ACT.Copy).then_inc(bank_free[1], 1)
                act.drain().then_inc(s("vt_ready"), 1)
                high("heads", i, 4, 4)
                act.wait_ge(s("negmax_ready"), i + 1)
                A(Pr[:, 0, :], WA[:, 0:P], ACT.Exp, bias=rowmax[:, 0:1], accum_out=rowsum[:, 0:1])
                A(Pr[:, 1:3, :].rearrange("p a b -> p (a b)"), WA[:, P:3 * P], ACT.Exp, bias=rowmax[:, 1:2],
                  accum_out=rowsum[:, 1:2])
                act.drain().then_inc(s("exps_ready"), 1)
                act.wait_ge(s("vrows_in_psum"), i + 1)
                A(Vr.rearrange("p a b -> p (a b)"), WB[:, 0:T], ACT.Copy).then_inc(s("vrows_ready"), 1)
                act.wait_ge(s("gates_in_psum"), i + 2)
                A(rg, WC[:, 0:T], ACT.Sigmoid, bias=V("lru_b_a")[:, bass.ds(i, 1)])
                A(ig, WC[:, T:2 * T], ACT.Sigmoid, bias=V("lru_b_x")[:, bass.ds(i, 1)])
                act.drain()
                A(ut, rg, ACT.Tanh, scale=sp8[:, 0, bass.ds(i, 1)])
                A(at_, rg, ACT.Exp, scale=sp8[:, 1, bass.ds(i, 1)])
                act.drain().then_inc(s("lru_u_ready"), 1)
                act.wait_ge(s("pt_in_psum"), i + 1)
                A(PT.rearrange("p a b -> p (a b)"), WB[:, 0:3 * P], ACT.Copy).then_inc(s("pt_ready"), 1)
                act.wait_ge(s("lru_t_ready"), i + 1)
                A(t2, t1, ACT.Sqrt, scale=2.0).then_inc(s("lru_sq_ready"), 1)
                product(act, "heads", i, 4)
                act.wait_ge(s("lru_done"), i + 1)
                A(LY, banks[3][:, 0:T], ACT.Gelu_apprx_tanh).then_inc(bank_free[3], 1)
                act.drain().then_inc(s("ly_ready"), 1)
                act.wait_ge(s("attn_in_psum"), i + 1)
                A(M[:, bass.ds(i, 1), :], WA[:, 0:T], ACT.Copy).then_inc(s("attn_ready"), 1)
            meet(act, met)
            act.sem_inc(s("norm_src"), 1)
            norm_squares("merged", M)
            norm_sqrt("merged")
            with act.Fori(0, 2) as i:
                for g in range(8):
                    high("w_out", i, g, 5 * (g // 2) + 2 * (g % 2))
            meet(act, met)
            act.sem_inc(s("norm_src"), 1)
            act.dma_start(k12, a["k12"]).then_inc(s("k_loaded"), 16)
            norm_squares("ffn", x)
            norm_sqrt("ffn")
            norm_bias(1, mod[:, 48:64])
            with act.Fori(0, 4) as i:
                for h in range(2):
                    n = 2 * i + h
                    for half in range(2):
                        high("topk", i, 2 * h + half, 4 * h + half)
                    act.wait_ge(s("s_in_psum"), n + 1)
                    for half in range(2):
                        product(act, "topk", i, 2 * h + half)
                        A(Qp[:, half, :], banks[half][:, 0:T], ACT.Copy).then_inc(bank_free[half], 1)
                    act.drain().then_inc(s("peerq_ready"), 1)
            act.wait_ge(s("vs_ready"), 1)
            A(picked[:, 2], picked[:, 2], ACT.Exp).then_inc(s("vs_exp"), 1)
            act.wait_ge(s("cols_in_psum"), 1)
            for w in range(3):
                A(cols[:, w, :], (WA, WB, WC)[w][:, 0:T], ACT.Copy)
            meet(act, met)
            act.sem_inc(s("wd_copied"), 2)

            def copy_unit(unit, bank, buf, tok):
                act.wait_ge(s("hot_used"), 2 * unit + 4)
                A(Wd[:, buf, :, bass.ds(tok, 16)],
                  bank[:].rearrange("p (t i) -> p i t", i=QW), ACT.Copy).then_inc(s("wd_copied"), 1)

            with act.Fori(0, 4) as i:
                for u in range(4):
                    copy_unit(4 * i + u, (WB, WC)[u % 2], 0, 64 * i + 16 * u)
            with act.Fori(0, 2) as o:
                for par in range(2):
                    act.wait_ge(s("g_ready"), 64 * o + 32 * par + 1)
                    with act.Fori(0, 4) as q:
                        g = 8 * o + 4 * par + q

                        def hidden(n):
                            product(act, "peer", g, n)
                            act.wait_ge(s("gelu_free"), 8 * g + n + 1)
                            A(GL[:, n % 2, :], banks[n % 4][:, 0:T], ACT.Gelu_apprx_tanh).then_inc(bank_free[n % 4], 1)
                            act.drain().then_inc(s("gelu_ready"), 1)

                        for n in range(8):
                            high("peer", g, n, 3 * (n // 2) + n % 2)
                            if n > 0:
                                hidden(n - 1)
                            if n == 5:
                                copy_unit(4 * g + 16, WB, 1 - par, 64 * q)
                        for n in range(8):
                            high("peer", g, 8 + n, 12 + 3 * (n // 2) + n % 2, True)
                            if n == 0:
                                hidden(7)
                            if n == 1:
                                copy_unit(4 * g + 17, WC, 1 - par, 64 * q + 16)
                            if n == 5:
                                copy_unit(4 * g + 18, WB, 1 - par, 64 * q + 32)
                        copy_unit(4 * g + 19, WC, 1 - par, 64 * q + 48)
            meet(act, met)
            act.dma_start(disc, a["disc"]).then_inc(s("disc_loaded"), 16)
            act.dma_start(CC, a["ssm_c"]).then_inc(s("disc_loaded"), 16)
            act.sem_inc(s("norm_src"), 1)
            norm_squares("final", x)
            norm_sqrt("final")
            norm_squares("l0", x)
            norm_sqrt("l0")
            norm_bias(2, mod[:, 96:112])
            act.wait_ge(s("disc_loaded"), 32)
            meet(act, met)

            def table(duo, col, n, free):
                for k in range(2):
                    A(ph[:, k, :], iota_t[:], ACT.Copy, scale=theta[:, bass.ds(col + k, 1)])
                act.drain()
                A(rn[:], ph[:], ACT.Copy, bias=MAGIC)
                act.drain()
                A(rn[:], rn[:], ACT.Copy, bias=-MAGIC).then_inc(s("phase_ready"), 1)
                act.wait_ge(s("frac_ready"), n + 1)
                if free is not None:
                    act.wait_ge(s("q_ready"), free)
                A(tab[:, duo, 1], ph[:], ACT.Sin, scale=TWO_PI)
                A(rn[:], ph[:], ACT.Abs)
                act.drain()
                A(tab[:, duo, 0], rn[:], ACT.Sin, scale=-TWO_PI, bias=cst[:, 1:2])
                act.drain().then_inc(s("table_ready"), 1)

            for duo in range(2):
                table(duo, 2 * duo, duo, None)
            with act.Fori(0, 8) as i:
                for t in range(2):
                    tile = 2 * i + t
                    high("ssm", i, 2 * t, 2 * t)
                    high("ssm", i, 2 * t + 1, 2 * t + 1)
                    product(act, "ssm", i, 2 * t)
                    act.wait_ge(s("y_read"), tile + 1)
                    A(Us[:, t, :], banks[2 * t][:, 0:T], ACT.Copy).then_inc(bank_free[2 * t], 1)
                    act.drain().then_inc(s("u_ready"), 1)
                    product(act, "ssm", i, 2 * t + 1)
                    A(SZ[:, bass.ds(tile, 1), :], banks[2 * t + 1][:, 0:T], ACT.Silu).then_inc(bank_free[2 * t + 1], 1)
                    for duo in range(2):
                        table(duo, 4 * tile + 4 + 2 * duo, 2 * tile + 2 + duo, 4 + 4 * tile + 2 * duo + 2)
            act.wait_ge(s("y_read"), KT + 2)
            for j in range(4):
                A(Y[:, 4 * j:4 * j + 4, :], Y[:, 4 * j:4 * j + 4, :], ACT.Gelu_apprx_tanh).then_inc(s("y_gelu"), 1)
            with act.Fori(0, 2) as i:
                for g in range(9):
                    if g < 8:
                        high("glu", i, g, g)
                    if g > 0:
                        m = 8 * i + g - 1
                        product(act, "glu", i, g - 1)
                        act.wait_ge(s("glu_free"), m + 1)
                        A(glt[:, (g - 1) % 2, :], banks[(g - 1) % 4][:, 0:T], ACT.Sigmoid,
                          bias=V("b_glu")[:, bass.ds(m, 1)]).then_inc(bank_free[(g - 1) % 4], 1)
                        act.drain().then_inc(s("sig_ready"), 1)
            with act.Fori(0, 2) as i:
                for g in range(8):
                    high("ssm_out", i, g, g)
            meet(act, met)
            for dst, name in ((W1, "cmp_w1"), (W2, "cmp_w2"), (wg, "w_gate")):
                act.dma_start(dst, a[name][:, 0] if name == "cmp_w1" else a[name]).then_inc(s("w1_loaded"), 16)
            act.sem_inc(s("norm_src"), 1)
            norm_squares("l1", x)
            norm_sqrt("l1")
            norm_bias(3, mod[:, 192:208])
            with act.Fori(0, 3) as i:
                for g in range(9):
                    if g < 8:
                        high("kv", i, g, g)
                    if g > 0:
                        product(act, "kv", i, g - 1)
                        A(KVT[:, bass.ds(8 * i + g - 1, 1), :], banks[(g - 1) % 4][:, 0:T], ACT.Copy)\
                            .then_inc(bank_free[(g - 1) % 4], 1)
                        act.drain().then_inc(s("kv_ready"), 1)
            for g in range(KV):
                act.wait_ge(s("vr_in_psum"), g + 1)
                A(VR[:, g].rearrange("p a b c -> p (a b c)"), (WA, WB)[g % 2][:], ACT.Copy).then_inc(s("vr_ready"), 1)
            act.wait_ge(s("w1b_used"), 1)
            act.dma_start(W1, a["cmp_w1"][:, 1]).then_inc(s("w1_loaded"), 16)
            for b in range(2):
                act.wait_ge(s("b1e_ready"), 1)
                A(GC, WC[:, 64 * b:64 * b + KV * NCMP], ACT.Gelu_apprx_tanh, bias=b1e[:, b:b + 1])\
                    .then_inc(s("cmp_gelu"), 1)
                act.wait_ge(s("cmp2_in_psum"), b + 1)
                A((KC, VCt)[b].rearrange("p a b -> p (a b)"), WC[:, 192 + 64 * b:192 + 64 * b + KV * NCMP],
                  ACT.Identity, bias=V("cmp_b2")[:, b:b + 1])
                act.drain().then_inc(s("kc_ready"), 1)
            act.wait_ge(s("vc_in_psum"), 1)
            A(VCr[0:NCMP].rearrange("p a b -> p (a b)"), WA[0:NCMP, :], ACT.Copy)
            norm_bias(4, mod[:, 144:160])
            act.wait_ge(s("gt_in_psum"), 1)
            A(GT, WB[:, 0:128].rearrange("p (a b) -> p a b", a=2)[:, :, 0:48], ACT.Sigmoid)
            meet(act, met)
            with act.Fori(0, KV) as g:
                def q_out(hh):
                    product(act, "nsa", g, hh)
                    A(Qg[:, hh, :], banks[hh][:, 0:T], ACT.Copy, scale=SCALE).then_inc(bank_free[hh], 1)
                    act.drain().then_inc(s("q_ready2"), 1)

                def z_silu(hh, br):
                    c = 4 + 3 * hh + br
                    product(act, "nsa", g, c)
                    A(SZn[:, hh % 2, br, :], banks[c % 4][:, 0:T], ACT.Silu).then_inc(bank_free[c % 4], 1)
                    act.drain().then_inc(s("sz_ready"), 1)

                high("nsa", g, 0, 0)
                for hh in range(1, HPG):
                    high("nsa", g, hh, hh)
                    q_out(hh - 1)
                high("nsa", g, 4, 4)
                q_out(HPG - 1)
                for hh in range(HPG):
                    n = 4 * g + hh
                    act.wait_ge(s("negmax2"), n + 1)
                    for br in range(2):
                        w = (WA, WB)[br]
                        A(Pn[:, br, 0, :], w[:, 0:P], ACT.Exp, bias=mx[:, 2 * br:2 * br + 1],
                          accum_out=sm[:, 2 * br:2 * br + 1])
                        A(Pn[:, br, 1:3, :].rearrange("p a b -> p (a b)"), w[:, P:3 * P], ACT.Exp,
                          bias=mx[:, 2 * br + 1:2 * br + 2], accum_out=sm[:, 2 * br + 1:2 * br + 2])
                    for qt in range(2):
                        A(Pc[:, qt, :], WC[:, 16 * qt:16 * qt + NCMP], ACT.Exp, bias=mx[:, 4 + qt:5 + qt],
                          accum_out=sm[:, 4 + qt:5 + qt])
                    act.drain().then_inc(s("exps2"), 1)
                    high("nsa", g, 5 + 3 * hh, 5 + 3 * hh)
                    z_silu(hh, 0)
                    act.wait_ge(s("ptn_in_psum"), n + 1)
                    for br in range(2):
                        A(PTn[:, br].rearrange("p a b -> p (a b)"), (WA, WB)[br][:, 0:3 * P], ACT.Copy)
                    A(PTc[0:NCMP].rearrange("p a b -> p (a b)"), WC[0:NCMP, 0:T], ACT.Copy)
                    act.drain().then_inc(s("ptn_ready"), 1)
                    high("nsa", g, 6 + 3 * hh, 6 + 3 * hh)
                    z_silu(hh, 1)
                    if hh < HPG - 1:
                        high("nsa", g, 7 + 3 * hh, 7 + 3 * hh)
                    z_silu(hh, 2)
            meet(act, met)
            with act.Fori(0, 2) as i:
                for g in range(8):
                    high("w_o", i, g, g)
            meet(act, met)
            act.sem_inc(s("norm_src"), 1)
            norm_squares("final2", x)
            norm_sqrt("final2")

        @block.vector
        def _(dve):
            v = nc.vector
            met = [0]

            def low(stage, i, g, pos, by_column=False):
                for half in range(2):
                    n = half_of(stage, i, g, half)
                    dve.wait_ge(s("hi_ready"), n + 1)
                    v.tensor_tensor(wlo[:, half, 0:DVE_K], half_chunk(pos, half, by_column)[:, 0:DVE_K],
                                    whi[:, half, 0:DVE_K].bitcast(F32), ALU.subtract).then_inc(s("lo_dve"), 1)
                dve.drain().then_inc(slot_free[pos % R], 1)

            def vec_times(stage, i, pos, which):
                loaded(dve, stage, i, pos)
                v.tensor_tensor(ring[:, pos % R], ring[:, pos % R],
                                cond[:, which].unsqueeze(2).broadcast_to([P, KT, P]), ALU.mult)
                dve.drain()

            def vec_sum(stage, i, n, pos, pool_n=None):
                v_, back = vec_of(stage, i, n)
                if pool_n is not None:
                    dve.wait_ge(s("prod_ready"), 2 * (POOL_VEC0[stage] + POOL_VECS[stage] * i + pool_n) + 2)
                dve.wait_ge(s("part_used"), v_ - back + 5)
                v.tensor_reduce(part[:, n % 4, :], ring[:, pos % R].rearrange("p k n -> p n k"), AX, ALU.add)\
                    .then_inc(s("part_ready"), 1)
                dve.drain().then_inc(slot_free[pos % R], 2)

            def split(name, src, waits=None):
                for j in range(4):
                    if waits is not None:
                        dve.wait_ge(s(waits[0]), waits[1] + (j + 1) * waits[2])
                    v.tensor_copy(Hhi[:, 4 * j:4 * j + 4, :], src[:, 4 * j:4 * j + 4, :]).then_inc(s("hhi_ready"), 1)
                    if j >= 2:
                        dve.drain()
                        v.tensor_tensor(Hlo[:, 4 * j:4 * j + 4, :], src[:, 4 * j:4 * j + 4, :],
                                        Hhi[:, 4 * j:4 * j + 4, :].bitcast(F32), ALU.subtract)\
                            .then_inc(s("h_ready"), 1)

            def norm_rstd(name, width):
                n = NORMS[name]
                groups = 2 if name == "merged" else 1
                dve.wait_ge(s("sums_ready"), n + 1)
                v.tensor_scalar(var[:, 0:groups], WA[:, 0:groups * T].rearrange("p (a b) -> p a b", b=T),
                                1.0 / width, EPS, ALU.mult, ALU.add)
                if groups == 1:
                    v.tensor_scalar(var[:, 1], WA[:, 0:T], 1.0 / width, EPS, ALU.mult, ALU.add)
                dve.drain().then_inc(s("var_ready"), 1)
                dve.wait_ge(s("sd_ready"), n + 1)
                v.reciprocal(rstd[:], sd[:])
                dve.drain()

            def norm_scale(dst, src, g, signal=None):
                for k in range(KT):
                    ins = v.scalar_tensor_tensor(dst[:, k, :], src[:, k, :], g[:, k:k + 1], rstd[:, k // 8, :],
                                                 ALU.mult, ALU.mult)
                    if signal:
                        ins.then_inc(s(signal), 1)
                dve.drain()

            def modulated_gain(n, g, scale):
                v.tensor_scalar(gain[:, n, :], scale, 1.0, None, ALU.add)
                dve.drain()
                v.tensor_tensor(gain[:, n, :], gain[:, n, :], g, ALU.mult)
                dve.drain()

            def take_mod(lo, hi):
                v.tensor_tensor(mod[:, lo:hi], ps_mod[:, lo:hi],
                                vec[:, VOFF["b_ada"] + lo:VOFF["b_ada"] + hi], ALU.add)
                dve.drain()

            def residual(stage, i, g, gate):
                product(dve, stage, i, g)
                m = 8 * i + g
                v.scalar_tensor_tensor(x[:, bass.ds(m, 1), :], banks[g % 4][:, 0:T], gate[:, bass.ds(m, 1)],
                                       x[:, bass.ds(m, 1), :], ALU.mult, ALU.add).then_inc(bank_free[g % 4], 1)

            def plain_residual(stage, gate):
                with dve.Fori(0, 2) as i:
                    for g in range(9):
                        if g < 8:
                            low(stage, i, g, g)
                        if g > 0:
                            residual(stage, i, g - 1, gate)

            for name in GRANTED["dve"]:
                dve.sem_inc(s(name), 1)
            v.memset(cst[:, 0:1], -MAGIC)
            v.memset(cst[:, 1:2], HALF_PI)
            norm_rstd("mix", D)
            dve.wait_ge(s("disc_e"), 1)
            v.reciprocal(e[4], e[4]).then_inc(s("disc_f"), 1)
            with dve.Fori(0, 8) as i:
                for n in range(2):
                    vec_times("shift_scale", i, 2 * n + 1, 0)
                    vec_sum("shift_scale", i, n, 2 * n + 1)
            dve.wait_ge(s("mod_ready"), 1)
            take_mod(0, 32)
            modulated_gain(0, V("g_mix"), mod[:, 16:32])
            meet(dve, met)
            norm_scale(SQ, x, gain[:, 0, :], "scaled_ready")
            split("mix", SQ, ("biased", 0, 4))
            v.memset(LX[:, 0:3], 0.0)
            v.tensor_scalar(sp8[:, 0, :], V("lru_lambda"), -1.0, 0.0, ALU.mult, ALU.max)
            dve.wait_ge(s("lam_ready"), 1)
            dve.drain()
            v.tensor_tensor(sp8[:, 0, :], sp8[:, 0, :], lam_t[:, 2, :], ALU.add)
            dve.drain()
            v.tensor_scalar(sp8[:, 0, :], sp8[:, 0, :], LRU_C, None, ALU.mult)
            dve.drain()
            v.tensor_scalar(sp8[:, 1, :], sp8[:, 0, :], -1.0, None, ALU.mult)
            dve.wait_ge(s("f_in_psum"), 1)
            v.tensor_scalar(fl[:, 0, :], WB[0:8, 0:T], b_f[:, 0:1], None, ALU.add).then_inc(s("f_ready"), 1)
            dve.drain()
            v.tensor_scalar(fl[:, 4, :], fl[:, 0, :], 0.0, None, ALU.min)
            dve.wait_ge(s("log1p_ready"), 1)
            dve.drain()
            v.tensor_tensor(fl[:, 4, :], fl[:, 4, :], fl[:, 3, :], ALU.subtract)
            dve.drain()
            v.tensor_tensor_scan(fl[:, 5, :], ones[0:8, :], fl[:, 4, :], 0.0, ALU.mult, ALU.add)
            dve.drain().then_inc(s("cum_ready"), 1)
            conv_w = V("conv_w").rearrange("p (a b) -> p a b", b=4)
            with dve.Fori(0, HEADS) as i:
                v.tensor_scalar(cm[:, 0, :], fl[:, 5, :], ident[0:8, bass.ds(i, 1)], None, ALU.mult)
                dve.drain()
                v.tensor_scalar(cm[:, 1, :], cm[:, 0, :], -1.0, None, ALU.mult).then_inc(s("cm_ready"), 1)
                for g in range(5):
                    low("heads", i, g, g)
                product(dve, "heads", i, 3)
                v.tensor_copy(LX[:, 3:3 + T], banks[2][:, 0:T]).then_inc(bank_free[2], 1)
                dve.drain()
                v.tensor_scalar(xc, LX[:, 0:T], conv_w[:, bass.ds(i, 1), 0], V("conv_b")[:, bass.ds(i, 1)],
                                ALU.mult, ALU.add)
                for w in range(1, 4):
                    dve.drain()
                    v.scalar_tensor_tensor(xc, LX[:, w:w + T], conv_w[:, bass.ds(i, 1), w], xc, ALU.mult, ALU.add)
                dve.drain().then_inc(s("xc_ready"), 1)
                dve.wait_ge(s("scores_ready"), i + 1)
                v.tensor_reduce(rowmax[:, 0:1], WA[:, 0:P], AX, ALU.max)
                v.tensor_reduce(rowmax[:, 1:2], WA[:, P:3 * P], AX, ALU.max)
                dve.drain()
                v.tensor_scalar(rowmax, rowmax, -1.0, None, ALU.mult).then_inc(s("negmax_ready"), 1)
                dve.wait_ge(s("exps_ready"), i + 1)
                v.reciprocal(rowrec, rowsum)
                dve.drain()
                v.tensor_scalar(Pr[:, 0, :], Pr[:, 0, :], rowrec[:, 0:1], None, ALU.mult)
                v.tensor_scalar(Pr[:, 1:3, :], Pr[:, 1:3, :], rowrec[:, 1:2], None, ALU.mult)
                dve.drain().then_inc(s("probs_ready"), 1)
                vec_times("heads", i, 7, 0)
                vec_sum("heads", i, 0, 5, 0)
                dve.wait_ge(s("lru_u_ready"), i + 2)
                v.tensor_tensor(gx, ig, xc, ALU.mult)
                v.tensor_scalar(t1, ut, 1.0, None, ALU.add)
                dve.drain()
                v.reciprocal(t1, t1)
                dve.drain()
                v.tensor_tensor(t1, t1, ut, ALU.mult).then_inc(s("lru_t_ready"), 1)
                vec_sum("heads", i, 1, 6, 1)
                dve.wait_ge(s("lru_sq_ready"), i + 1)
                v.tensor_tensor(gx, gx, t2, ALU.mult)
                dve.drain()
                v.tensor_tensor_scan(t1, at_, gx, 0.0, ALU.mult, ALU.add)
                vec_sum("heads", i, 2, 7)
                dve.wait_ge(s("ly_ready"), i + 1)
                v.tensor_tensor(M[:, bass.ds(HEADS + i, 1), :], t1, LY, ALU.mult).then_inc(s("lru_done"), 1)
            meet(dve, met)
            take_mod(32, 56)
            norm_rstd("merged", D // 2)
            norm_scale(SQ, M, V("g_merge"))
            split("merged", SQ)
            with dve.Fori(0, 2) as i:
                for g in range(8):
                    m = g // 2
                    low("w_out", i, g, 5 * m + 2 * (g % 2))
                    if g > 0:
                        residual("w_out", i, g - 1, mod[:, 32:48])
                    if g % 2 == 0:
                        vec_sum("w_out", i, 3 * m, 5 * m + 1, 2 * m + m // 2 if False else (0, 3, 5, 7)[m])
                    else:
                        vec_sum("w_out", i, 3 * m + 1, 5 * m + 3, (1, 4, 6, 8)[m])
                        if m > 0:
                            vec_times("w_out", i, 5 * m + 4, 0)
                            vec_sum("w_out", i, 3 * m + 2, 5 * m + 4)
                        else:
                            vec_sum("w_out", i, 3 * m + 2, 5 * m + 4, 2)
                residual("w_out", i, 7, mod[:, 32:48])
            meet(dve, met)
            take_mod(56, 80)
            modulated_gain(1, V("g_ffn"), mod[:, 64:80])
            norm_rstd("ffn", D)
            norm_scale(SQ, x, gain[:, 1, :], "scaled_ready")
            split("ffn", SQ, ("biased", KT, 4))

            def top16(vals, idx, src):
                v.max(vals[:, 0:8], src)
                dve.drain()
                v.max_index(idx[:, 0:8], vals[:, 0:8], src)
                dve.drain()
                v.match_replace(src, vals[:, 0:8], src, LOW)
                dve.drain()
                v.max(vals[:, 8:16], src)
                dve.drain()
                v.max_index(idx[:, 8:16], vals[:, 8:16], src)

            iota_k = iota[:, 0:TOPK].unsqueeze(1).broadcast_to([P, TOPK, TOPK])
            with dve.Fori(0, HEADS) as i:
                dve.wait_ge(s("s_in_psum"), i + 2)
                v.tensor_copy(S4.rearrange("p a b -> p (a b)"), WA[:]).then_inc(s("s_ready"), 1)
                dve.drain()
                for tt in range(2):
                    top16(v1f, i1u, S4[:, 2 * tt, :])
                    top16(v2f, i2u, S4[:, 2 * tt + 1, :])
                    dve.drain()
                    v.tensor_copy(i1f, i1u)
                    v.tensor_copy(i2f, i2u)
                    v.tensor_tensor(cand, v1f.unsqueeze(2).broadcast_to([P, TOPK, TOPK]),
                                    v2f.unsqueeze(1).broadcast_to([P, TOPK, TOPK]), ALU.add)
                    dve.drain()
                    top16(vs, ic, cand.rearrange("p a b -> p (a b)"))
                    dve.drain()
                    v.tensor_scalar(ich, ic, 4, None, ALU.logical_shift_right)
                    v.tensor_scalar(icl, ic, 15, None, ALU.bitwise_and)
                    dve.drain()
                    v.tensor_copy(chf, ich)
                    v.tensor_copy(clf, icl)
                    dve.drain()
                    for cf, hot, idx in ((chf, hot1, i1f), (clf, hot2, i2f)):
                        v.tensor_tensor(hot, cf.unsqueeze(2).broadcast_to([P, TOPK, TOPK]), iota_k, ALU.is_equal)
                    dve.drain()
                    for cf, hot, idx in ((chf, hot1, i1f), (clf, hot2, i2f)):
                        v.tensor_tensor(hot, hot, idx.unsqueeze(1).broadcast_to([P, TOPK, TOPK]), ALU.mult)
                    dve.drain()
                    for w, hot in enumerate((hot1, hot2)):
                        v.tensor_reduce(picked[:, w, tt, bass.ds(i, 1), :].rearrange("p a b -> p (a b)"), hot, AX, ALU.add)
                    v.tensor_copy(picked[:, 2, tt, bass.ds(i, 1), :].rearrange("p a b -> p (a b)"), vs)
                    dve.drain()
            v.tensor_copy(pmax, picked[:, 2, :, :, 0])
            dve.drain()
            for tt in range(2):
                v.tensor_tensor(picked[:, 2, tt], picked[:, 2, tt],
                                pmax[:, tt].unsqueeze(2).broadcast_to([P, HEADS, TOPK]), ALU.subtract)
            dve.drain().then_inc(s("vs_ready"), 1)
            dve.wait_ge(s("vs_exp"), 1)
            v.tensor_reduce(psum_, picked[:, 2], AX, ALU.add)
            dve.drain()
            v.reciprocal(prec, psum_)
            dve.drain()
            for tt in range(2):
                v.tensor_tensor(picked[:, 2, tt], picked[:, 2, tt],
                                prec[:, tt].unsqueeze(2).broadcast_to([P, HEADS, TOPK]), ALU.mult)
            dve.drain().then_inc(s("picked_ready"), 1)
            dve.wait_ge(s("mod_ready"), 2)
            take_mod(80, 96)
            meet(dve, met)
            rest = var[:, 0]
            bf = sd[:].rearrange("p a b -> p (a b)").bitcast(BF16)[:, 0:T]
            v.tensor_copy(rest, cols[:, 2, :])
            for k in range(3):
                dve.drain()
                v.tensor_copy(bf, rest)
                dve.drain()
                v.tensor_copy(cols[:, 2 + k, :], bf)
                dve.drain()
                if k < 2:
                    v.tensor_tensor(rest, rest, cols[:, 2 + k, :], ALU.subtract)
            dve.drain()

            def one_hots(unit, h, tok):
                dve.wait_ge(s("hot_used"), 2 * unit + h + 1)
                for j in range(8):
                    v.tensor_scalar(hotA[:, h, j, :], iota16b[:], cols[:, 0, bass.ds(tok + j, 1)], None, ALU.is_equal)
                v.tensor_tensor(eqB, iota[:, 0:QW].unsqueeze(1).broadcast_to([P, 8, QW]),
                                cols[:, 1, bass.ds(tok, 8)].unsqueeze(2).broadcast_to([P, 8, QW]), ALU.is_equal)
                dve.drain()
                for k in range(3):
                    v.tensor_tensor(hotB[:, h, :, k, :], eqB,
                                    cols[:, 2 + k, bass.ds(tok, 8)].unsqueeze(2).broadcast_to([P, 8, QW]), ALU.mult)
                dve.drain().then_inc(s("hot_ready"), 1)

            eqB = var[:, 0].rearrange("p (b c) -> p b c", c=QW)
            with dve.Fori(0, 4) as i:
                for u in range(4):
                    for h in range(2):
                        one_hots(4 * i + u, h, 64 * i + 16 * u + 8 * h)
            with dve.Fori(0, 2) as o:
                for par in range(2):
                    dve.wait_ge(s("wd_copied"), 2 + 16 + 32 * o + 16 * par)
                    v.tensor_scalar(cols[:, 1, :], cols[:, 1, :], float(QW), None, ALU.subtract)
                    dve.drain()
                    with dve.Fori(0, 4) as q:
                        g = 8 * o + 4 * par + q

                        def weigh(n):
                            b = GL[:, n % 2, :]
                            dve.wait_ge(s("gelu_ready"), 8 * g + n + 1)
                            v.tensor_tensor(b, b, Wd[:, par, bass.ds(8 * q + n, 1), :], ALU.mult)
                            dve.drain()
                            v.tensor_copy(Ghi[:, n, :], b)
                            dve.drain()
                            v.tensor_tensor(Glo[:, n, :], b, Ghi[:, n, :].bitcast(F32), ALU.subtract)\
                                .then_inc(s("g_ready"), 1)
                            dve.drain().then_inc(s("gelu_free"), 1)

                        def sum_vec(n):
                            vec_sum("peer", g, n, 3 * n + 2, n)

                        def result(n):
                            product(dve, "peer", g, 8 + n)
                            for dd in range(2):
                                m = 2 * n + dd
                                last = v.scalar_tensor_tensor(x[:, m, :], banks[n % 4][:, T * dd:T * dd + T],
                                                              mod[:, 80 + m:81 + m], x[:, m, :], ALU.mult, ALU.add)
                            last.then_inc(bank_free[n % 4], 1)

                        for n in range(8):
                            low("peer", g, n, 3 * (n // 2) + n % 2)
                            if n % 2 == 0:
                                one_hots(4 * g + 16 + n // 4, n // 2 % 2, 64 * q + 8 * (n // 2))
                            if n > 1:
                                weigh(n - 2)
                            if n in (3, 5, 7):
                                sum_vec((n - 3) // 2)
                        low("peer", g, 8, 12, True)
                        weigh(6)
                        weigh(7)
                        one_hots(4 * g + 18, 0, 64 * q + 32)
                        for n in range(1, 8):
                            low("peer", g, 8 + n, 12 + 3 * (n // 2) + n % 2, True)
                            result(n - 1)
                            if n in (1, 3, 5, 7):
                                sum_vec(3 + (n - 1) // 2)
                            if n in (2, 4, 5):
                                one_hots(4 * g + 18 + n // 4, (n // 2 % 2) if n < 5 else 1,
                                         64 * q + 8 * {2: 5, 4: 6, 5: 7}[n])
                        result(7)
                        sum_vec(7)
            meet(dve, met)
            take_mod(96, 224)
            norm_rstd("final", D)
            norm_scale(x, x, V("g_final"))
            dve.drain().then_inc(s("norm_src"), 1)
            modulated_gain(2, V("g_l0"), mod[:, 112:128])
            norm_rstd("l0", D)
            norm_scale(SQ, x, gain[:, 2, :], "scaled_ready")
            split("l0", SQ, ("biased", 2 * KT, 4))
            meet(dve, met)
            with dve.Fori(0, 8) as i:
                for t in range(2):
                    tile = 2 * i + t
                    low("ssm", i, 2 * t, 2 * t)
                    low("ssm", i, 2 * t + 1, 2 * t + 1)
                    for j in range(4):
                        duo, k = j // 2, j % 2
                        bu = (WA, WB)[j % 2][:].rearrange("p (a b) -> p a b", a=2)
                        dve.wait_ge(s("table_ready"), 2 * tile + duo + 1)
                        dve.wait_ge(s("bu_in_psum"), 4 * tile + j + 1)
                        v.tensor_tensor(P1, bu, tab[:, duo, 0, k:k + 1, :].broadcast_to([P, 2, T]), ALU.mult)
                        v.tensor_tensor(P2, bu, tab[:, duo, 1, k:k + 1, :].broadcast_to([P, 2, T]), ALU.mult)
                        dve.drain().then_inc(s("bu_read"), 1)
                        v.tensor_tensor(Wr[:, 0, :], P1[:, 0, :], P2[:, 1, :], ALU.add)
                        v.tensor_tensor(Wr[:, 1, :], P1[:, 1, :], P2[:, 0, :], ALU.subtract)
                        dve.drain()
                        dve.wait_ge(s("q_ready"), 4 + 4 * tile + j - 1)
                        m = mag[:, bass.ds(4 * tile + j, 1)].broadcast_to([P, T])
                        for ri in range(2):
                            v.tensor_tensor_scan(Z[:, j % 2, ri, :], m, Wr[:, ri, :], 0.0, ALU.mult, ALU.add)
                        dve.drain().then_inc(s("z_ready"), 1)
                    dve.wait_ge(s("y_pair"), 4 * tile + 9)
                    v.scalar_tensor_tensor(Y[:, bass.ds(tile, 1), :], Us[:, t, :], V("ssm_d")[:, bass.ds(tile, 1)],
                                           WC[:, 0:T], ALU.mult, ALU.add)
                    dve.drain().then_inc(s("y_read"), 1)
            split("y", Y, ("y_gelu", 0, 1))
            dve.sem_inc(s("glu_free"), 2)
            with dve.Fori(0, 2) as i:
                for g in range(9):
                    if g < 8:
                        low("glu", i, g, g)
                    if g > 0:
                        m = 8 * i + g - 1
                        dve.wait_ge(s("sig_ready"), m + 1)
                        v.tensor_tensor(Y[:, bass.ds(m, 1), :], glt[:, (g - 1) % 2, :], Y[:, bass.ds(m, 1), :], ALU.mult)
                        dve.drain().then_inc(s("glu_free"), 1)
                        v.tensor_tensor(SZ[:, bass.ds(m, 1), :], Y[:, bass.ds(m, 1), :], SZ[:, bass.ds(m, 1), :], ALU.mult)
            dve.drain()
            product(dve, "glu", 1, 7)
            split("glu", SZ)
            plain_residual("ssm_out", mod[:, 128:144])
            meet(dve, met)
            modulated_gain(3, V("g_kv"), mod[:, 208:224])
            modulated_gain(4, V("g_l1"), mod[:, 160:176])
            norm_rstd("l1", D)
            norm_scale(SQ, x, gain[:, 3, :], "scaled_ready")
            split("kv", SQ, ("biased", 3 * KT, 4))
            with dve.Fori(0, 3) as i:
                for g in range(8):
                    low("kv", i, g, g)
            dve.wait_ge(s("w1b_used"), 2)
            v.tensor_tensor(b1e, WC[:, 128:130], V("cmp_b1"), ALU.add).then_inc(s("b1e_ready"), 1)
            norm_scale(SQ, x, gain[:, 4, :], "scaled_ready")
            split("l1", SQ, ("biased", 4 * KT, 4))
            meet(dve, met)
            gates = GT.rearrange("p t (b n) -> p t b n", b=3)
            with dve.Fori(0, KV) as g:
                for hh in range(HPG):
                    low("nsa", g, hh, hh)
                low("nsa", g, 4, 4)
                for hh in range(HPG):
                    n = 4 * g + hh
                    dve.wait_ge(s("sn_in_psum"), n + 1)
                    for br in range(2):
                        w = (WA, WB)[br]
                        v.tensor_reduce(mx[:, 2 * br:2 * br + 1], w[:, 0:P], AX, ALU.max)
                        v.tensor_reduce(mx[:, 2 * br + 1:2 * br + 2], w[:, P:3 * P], AX, ALU.max)
                    v.tensor_reduce(mx[:, 4:6], WC[:, 0:32].rearrange("p (a b) -> p a b", a=2)[:, :, 0:NCMP], AX, ALU.max)
                    dve.drain()
                    v.tensor_scalar(mx, mx, -1.0, None, ALU.mult).then_inc(s("negmax2"), 1)
                    dve.wait_ge(s("exps2"), n + 1)
                    v.reciprocal(rc, sm)
                    dve.drain()
                    for k, br in enumerate((1, 2, 0)):
                        v.tensor_tensor(rc[:, 2 * k:2 * k + 2], rc[:, 2 * k:2 * k + 2],
                                        gates[:, :, br, bass.ds(n, 1)].rearrange("p a b -> p (a b)"), ALU.mult)
                    dve.drain()
                    for br in range(2):
                        v.tensor_scalar(Pn[:, br, 0, :], Pn[:, br, 0, :], rc[:, 2 * br:2 * br + 1], None, ALU.mult)
                        v.tensor_scalar(Pn[:, br, 1:3, :], Pn[:, br, 1:3, :], rc[:, 2 * br + 1:2 * br + 2], None, ALU.mult)
                    for qt in range(2):
                        v.scalar_tensor_tensor(Pc[:, qt, :], Pc[:, qt, :], rc[:, 4 + qt:5 + qt], cmp_one[:, qt, :],
                                               ALU.mult, ALU.mult)
                    dve.drain().then_inc(s("probs2"), 1)
                    low("nsa", g, 5 + 3 * hh, 5 + 3 * hh)
                    low("nsa", g, 6 + 3 * hh, 6 + 3 * hh)
                    if hh < HPG - 1:
                        low("nsa", g, 7 + 3 * hh, 7 + 3 * hh)
                    dve.wait_ge(s("sz_ready"), 3 * n + 3)
                    dve.wait_ge(s("on_in_psum"), n + 2)
                    v.tensor_tensor(ot[:, 0, :], WA[:, 0:T], SZn[:, hh % 2, 1, :], ALU.mult)
                    v.tensor_tensor(ot[:, 1, :], WB[:, 0:T], SZn[:, hh % 2, 2, :], ALU.mult)
                    v.tensor_tensor(ot[:, 2, :], WC[:, 0:T], SZn[:, hh % 2, 0, :], ALU.mult)
                    dve.drain()
                    v.tensor_tensor(ot[:, 0, :], ot[:, 0, :], ot[:, 1, :], ALU.add)
                    dve.drain()
                    v.tensor_tensor(O[:, bass.ds(n, 1), :], ot[:, 0, :], ot[:, 2, :], ALU.add)
                    dve.drain().then_inc(s("combined"), 1)
            meet(dve, met)
            split("o", O)
            plain_residual("w_o", mod[:, 176:192])
            meet(dve, met)
            norm_rstd("final2", D)
            norm_scale(SQ, x, V("g_final2"))
            dve.drain().then_inc(s("out_ready"), 1)

        @block.gpsimd
        def _(pool):
            gp = nc.gpsimd
            met = [0]

            def low(stage, i, g, pos, by_column=False, first=DVE_K, between=None):
                for half in range(2):
                    n = half_of(stage, i, g, half)
                    pool.wait_ge(s("hi_ready"), n + 1)
                    gp.tensor_tensor(wlo[:, half, first:8], half_chunk(pos, half, by_column)[:, first:8],
                                     whi[:, half, first:8].bitcast(F32), ALU.subtract).then_inc(s("lo_pool"), 1)
                    if first == 0:
                        pool.drain().then_inc(s("lo_dve"), 1)
                    if half == 1:
                        pool.drain().then_inc(slot_free[pos % R], 2 if first == 0 else 1)
                    if between is not None:
                        between(half)

            def vec_times(stage, i, pos, which, half):
                if half == 0:
                    loaded(pool, stage, i, pos)
                w = ring[:, pos % R, 8 * half:8 * half + 8, :]
                gp.tensor_tensor(w, w, cond[:, which, 8 * half:8 * half + 8].unsqueeze(2).broadcast_to([P, 8, P]),
                                 ALU.mult).then_inc(s("prod_ready"), 1)

            def split(name, src):
                for j in range(2):
                    pool.wait_ge(s("hhi_ready"), 4 * SPLITS[name] + j + 1)
                    gp.tensor_tensor(Hlo[:, 4 * j:4 * j + 4, :], src[:, 4 * j:4 * j + 4, :],
                                     Hhi[:, 4 * j:4 * j + 4, :].bitcast(F32), ALU.subtract).then_inc(s("h_ready"), 1)

            def plain(stage):
                body, n = STAGES[stage][0:2]
                with pool.Fori(0, n) as i:
                    for g in range(body):
                        low(stage, i, g, g)

            gp.memset(ones[:], 1.0)
            gp.iota(itmp, [[1, T]], base=0, channel_multiplier=0)
            pool.drain()
            gp.tensor_copy(iota_t[:], itmp)
            gp.tensor_copy(iota[:], itmp[:, 0:P])
            gp.tensor_copy(iota16b[:], itmp[:, 0:P])

            def select(out, src, base, pattern, cm_, op, fill):
                pool.drain()
                gp.affine_select(out=out, in_=src, compare_op=op, fill=fill, base=base, pattern=pattern,
                                 channel_multiplier=cm_)

            select(ident[:], ones[:, 0:P], 0, [[-1, P]], 1, ALU.is_equal, 0.0)
            gp.memset(causal16[:], 0.0)
            select(causal16[:], causal16[:], 0, [[-1, P]], 1, ALU.is_ge, NEG)
            gp.tensor_copy(ident16[:], ident[:])
            gp.memset(cmp_neg[:], 0.0)
            select(cmp_neg[:], cmp_neg[:], -31, [[P, 2], [-16, NCMP]], 1, ALU.is_ge, NEG)
            gp.memset(cmp_one[:], 1.0)
            select(cmp_one[:], cmp_one[:], -31, [[P, 2], [-16, NCMP]], 1, ALU.is_ge, 0.0)
            select(in16[:], ones[:, 0:8], 0, [[-16, 8]], 1, ALU.is_ge, 0.0)
            select(in16[:], in16[:], 15, [[16, 8]], -1, ALU.is_ge, 0.0)
            select(in64[:], ones[:, 0:2], 0, [[-64, 2]], 1, ALU.is_ge, 0.0)
            select(in64[:], in64[:], 63, [[64, 2]], -1, ALU.is_ge, 0.0)
            pool.drain()
            i16 = in16[:].rearrange("p (a b) -> p b a", b=2)
            gp.tensor_tensor(par16[:], i16[:, :, 0], i16[:, :, 1], ALU.add)
            gp.tensor_scalar(neg64[:], in64[:], -1.0, None, ALU.mult)
            for k in (2, 3):
                pool.drain()
                gp.tensor_tensor(par16[:], par16[:], i16[:, :, k], ALU.add)
            pool.drain().then_inc(s("consts_ready"), 1)

            def tt(out, a_, b_, op):
                gp.tensor_tensor(out, a_, b_, op)

            pool.wait_ge(s("disc_a"), 1)
            lr, li = bl[:, 0], bl[:, 1]
            dt = bst_.unsqueeze(2).broadcast_to([P, KT, 64])
            tt(e[0], lr, dt, ALU.mult)
            tt(e[1], li, dt, ALU.mult)
            tt(pe_[0], V("lam_re"), pst, ALU.mult)
            tt(pe_[1], V("lam_im"), pst, ALU.mult)
            tt(e[4], lr, lr, ALU.mult)
            tt(e[5], li, li, ALU.mult)
            pool.drain()
            tt(e[4], e[4], e[5], ALU.add)
            pool.drain().then_inc(s("disc_e"), 1)
            for ang, tmp in ((e[1], e[2]), (pe_[1], pe_[2])):
                gp.tensor_scalar(ang, ang, 1.0 / (2 * np.pi), None, ALU.mult)
                pool.drain()
                gp.tensor_scalar(tmp, ang, MAGIC, None, ALU.add)
                pool.drain()
                gp.tensor_scalar(tmp, tmp, MAGIC, None, ALU.subtract)
                pool.drain()
                tt(ang, ang, tmp, ALU.subtract)
                pool.drain()
            gp.tensor_copy(theta[:, 0:PAIRS], pe_[1])
            gp.memset(theta[:, PAIRS:PAIRS + 4], 0.0)
            pool.drain().then_inc(s("disc_b"), 1)
            pool.wait_ge(s("disc_c"), 1)
            tt(e[2], e[0], e[2], ALU.mult)
            tt(e[3], e[0], e[3], ALU.mult)
            pool.drain()
            gp.tensor_scalar(e[2], e[2], 1.0, None, ALU.subtract)
            pool.drain()
            tt(e[0], e[2], lr, ALU.mult)
            tt(e[1], e[3], li, ALU.mult)
            tt(e[5], e[3], lr, ALU.mult)
            tt(e[6], e[2], li, ALU.mult)
            pool.drain()
            tt(e[0], e[0], e[1], ALU.add)
            tt(e[5], e[5], e[6], ALU.subtract)
            pool.wait_ge(s("disc_f"), 1)
            pool.drain()
            tt(e[0], e[0], e[4], ALU.mult)
            tt(e[5], e[5], e[4], ALU.mult)
            pool.drain()
            tt(BB[:, 0], e[0], br_[:, 0], ALU.mult)
            tt(e[1], e[5], br_[:, 1], ALU.mult)
            tt(BB[:, 1], e[0], br_[:, 1], ALU.mult)
            tt(e[2], e[5], br_[:, 0], ALU.mult)
            pool.drain()
            tt(BB[:, 0], BB[:, 0], e[1], ALU.subtract)
            tt(BB[:, 1], BB[:, 1], e[2], ALU.add)
            pool.drain().then_inc(s("disc_done"), 1)
            meet(pool, met)
            split("mix", SQ)
            with pool.Fori(0, HEADS) as i:
                for g in range(5):
                    low("heads", i, g, g)
                for n in range(2):
                    for half in range(2):
                        vec_times("heads", i, 5 + n, 0, half)
            meet(pool, met)
            split("merged", SQ)
            with pool.Fori(0, 2) as i:
                for g in range(8):
                    m = g // 2

                    def after(half):
                        if g % 2 == 0:
                            vec_times("w_out", i, 5 * m + 1, 0, half)
                        else:
                            vec_times("w_out", i, 5 * m + 3, 0, half)

                    low("w_out", i, g, 5 * m + 2 * (g % 2), between=after)
                    if g == 1:
                        for half in range(2):
                            vec_times("w_out", i, 4, 0, half)
            meet(pool, met)
            split("ffn", SQ)
            with pool.Fori(0, 4) as i:
                for h in range(2):
                    for half in range(2):
                        low("topk", i, 2 * h + half, 4 * h + half, first=0)
            pool.sem_inc(s("gelu_free"), 2)
            meet(pool, met)
            with pool.Fori(0, 16) as g:
                for n in range(16):
                    pos = 12 * (n // 8) + 3 * (n % 8 // 2) + n % 2
                    vec = n // 2 - 1

                    def after(half):
                        if n % 2 == 0 and n > 0:
                            vec_times("peer", g, 3 * vec + 2, 1, half)

                    low("peer", g, n, pos, n >= 8, between=after)
                for half in range(2):
                    vec_times("peer", g, 23, 1, half)
            meet(pool, met)
            split("l0", SQ)
            pool.sem_inc(s("q_ready"), 4)
            pool.sem_inc(s("y_pair"), 5)
            pool.sem_inc(s("y_read"), 2)
            meet(pool, met)

            def fraction(n):
                pool.wait_ge(s("phase_ready"), n + 1)
                gp.tensor_tensor(ph[:], ph[:], rn[:], ALU.subtract)
                pool.drain().then_inc(s("frac_ready"), 1)

            fraction(0)
            fraction(1)
            with pool.Fori(0, 8) as i:
                for t in range(2):
                    tile = 2 * i + t
                    pool.wait_ge(s("y_pair"), 4 * tile + 1)
                    for ri in range(2):
                        gp.tensor_tensor(Bst[:, t, ri], BB[:, ri, bass.ds(tile, 1), :].broadcast_to([P, 2, 64]),
                                         par16[:].unsqueeze(2).broadcast_to([P, 2, 64]), ALU.mult)
                    for ri in range(2):
                        gp.tensor_tensor(Cst[:, t, ri],
                                         CC[:, ri, bass.ds(4 * tile, 4), :].unsqueeze(2).broadcast_to([P, 4, 2, 16]),
                                         (in64, neg64)[ri][:].unsqueeze(1).unsqueeze(3).broadcast_to([P, 4, 2, 16]),
                                         ALU.mult)
                    pool.drain().then_inc(s("masks_built"), 1)
                    low("ssm", i, 2 * t, 2 * t)
                    low("ssm", i, 2 * t + 1, 2 * t + 1)
                    for j in range(4):
                        duo, k = j // 2, j % 2
                        pool.wait_ge(s("z_ready"), 4 * tile + j + 1)
                        gp.tensor_tensor(Q1, Z[:, j % 2], tab[:, duo, 0, k:k + 1, :].broadcast_to([P, 2, T]), ALU.mult)
                        gp.tensor_tensor(Q2, Z[:, j % 2], tab[:, duo, 1, k:k + 1, :].broadcast_to([P, 2, T]), ALU.mult)
                        pool.drain()
                        pool.wait_ge(s("y_pair"), 4 * tile + j + 4)
                        gp.tensor_tensor(X[:, j % 2, 0, :], Q1[:, 0, :], Q2[:, 1, :], ALU.subtract)
                        gp.tensor_tensor(X[:, j % 2, 1, :], Q2[:, 0, :], Q1[:, 1, :], ALU.add)
                        pool.drain().then_inc(s("q_ready"), 1)
                        if j % 2 == 1:
                            fraction(2 * tile + 2 + duo)
            split("y", Y)
            plain("glu")
            split("glu", SZ)
            plain("ssm_out")
            meet(pool, met)
            split("kv", SQ)
            plain("kv")
            split("l1", SQ)
            meet(pool, met)
            with pool.Fori(0, KV) as g:
                pool.wait_ge(s("on_in_psum"), 4 * g + 1)
                gp.tensor_copy(Vg, VR[:, bass.ds(g, 1)].rearrange("p g a b c -> p (g a) b c"))
                gp.tensor_copy(VCg[0:NCMP], VCr[0:NCMP, bass.ds(g, 1), :].rearrange("p a b -> p (a b)"))
                pool.drain().then_inc(s("vg_ready"), 1)
                for c in range(16):
                    low("nsa", g, c, c)
            meet(pool, met)
            split("o", O)
            plain("w_o")
            meet(pool, met)


def _tiles(w):
    return np.ascontiguousarray(w.reshape(KT, P, w.shape[1] // P, P).transpose(2, 1, 0, 3))


def _cols(v):
    return v.reshape(-1, P).T


def kernel(**inputs):
    import concourse.bacc as bacc
    from concourse.bass_utils import run_bass_kernel_spmd
    i = {k: np.asarray(v) for k, v in inputs.items()}
    w_in = i["w_in"][0]
    heads = [w_in[:, off + P * h:off + P * (h + 1)] for h in range(HEADS) for off in (0, 1024, 2048, 3080, 4104)]
    qg = i["nsa_w_qg_2"][0]
    qz = []
    for g in range(KV):
        qz += [qg[:, P * (HPG * g + h):P * (HPG * g + h + 1)] for h in range(HPG)]
        qz += [qg[:, 2096 + P * (16 * b + HPG * g + h):2096 + P * (16 * b + HPG * g + h + 1)]
               for h in range(HPG) for b in range(3)]
    vecs = dict(
        c=_cols(i["c"]), c2=_cols(i["c_2"]), b_ada=_cols(i["b_ada"]),
        b_mod2=np.concatenate([_cols(i["mod_b_2"]), _cols(i["kv_mod_b_2"])], axis=1),
        g_mix=_cols(i["g_mix"]), g_ffn=_cols(i["g_ffn"]), g_final=_cols(i["g_final"]),
        g_merge=np.concatenate([_cols(i["g_attn_out"]), _cols(i["g_lru_out"])], axis=1),
        g_l0=_cols(i["norm_g_2"][0]), g_l1=_cols(i["norm_g_2"][1]), g_kv=_cols(i["kv_norm_g_2"]),
        g_final2=_cols(i["final_norm_g_2"]),
        conv_w=i["conv_w"][0].reshape(4, HEADS, P).transpose(2, 1, 0).reshape(P, 32),
        conv_b=_cols(i["conv_b"]), lru_b_a=_cols(i["lru_b_a"]), lru_b_x=_cols(i["lru_b_x"]),
        lru_lambda=_cols(i["lru_lambda"]), ssm_d=_cols(i["ssm_d_2"]), b_glu=_cols(i["ssm_b_glu_2"]),
        cmp_b1=_cols(i["cmp_b1_2"]), cmp_b2=_cols(i["cmp_b2_2"]), cmp_pe=_cols(i["cmp_pe_2"]),
        lam_re=i["ssm_lam_re_2"].reshape(PAIRS, P).T, lam_im=i["ssm_lam_im_2"].reshape(PAIRS, P).T)
    arrays = dict(
        x=i["x"][0].reshape(T, KT, P).transpose(2, 1, 0),
        vec=np.concatenate([vecs[n] for n, _ in VEC], axis=1),
        w_f=w_in[:, 3072:3080].reshape(KT, P, 8).transpose(1, 0, 2),
        b_f=i["b_f"].reshape(8, 1),
        w_ada=_tiles(i["w_ada"][0]),
        w_in=_tiles(np.concatenate(heads, axis=1)),
        gate_w=np.stack([i["lru_w_a"][0], i["lru_w_x"][0]], axis=2).reshape(HEADS, P, 2, P),
        w_out=_tiles(i["w_out"][0]),
        w_q=_tiles(i["peer_w_q"][0]),
        k12=np.stack([i["peer_k1"][0], i["peer_k2"][0]]).transpose(3, 0, 1, 2),
        w_mod2=_tiles(np.concatenate([i["mod_w_2"][0], i["mod_w_2"][1], i["kv_mod_w_2"]], axis=1)),
        peer_u=i["peer_u"][0].reshape(P, P, KT, P).transpose(1, 3, 2, 0),
        peer_v=i["peer_v"][0].reshape(P, 16, 8, 8, 2 * P).transpose(1, 3, 0, 2, 4).reshape(P, P, KT, P),
        ssm_in=_tiles(i["ssm_w_in_2"][0]),
        step_pair=i["ssm_log_step_2"].reshape(PAIRS, 2).T,
        step_tile=i["ssm_log_step_2"].reshape(KT, 8).T,
        lam_tile=np.stack([i["ssm_lam_re_2"].reshape(KT, 8, 64), i["ssm_lam_im_2"].reshape(KT, 8, 64)]).transpose(2, 0, 1, 3),
        ssm_b=np.stack([i["ssm_b_re_2"], i["ssm_b_im_2"]]).reshape(2, KT, 8, 64, 16).transpose(2, 4, 0, 1, 3).reshape(P, 2, KT, 64),
        ssm_c=np.stack([i["ssm_c_re_2"], i["ssm_c_im_2"]]).reshape(2, PAIRS, 2, 16, 64).transpose(2, 4, 0, 1, 3).reshape(P, 2, PAIRS, 16),
        w_glu=_tiles(i["ssm_w_glu_2"][0]), ssm_out=_tiles(i["ssm_w_out_2"][0]),
        w_kv=_tiles(i["w_kv_2"]),
        cmp_w1=i["cmp_w1_2"].reshape(2, CMP_L, P, P).transpose(2, 0, 1, 3),
        cmp_w2=i["cmp_w2_2"].transpose(1, 0, 2),
        w_gate=qg[:, 2048:2096].reshape(KT, P, 48).transpose(1, 0, 2),
        w_qz=_tiles(np.concatenate(qz, axis=1)), w_o=_tiles(i["nsa_w_o_2"][0]))
    nc = bacc.Bacc("TRN2", target_bir_lowering=False, num_devices=1)
    feed, aps = {}, {}
    for name, value in arrays.items():
        feed["in_" + name] = np.ascontiguousarray(value)
        aps[name] = nc.dram_tensor("in_" + name, value.shape, mybir.dt.from_np(value.dtype), kind="ExternalInput").ap()
    aps["disc"] = nc.dram_tensor("discretised", (P, 2 * KT * 64 + 2 * PAIRS + 4), F32, kind="Internal").ap()
    aps["out"] = nc.dram_tensor("out_0", (P, KT, T), F32, kind="ExternalOutput").ap()
    build(nc, aps)
    res = run_bass_kernel_spmd(nc, [feed], core_ids=[0])
    return np.ascontiguousarray(res.results[0]["out_0"].transpose(2, 1, 0)).reshape(1, T, D)
```

```python
import concourse.bass as bass
from concourse import mybir
from contextlib import ExitStack
import numpy as np

F32 = mybir.dt.float32
F32R = mybir.dt.float32r
BF16 = mybir.dt.bfloat16
U32 = mybir.dt.uint32
I32 = mybir.dt.int32
ALU = mybir.AluOpType
ACT = mybir.ActivationFunctionType
AX = mybir.AxisListType.X

P = 128
T = 256
D = 2048
KT = D // P
R = 4
HEADS = 8
SCALE = float(P) ** -0.5
EPS = 1e-6
NEG = -1e30
LOW = -3.0e38
LRU_C = 8.0
TOPK = 16
SLOTS = HEADS * TOPK
NQ = 4
QW = P // NQ
KV = 4
HPG = 4
NCMP = (T - 32) // 16 + 1
CMP_L = 32
PAIRS = 64
MAGIC = 12582912.0
TWO_PI = 6.283185
HALF_PI = 1.5707963

STAGES = dict(shift_scale=(4, 8, 0, 2), heads=(8, HEADS, 5, 3), w_out=(20, 2, 8, 12), topk=(8, 4, 4, 0),
              peer=(24, 16, 16, 8), ssm=(4, 8, 4, 0), glu=(8, 2, 8, 0), ssm_out=(8, 2, 8, 0), kv=(8, 3, 8, 0),
              nsa=(16, KV, 16, 0), w_o=(8, 2, 8, 0))
STREAM = [(name, b * n) for name, (b, n, _, _) in STAGES.items()]
CHUNK0, GEMM0, VEC0 = {}, {}, {}
_c = _g = _v = 0
for _name, (_b, _n, _gb, _vb) in STAGES.items():
    CHUNK0[_name], GEMM0[_name], VEC0[_name] = _c, _g, _v
    _c, _g, _v = _c + _b * _n, _g + _gb * _n, _v + _vb * _n
DVE_K = 5


def use_of(stage, i, pos):
    return CHUNK0[stage] // R + (STAGES[stage][0] // R) * i + pos // R


def half_of(stage, i, gemm, half):
    return 2 * (GEMM0[stage] + STAGES[stage][2] * i + gemm) + half


VEC = [("b_ada", 96), ("b_mod2", 128), ("g_mix", 16), ("g_ffn", 16),
       ("g_final", 16), ("g_merge", 16), ("g_l0", 16), ("g_l1", 16), ("g_kv", 16), ("g_final2", 16),
       ("conv_w", 32), ("conv_b", 8), ("lru_b_a", 8), ("lru_b_x", 8), ("lru_lambda", 8), ("ssm_d", 16),
       ("b_glu", 16), ("cmp_b1", 2), ("cmp_b2", 2), ("cmp_pe", 64), ("lam_re", 64), ("lam_im", 64)]
VOFF = {}
for _name, _n in VEC:
    VOFF[_name] = sum(n for m, n in VEC if m in VOFF)
NVEC = sum(n for _, n in VEC)


def build(nc, a):
    ctx = ExitStack()
    with ctx:
        def sb(name, shape, dt=F32):
            return ctx.enter_context(nc.sbuf_tensor(name, shape, dt))

        def sem(name):
            return ctx.enter_context(nc.semaphore(name))

        ring = sb("ring", [P, R, KT, P])
        x = sb("x", [P, KT, T])
        Hhi = sb("Hhi", [P, KT, T], F32R)
        Hlo = sb("Hlo", [P, KT, T], F32R)
        Ghi = sb("Ghi", [P, 8, T], F32R)
        Glo = sb("Glo", [P, 8, T], F32R)
        whi = sb("whi", [P, 2, 8, P], F32R)
        wlo = sb("wlo", [P, 2, 8, P], F32R)
        vec = sb("vec", [P, NVEC])
        mod_ab = sb("mod_ab", [P, 2, 224])
        mod = mod_ab[:, 0]
        sums = sb("sums", [P, R, 2])
        gain = sb("gain", [P, 5, KT])
        cond = sb("cond", [P, D])
        cst = sb("cst", [P, 2])
        ident = sb("ident", [P, P])
        ones = sb("ones", [P, T])
        iota_t = sb("iota_t", [P, T])
        cmp_neg = sb("cmp_neg", [P, 2, NCMP])
        cmp_one = sb("cmp_one", [P, 2, NCMP])
        in16 = sb("in16", [P, 8])
        par16 = sb("par16", [P, 2])
        in64 = sb("in64", [P, 2])
        neg64 = sb("neg64", [P, 2])
        ident16 = sb("ident16", [P, P], BF16)
        causal16 = sb("causal16", [P, P], BF16)
        iota16b = sb("iota16b", [P, P], BF16)
        var = sb("var", [P, 2, T])
        sd = sb("sd", [P, 2, T])
        rstd = sb("rstd", [P, 2, T])
        NA = 18800
        arena = sb("arena", [P, NA])
        banks = [ctx.enter_context(nc.psum_tensor(f"bank{i}", [P, 512], F32)) for i in range(4)]
        WA = ctx.enter_context(nc.psum_tensor("work_a", [P, 512], F32))
        WB = ctx.enter_context(nc.psum_tensor("work_b", [P, 512], F32))
        WC = ctx.enter_context(nc.psum_tensor("work_c", [P, 512], F32))

        def V(name, n=None):
            o = VOFF[name]
            return vec[:, o:o + (n or dict(VEC)[name])]

        class Region:
            def __init__(self, at=0):
                self.at = at

            def __call__(self, *shape, parts=P, dt=None):
                n = int(np.prod(shape))
                v = arena[0:parts, self.at:self.at + n]
                self.at += n
                assert self.at <= NA, self.at
                if dt is not None:
                    v = v.bitcast(dt)
                if len(shape) == 1:
                    return v
                names = "abcdef"[:len(shape)]
                return v.rearrange(f"p ({' '.join(names)}) -> p {' '.join(names)}",
                                   **{k: s for k, s in zip(names[1:], shape[1:])})

        r = Region()
        M = r(KT, T)
        Qh, Kh, VTh = r(T), r(T), r(T)
        LX = r(T + 4)
        LY = r(T)
        Vr = r(2, P)
        Pr = r(3, P)
        PT = r(3, P)
        xc, rg, ig, ut, at_, t1, t2, gx = [r(T) for _ in range(8)]
        gate_w = r(2, P)
        w_f = Region(18568)(KT, 8)
        rowmax, rowsum, rowrec = r(2), r(2), r(2)
        sp8, lam_t = r(2, 8), r(3, 8)
        fl = r(6, T, parts=8)
        cm = r(2, T, parts=8)
        SQ = Region(14472)(KT, T)
        itmp = Region(14472)(T, dt=I32)
        b_f = sb("b_f", [8, 1])


        r = Region()
        cols = r(2, T)
        parts = arena[:, 2 * T:7 * T // 2].bitcast(BF16).rearrange("p (a b) -> p a b", a=3)
        r.at = 7 * T // 2
        weight = var[:, 0]
        eqB = [var[:, 0, P * k:P * k + P].bitcast(BF16).rearrange("p (b c) -> p b c", c=QW) for k in range(2)]
        Wd = r(2, QW, T)
        GL = rstd
        hotA = [h.bitcast(BF16).rearrange("p (b c) -> p b c", b=8)
                for h in (arena[:, r.at:r.at + 512], sd[:].rearrange("p a b -> p (a b)"))]
        r.at += 512
        hotB = arena[:, r.at:r.at + 768].bitcast(BF16).rearrange("p (a b k c) -> p a b k c", a=2, b=8, k=3)
        r.at += 768
        assert r.at <= NA
        r = Region(5 * T)
        k12 = r(2, HEADS, P)
        Qp = r(2, T)
        S4 = r(4, P)
        v1f, v2f = r(TOPK), r(TOPK)
        i1u, i2u = r(TOPK, dt=U32), r(TOPK, dt=U32)
        i1f, i2f = r(TOPK), r(TOPK)
        cand = r(TOPK, TOPK)
        vs = r(TOPK)
        ic, ich, icl = r(TOPK, dt=U32), r(TOPK, dt=U32), r(TOPK, dt=U32)
        chf, clf = r(TOPK), r(TOPK)
        hot1, hot2 = r(TOPK, TOPK), r(TOPK, TOPK)
        picked = r(3, 2, HEADS, TOPK)
        pmax, psum_, prec = r(2, HEADS), r(2, HEADS), r(2, HEADS)

        r = Region()
        Y = r(KT, T)
        SZ = r(KT, T)
        BB = r(2, KT, 64)
        theta = r(PAIRS + 4)
        mag = r(PAIRS)
        disc = arena[:, 2 * KT * T:r.at]
        CC = r(2, PAIRS, 16)
        ssm_at = r.at
        Bst = r(2, 2, 2, 64)
        Cst = r(2, 2, 4, 2, 16)
        Us = r(2, T)
        tab = cond[:].rearrange("p (a b c d) -> p a b c d", a=2, b=2, c=2)
        ph, rn, Wr = sd, rstd, var
        P1, P2 = r(2, T), r(2, T)
        Z = r(2, 2, T)
        Q1, Q2 = r(2, T), r(2, T)
        X = r(2, 2, T)
        glt = P1
        r = Region()
        bl = r(2, KT, 64)
        bst_ = r(KT)
        br_ = r(2, KT, 64)
        pst = r(PAIRS)
        pe_ = [r(PAIRS) for _ in range(3)]
        e = [r(KT, 64) for _ in range(3)]
        assert r.at <= 2 * KT * T
        r = Region(ssm_at - 2 * PAIRS * 16)
        e += [r(KT, 64) for _ in range(4)]
        assert r.at <= 14472

        r = Region()
        KVT = r(6 * KV, T)
        VR = r(KV, 2, 2, P)
        VCr = r(KV, P, parts=16)
        KC, VCt = r(KV, NCMP), r(KV, NCMP)
        wg = r(KT, 48)
        GT = r(2, 48)
        nsa_at = r.at
        W1 = r(CMP_L, P)
        W2 = r(2, P)
        GC = r(KV * NCMP)
        b1e = r(2)
        r = Region(nsa_at)
        O = r(KT, T)
        Qg = r(HPG, T)
        Vg = r(2, 2, P)
        VCg = r(P, parts=16)
        Pn = r(2, 3, P)
        Pc = r(2, NCMP)
        PTn = r(2, 3, P)
        PTc = r(2, P, parts=16)
        SZn = cond[:, 0:2 * 3 * T].rearrange("p (a b c) -> p a b c", a=2, b=3)
        ot = r(3, T)
        mx, sm, rc = r(6), r(6), r(6)

        slot_loaded = [sem(f"slot{i}_loaded") for i in range(R)]
        slot_free = [sem(f"slot{i}_free") for i in range(R)]
        bank_free = [sem(f"bank{i}_free") for i in range(4)]
        stage_end = sem("stage_end")
        params = sem("params_loaded")
        x_loaded = sem("x_loaded")
        S = {}

        def s(name):
            if name not in S:
                S[name] = sem(name)
            return S[name]

        for name in ("consts_ready cond_ready norm_src half_done hi_ready lo_dve lo_pool prod_ready biased "
                     "hhi_ready disc_e disc_f disc_saved hot_equal lam_ready cond_loaded disc_loaded w1b_used "
                     "squares_ready sums_ready var_ready sd_ready scaled_ready h_ready f_in_psum f_ready "
                     "log1p_ready cum_ready gatew_loaded qk_ready vt_ready cm_ready scores_ready negmax_ready "
                     "exps_ready probs_ready xc_ready gates_in_psum lru_u_ready lru_t_ready lru_sq_ready "
                     "ly_ready lru_done vrows_in_psum vrows_ready pt_in_psum pt_ready attn_in_psum attn_ready "
                     "k_loaded peerq_ready s_in_psum s_ready vs_ready vs_exp picked_ready cols_in_psum hot_ready "
                     "hot_used wd_copied gelu_ready g_ready ssm_loaded disc_a disc_b disc_c disc_done "
                     "masks_built u_ready bu_in_psum bu_read phase_ready frac_ready table_ready z_ready q_ready "
                     "y_pair gelu_free glu_free y_read y_gelu sig_ready w1_loaded kv_ready vr_in_psum vr_ready "
                     "b1e_ready cmp_gelu cmp2_in_psum kc_ready vc_in_psum gt_in_psum vg_ready q_ready2 "
                     "sn_in_psum negmax2 exps2 probs2 ptn_in_psum ptn_ready on_in_psum sz_ready combined "
                     "out_ready stored").split():
            s(name)

        block = ctx.enter_context(nc.Block())

        def meet(eng, state):
            eng.drain().then_inc(stage_end, 1)
            state[0] += 4
            eng.wait_ge(stage_end, state[0])

        def norm_groups(g):
            return [(j, 0 if g == 1 or j < 2 else 1) for j in range(4)]


        GRANTED = dict(pe=('gates_in_psum', 's_in_psum', 'on_in_psum'), act=('attn_ready', 'pt_ready', 'lru_u_ready'),
                       dve=('lru_done', 's_ready', 'g_ready', 'combined'))

        NORMS = dict(mix=0, merged=1, ffn=2, final=3, l0=4, l1=5, final2=6)

        POOL_VECS = dict(topk=4, peer=4)
        POOL_VEC0 = dict(topk=0, peer=16)
        half_done = s("half_done")
        SPLITS = dict(mix=0, merged=1, ffn=2, l0=3, y=4, glu=5, kv=6, l1=7, o=8)

        def loaded(eng, stage, i, pos):
            eng.wait_ge(slot_loaded[pos % R], 16 * (use_of(stage, i, pos) + 1))

        def product(eng, stage, i, gemm):
            eng.wait_ge(half_done, half_of(stage, i, gemm, 1) + 3)

        def half_chunk(pos, half, by_column=False):
            if by_column:
                return ring[:, pos % R].rearrange("p k n -> p (k n)")\
                    .rearrange("p (k n) -> p k n", k=8)[:, :, P * half:P * half + P]
            return ring[:, pos % R, 8 * half:8 * half + 8, :]

        @block.sync
        def _(sp):
            def load(stage, i, pos, src, first=False):
                if not first:
                    sp.wait_ge(slot_free[pos % R], 2 * use_of(stage, i, pos))
                sp.dma_start(ring[:, pos % R], src).then_inc(slot_loaded[pos % R], 16)

            def plain(stage, src, at=0):
                body, n = STAGES[stage][0:2]
                with sp.Fori(0, n) as i:
                    for pos in range(body):
                        load(stage, i, pos, src[at + body * i + pos])

            sp.dma_start(x[:], a["x"]).then_inc(x_loaded, 16)
            for pos in range(4):
                load("shift_scale", 0, pos, a["w_ada"][pos], first=True)
            with sp.Fori(1, 8) as i:
                for pos in range(4):
                    load("shift_scale", i, pos, a["w_ada"][4 * i + pos])
            sp.wait_ge(stage_end, 4)
            with sp.Fori(0, HEADS) as i:
                load("heads", i, 0, a["w_in"][5 * i])
                sp.wait_ge(s("gates_in_psum"), i + 1)
                sp.dma_start(gate_w, a["gate_w"][i]).then_inc(s("gatew_loaded"), 16)
                for pos in range(1, 5):
                    load("heads", i, pos, a["w_in"][5 * i + pos])
                for pos in range(3):
                    load("heads", i, 5 + pos, a["w_ada"][32 + 3 * i + pos])
            with sp.Fori(0, 2) as i:
                for m in range(4):
                    for k, pos in enumerate((0, 1, 2, 3, 4)):
                        src = a["w_out"][8 * i + 2 * m + k // 2] if k in (0, 2) else \
                            a["w_ada"][56 + 12 * i + 3 * m + (0, 0, 0, 1, 2)[k]]
                        load("w_out", i, 5 * m + pos, src)
            with sp.Fori(0, 4) as i:
                for h in range(2):
                    for k in range(2):
                        load("topk", i, 4 * h + k, a["w_q"][4 * i + 2 * h + k])
                    for k in range(2):
                        load("topk", i, 4 * h + 2 + k, a["w_ada"][80 + 4 * i + 2 * h + k])
            with sp.Fori(0, 16) as g:
                for half, name in enumerate(("peer_u", "peer_v")):
                    for m in range(4):
                        for k in range(2):
                            load("peer", g, 12 * half + 3 * m + k, a[name][8 * g + 2 * m + k])
                        load("peer", g, 12 * half + 3 * m + 2, a["w_mod2"][8 * g + 4 * half + m])
            with sp.Fori(0, 8) as i:
                for t in range(2):
                    load("ssm", i, 2 * t, a["ssm_in"][2 * i + t])
                    load("ssm", i, 2 * t + 1, a["ssm_in"][KT + 2 * i + t])
            plain("glu", a["w_glu"])
            plain("ssm_out", a["ssm_out"])
            plain("kv", a["w_kv"])
            plain("nsa", a["w_qz"])
            plain("w_o", a["w_o"])
            sp.wait_ge(s("out_ready"), 1)
            sp.dma_start(a["out"], SQ).then_inc(s("stored"), 16)
            sp.wait_ge(s("stored"), 16)

        @block.tensor
        def _(pe):
            mm = nc.tensor.matmul
            met = [0]
            uses = [0, 0, 0, 0]

            def gemm(stage, i, g, out, bank, need=None, rhs=(Hhi, Hlo), halves=(0, 1)):
                if need is not None:
                    pe.wait_ge(bank_free[bank], need + 1)
                for half in halves:
                    n = half_of(stage, i, g, half)
                    pe.wait_ge(s("hi_ready"), n + 1)
                    for k in range(8):
                        kk = 8 * half + k
                        mm(out, whi[:, half, k, :], rhs[0][:, kk, :], start=(kk == 0), stop=False)
                        mm(out, whi[:, half, k, :], rhs[1][:, kk, :], start=False, stop=False)
                    pe.wait_ge(s("lo_dve"), n + 1)
                    pe.wait_ge(s("lo_pool"), n + 1)
                    for k in range(8):
                        kk = 8 * half + k
                        last = mm(out, wlo[:, half, k, :], rhs[0][:, kk, :], start=False, stop=(kk == KT - 1))
                    last.then_inc(half_done, 1)

            def gemm_v(g, n_, bank, need):
                pe.wait_ge(bank_free[bank], need + 1)
                for dd in range(2):
                    n = half_of("peer", g, 8 + n_, dd)
                    out = banks[bank][:, T * dd:T * dd + T]
                    pe.wait_ge(s("hi_ready"), n + 1)
                    for k in range(8):
                        if n_ == 0 and dd == 0:
                            pe.wait_ge(s("g_ready"), 8 * g + k + 2)
                        mm(out, whi[:, dd, k, :], Ghi[:, k, :], start=(k == 0), stop=False)
                        mm(out, whi[:, dd, k, :], Glo[:, k, :], start=False, stop=False)
                    pe.wait_ge(s("lo_dve"), n + 1)
                    pe.wait_ge(s("lo_pool"), n + 1)
                    for k in range(8):
                        last = mm(out, wlo[:, dd, k, :], Ghi[:, k, :], start=False, stop=(k == 7))
                    last.then_inc(half_done, 1)

            def norm_sums(name, groups=1):
                n = NORMS[name]
                for j, g in norm_groups(groups):
                    pe.wait_ge(s("squares_ready"), 4 * n + j + 1)
                    for k in range(4):
                        t = 4 * j + k
                        last = mm(WA[:, g * T:(g + 1) * T], ones[:, 0:P], SQ[:, t, :],
                                  start=(t % (KT // groups) == 0), stop=(t % (KT // groups) == KT // groups - 1))
                last.then_inc(s("sums_ready"), 1)

            def split_done(name):
                pe.wait_ge(s("h_ready"), 4 * (SPLITS[name] + 1))

            def plain(stage):
                body, n = STAGES[stage][0:2]
                with pe.Fori(0, n) as i:
                    for g in range(body):
                        gemm(stage, i, g, banks[g % 4][:, 0:T], g % 4, uses[g % 4] + body // 4 * i + g // 4)
                for b in range(4):
                    uses[b] += body * n // 4

            for name in GRANTED["pe"]:
                pe.sem_inc(s(name), 1)
            pe.sem_inc(half_done, 2)
            pe.wait_ge(s("consts_ready"), 1)
            norm_sums("mix")
            meet(pe, met)
            split_done("mix")
            for k in range(KT):
                last = mm(WB[0:8, 0:T], w_f[:, k, :], SQ[:, k, :], start=(k == 0), stop=(k == KT - 1))
            last.then_inc(s("f_in_psum"), 1)
            pe.wait_ge(s("cum_ready"), 1)
            with pe.Fori(0, HEADS) as i:
                gemm("heads", i, 0, banks[2][:, 0:T], 2, i)
                gemm("heads", i, 1, banks[0][:, 0:T], 0, i)
                gemm("heads", i, 2, banks[0][:, T:2 * T], 0)
                pe.wait_ge(s("xc_ready"), i + 1)
                pe.wait_ge(s("gatew_loaded"), 16 * (i + 1))
                pe.wait_ge(s("lru_u_ready"), i + 1)
                for g in range(2):
                    last = mm(WC[:, T * g:T * g + T], gate_w[:, g, :], xc, start=True, stop=True)
                last.then_inc(s("gates_in_psum"), 1)
                gemm("heads", i, 3, banks[1][:, 0:T], 1, i, halves=(0,))
                pe.wait_ge(s("qk_ready"), i + 1)
                pe.wait_ge(s("cm_ready"), i + 1)
                pe.wait_ge(s("attn_ready"), i + 1)
                for qt in range(2):
                    nk = P * (qt + 1)
                    out = WA[:, P * qt:P * qt + nk]
                    mm(out, Qh[:, P * qt:P * qt + P], Kh[:, 0:nk], start=True, stop=False)
                    mm(out, cm[:, 0, P * qt:P * qt + P], ones[0:8, 0:nk], start=False, stop=False)
                    mm(out, ones[0:8, 0:P], cm[:, 1, 0:nk], start=False, stop=False)
                    last = mm(out[:, P * qt:P * qt + P], ident16[:], causal16[:], start=False, stop=True)
                last.then_inc(s("scores_ready"), 1)
                gemm("heads", i, 3, banks[1][:, 0:T], 1, halves=(1,))
                gemm("heads", i, 4, banks[3][:, 0:T], 3, i, halves=(0,))
                pe.wait_ge(s("vt_ready"), i + 1)
                for kt in range(2):
                    last = nc.tensor.transpose(banks[1][:, T + P * kt:T + P * kt + P], VTh[:, P * kt:P * kt + P], ident[:])
                last.then_inc(s("vrows_in_psum"), 1)
                pe.wait_ge(s("probs_ready"), i + 1)
                pe.wait_ge(s("pt_ready"), i + 1)
                for b in range(3):
                    last = nc.tensor.transpose(WB[:, P * b:P * b + P], Pr[:, b, :], ident[:])
                last.then_inc(s("pt_in_psum"), 1)
                gemm("heads", i, 4, banks[3][:, 0:T], 3, halves=(1,))
                pe.wait_ge(s("vrows_ready"), i + 1)
                pe.wait_ge(s("pt_ready"), i + 2)
                mm(WA[:, 0:P], Vr[:, 0, :], PT[:, 0, :], start=True, stop=True)
                mm(WA[:, P:T], Vr[:, 0, :], PT[:, 1, :], start=True, stop=False)
                mm(WA[:, P:T], Vr[:, 1, :], PT[:, 2, :], start=False, stop=True).then_inc(s("attn_in_psum"), 1)
            for b in range(4):
                uses[b] += HEADS
            meet(pe, met)
            norm_sums("merged", 2)
            split_done("merged")
            with pe.Fori(0, 2) as i:
                for g in range(8):
                    gemm("w_out", i, g, banks[g % 4][:, 0:T], g % 4, uses[g % 4] + 2 * i + g // 4)
            for b in range(4):
                uses[b] += 4
            meet(pe, met)
            norm_sums("ffn")
            split_done("ffn")
            pe.wait_ge(s("k_loaded"), 16)
            with pe.Fori(0, 4) as i:
                for h in range(2):
                    n = 2 * i + h
                    gemm("topk", i, 2 * h, banks[0][:, 0:T], 0, uses[0] + n)
                    gemm("topk", i, 2 * h + 1, banks[1][:, 0:T], 1, uses[1] + n)
                    pe.wait_ge(s("peerq_ready"), n + 1)
                    pe.wait_ge(s("s_ready"), n + 1)
                    for tt in range(2):
                        for half in range(2):
                            q = 2 * tt + half
                            last = mm(WA[:, P * q:P * q + P], Qp[:, half, P * tt:P * tt + P], k12[:, half, n, :],
                                      start=True, stop=True)
                    last.then_inc(s("s_in_psum"), 1)
            uses[0] += HEADS
            uses[1] += HEADS
            pe.wait_ge(s("picked_ready"), 1)
            for w in range(3):
                for tt in range(2):
                    last = nc.tensor.transpose((WA, WB, WC)[w][:, P * tt:P * tt + P],
                                               picked[:, w, tt].rearrange("p h k -> p (h k)"), ident[:])
            last.then_inc(s("cols_in_psum"), 1)
            meet(pe, met)

            pe.sem_inc(s("hot_used"), 2)

            def spread_unit(unit, bank):
                pe.wait_ge(s("wd_copied"), unit + 1)
                for h in range(2):
                    pe.wait_ge(s("hot_ready"), 2 * unit + h + 1)
                    for j in range(8):
                        o = QW * (8 * h + j)
                        for k in range(3):
                            last = mm(bank[:, o:o + QW], hotA[h][:, j, :], hotB[:, h, j, k, :],
                                      start=(k == 0), stop=(k == 2))
                    last.then_inc(s("hot_used"), 1)

            with pe.Fori(0, 4) as i:
                for u in range(4):
                    spread_unit(4 * i + u, (WB, WC)[u % 2])
            with pe.Fori(0, 16) as g:
                for n in range(8):
                    gemm("peer", g, n, banks[n % 4][:, 0:T], n % 4, uses[n % 4] + 4 * g + n // 4)
                    if n % 4 == 2:
                        spread_unit(4 * g + 16 + n // 4, (WB, WC)[n // 4])
                for n in range(8):
                    gemm_v(g, n, n % 4, uses[n % 4] + 4 * g + 2 + n // 4)
                    if n % 4 == 2:
                        spread_unit(4 * g + 18 + n // 4, (WB, WC)[n // 4])
            for b in range(4):
                uses[b] += 64
            meet(pe, met)
            norm_sums("final")
            norm_sums("l0")
            split_done("l0")
            meet(pe, met)
            pe.sem_inc(s("bu_read"), 2)
            def u_half(i, t, half):
                b = 2 * t % 4
                gemm("ssm", i, 2 * t, banks[b][:, 0:T], b, uses[b] + i + t // 2 if half == 0 else None, halves=(half,))

            def z_half(i, t, half):
                b = (2 * t + 1) % 4
                gemm("ssm", i, 2 * t + 1, banks[b][:, 0:T], b, uses[b] + i + t // 2 if half == 0 else None, halves=(half,))

            def b_times_u(i, t, j):
                tile = 2 * i + t
                if j == 0:
                    pe.wait_ge(s("u_ready"), tile + 1)
                    pe.wait_ge(s("masks_built"), tile + 1)
                pe.wait_ge(s("bu_read"), 4 * tile + j + 1)
                for ri in range(2):
                    done = mm((WA, WB)[j % 2][:, T * ri:T * ri + T],
                              Bst[32 * j:32 * j + 32, t % 2, ri].rearrange("p a b -> p (a b)"),
                              Us[32 * j:32 * j + 32, t % 2, :], start=True, stop=True, tile_position=(32 * j, 0))
                done.then_inc(s("bu_in_psum"), 1)

            def c_times_x(i, t, j):
                tile = 2 * i + t
                if j == 0:
                    pe.wait_ge(s("y_read"), tile + 2)
                pe.wait_ge(s("q_ready"), 4 + 4 * tile + j + 1)
                for ri in range(2):
                    done = mm(WC[32 * j:32 * j + 32, 0:T], Cst[:, t % 2, ri, j].rearrange("p a b -> p (a b)"),
                              X[:, j % 2, ri, :], start=(ri == 0), stop=(ri == 1), tile_position=(0, 32 * j))
                done.then_inc(s("y_pair"), 1)

            def ssm_tile(i, t, last=False):
                z_half(i, t, 0)
                b_times_u(i, t, 2)
                z_half(i, t, 1)
                c_times_x(i, t, 0)
                b_times_u(i, t, 3)
                if not last:
                    u_half(i, t + 1, 0)
                c_times_x(i, t, 1)
                if not last:
                    u_half(i, t + 1, 1)
                c_times_x(i, t, 2)
                if not last:
                    b_times_u(i, t + 1, 0)
                c_times_x(i, t, 3)
                if not last:
                    b_times_u(i, t + 1, 1)

            u_half(0, 0, 0)
            u_half(0, 0, 1)
            b_times_u(0, 0, 0)
            b_times_u(0, 0, 1)
            ssm_tile(0, 0)
            with pe.Fori(0, 7) as i:
                for t in (1, 2):
                    ssm_tile(i, t)
            ssm_tile(7, 1, last=True)
            for b in range(4):
                uses[b] += 8
            split_done("y")
            plain("glu")
            split_done("glu")
            plain("ssm_out")
            meet(pe, met)
            norm_sums("l1")
            split_done("kv")
            plain("kv")
            pe.wait_ge(s("kv_ready"), 6 * KV)
            for g in range(KV):
                if g >= 2:
                    pe.wait_ge(s("vr_ready"), g - 1)
                for b in range(2):
                    for kt in range(2):
                        o = P * (2 * b + kt)
                        last = nc.tensor.transpose((WA, WB)[g % 2][:, o:o + P],
                                                   KVT[:, (3 + 2 * b) * KV + g, P * kt:P * kt + P], ident[:])
                last.then_inc(s("vr_in_psum"), 1)
            nb = KV * NCMP
            for b in range(2):
                pe.wait_ge(s("w1_loaded"), (48, 64)[b])
                for l in range(CMP_L):
                    mm(WC[:, 64 * b:64 * b + nb], W1[:, l, :],
                       KVT[:, b * KV:(b + 1) * KV, l:l + 16 * (NCMP - 1) + 1:16],
                       start=(l == 0), stop=(l == CMP_L - 1))
                for l in range(CMP_L):
                    last = mm(WC[:, 128 + b:129 + b], W1[:, l, :], V("cmp_pe")[:, CMP_L * b + l:CMP_L * b + l + 1],
                              start=(l == 0), stop=(l == CMP_L - 1))
                last.then_inc(s("w1b_used"), 1)
            for b in range(2):
                pe.wait_ge(s("cmp_gelu"), b + 1)
                mm(WC[:, 192 + 64 * b:192 + 64 * b + nb], W2[:, b, :], GC, start=True, stop=True)\
                    .then_inc(s("cmp2_in_psum"), 1)
                pe.wait_ge(s("kc_ready"), b + 1)
            pe.wait_ge(s("vr_ready"), KV)
            for g in range(KV):
                last = nc.tensor.transpose(WA[0:NCMP, P * g:P * g + P], VCt[:, g, :], ident[:])
            last.then_inc(s("vc_in_psum"), 1)
            split_done("l1")
            for tt in range(2):
                for k in range(KT):
                    last = mm(WB[:, 64 * tt:64 * tt + 48], SQ[:, k, P * tt:P * tt + P], wg[:, k, :],
                              start=(k == 0), stop=(k == KT - 1))
            last.then_inc(s("gt_in_psum"), 1)
            meet(pe, met)
            with pe.Fori(0, KV) as g:
                for hh in range(HPG):
                    gemm("nsa", g, hh, banks[hh][:, 0:T], hh, uses[hh] + 4 * g)
                def z_half(z, half):
                    c = 4 + z
                    gemm("nsa", g, c, banks[c % 4][:, 0:T], c % 4, uses[c % 4] + 4 * g + c // 4 if half == 0 else None,
                         halves=(half,))

                z_half(0, 0)
                for hh in range(HPG):
                    n = 4 * g + hh
                    pe.wait_ge(s("q_ready2"), n + 1)
                    pe.wait_ge(s("combined"), n + 1)
                    for br in range(2):
                        for qt in range(2):
                            nk = P * (qt + 1)
                            out = (WA, WB)[br][:, P * qt:P * qt + nk]
                            mm(out, Qg[:, hh, P * qt:P * qt + P], KVT[:, (2 + 2 * br) * KV + g, 0:nk],
                               start=True, stop=False)
                            last = mm(out[:, P * qt:P * qt + P], ident16[:], causal16[:], start=False, stop=True)
                    for qt in range(2):
                        out = WC[:, 16 * qt:16 * qt + NCMP]
                        mm(out, Qg[:, hh, P * qt:P * qt + P], KC[:, g, :], start=True, stop=False)
                        last = mm(out, ident[:], cmp_neg[:, qt, :], start=False, stop=True)
                    last.then_inc(s("sn_in_psum"), 1)
                    z_half(3 * hh, 1)
                    z_half(3 * hh + 1, 0)
                    z_half(3 * hh + 1, 1)
                    z_half(3 * hh + 2, 0)
                    pe.wait_ge(s("probs2"), n + 1)
                    for br in range(2):
                        for b in range(3):
                            nc.tensor.transpose((WA, WB)[br][:, P * b:P * b + P], Pn[:, br, b, :], ident[:])
                    for qt in range(2):
                        last = nc.tensor.transpose(WC[0:NCMP, P * qt:P * qt + P], Pc[:, qt, :], ident[:])
                    last.then_inc(s("ptn_in_psum"), 1)
                    z_half(3 * hh + 2, 1)
                    pe.wait_ge(s("ptn_ready"), n + 1)
                    pe.wait_ge(s("vg_ready"), g + 1)
                    for br in range(2):
                        w = (WA, WB)[br]
                        mm(w[:, 0:P], Vg[:, br, 0, :], PTn[:, br, 0, :], start=True, stop=True)
                        mm(w[:, P:T], Vg[:, br, 0, :], PTn[:, br, 1, :], start=True, stop=False)
                        mm(w[:, P:T], Vg[:, br, 1, :], PTn[:, br, 2, :], start=False, stop=True)
                    for qt in range(2):
                        last = mm(WC[:, P * qt:P * qt + P], VCg[0:NCMP, :], PTc[0:NCMP, qt, :], start=True, stop=True)
                    last.then_inc(s("on_in_psum"), 1)
                    if hh < HPG - 1:
                        z_half(3 * hh + 3, 0)
            for b in range(4):
                uses[b] += 16
            meet(pe, met)
            split_done("o")
            plain("w_o")
            meet(pe, met)
            norm_sums("final2")

        @block.scalar
        def _(act):
            A = nc.scalar.activation
            met = [0]

            def high(stage, i, g, pos, by_column=False, work=None, halves=(0, 1)):
                if 0 in halves:
                    loaded(act, stage, i, pos)
                for half in halves:
                    n = half_of(stage, i, g, half)
                    act.wait_ge(half_done, n + 1)
                    A(whi[:, half], half_chunk(pos, half, by_column), ACT.Copy).then_inc(s("hi_ready"), 1)
                    if work is not None:
                        work(half)

            def vec_sum(stage, i, pos, n, col, half):
                act.wait_ge(s("prod_ready"), 2 * (POOL_VEC0[stage] + POOL_VECS[stage] * i + n) + half + 1)
                w = ring[:, pos % R, 8 * half:8 * half + 8, :].rearrange("p k n -> p (k n)")
                A(w, w, ACT.Copy, accum_out=mod_ab[:, half, bass.ds(col, 1)])
                if half == 1:
                    act.drain().then_inc(slot_free[pos % R], 2)

            def norm_squares(name, src):
                n = NORMS[name]
                act.wait_ge(s("norm_src"), n + 1)
                for j in range(4):
                    A(SQ[:, 4 * j:4 * j + 4, :], src[:, 4 * j:4 * j + 4, :], ACT.Square).then_inc(s("squares_ready"), 1)

            def norm_sqrt(name):
                n = NORMS[name]
                act.wait_ge(s("var_ready"), n + 1)
                A(sd[:], var[:], ACT.Sqrt).then_inc(s("sd_ready"), 1)

            def norm_bias(call, bias):
                for k in range(KT):
                    act.wait_ge(s("scaled_ready"), KT * call + k + 1)
                    A(SQ[:, k, :], SQ[:, k, :], ACT.Identity, bias=bias[:, k:k + 1]).then_inc(s("biased"), 1)

            for name in GRANTED["act"]:
                act.sem_inc(s(name), 1)
            for b in range(4):
                act.sem_inc(bank_free[b], 1)
            act.dma_start(cond[:], a["c"].broadcast_to([P, D])).then_inc(s("cond_loaded"), 16)
            for name, dst in (("vec", vec[:]), ("w_f", w_f), ("b_f", b_f[:])):
                act.dma_start(dst, a[name]).then_inc(params, 16)
            for k in range(2):
                act.dma_start(pst[64 * k:64 * k + 64], a["step_pair"][k:k + 1, :].broadcast_to([64, PAIRS]))\
                    .then_inc(s("ssm_loaded"), 16)
            for k in range(8):
                act.dma_start(bl[16 * k:16 * k + 16], a["lam_tile"][k:k + 1].broadcast_to([16, 2, KT, 64]))\
                    .then_inc(s("ssm_loaded"), 16)
                act.dma_start(bst_[16 * k:16 * k + 16], a["step_tile"][k:k + 1, :].broadcast_to([16, KT]))\
                    .then_inc(s("ssm_loaded"), 16)
            act.dma_start(br_, a["ssm_b"]).then_inc(s("ssm_loaded"), 16)
            act.wait_ge(s("cond_loaded"), 16)
            A(cond[:], cond[:], ACT.Silu).then_inc(s("cond_ready"), 1)
            act.wait_ge(params, 48)
            act.wait_ge(x_loaded, 16)
            act.wait_ge(s("consts_ready"), 1)
            act.sem_inc(s("norm_src"), 1)
            norm_squares("mix", x)
            act.wait_ge(s("ssm_loaded"), 19 * 16)
            A(pst, pst, ACT.Exp)
            A(bst_, bst_, ACT.Exp)
            act.drain().then_inc(s("disc_a"), 1)
            norm_sqrt("mix")
            act.wait_ge(s("disc_b"), 1)
            A(e[0], e[0], ACT.Exp)
            A(mag, pe_[0], ACT.Exp)
            A(e[3], e[1], ACT.Sin, scale=TWO_PI)
            A(e[2], e[1], ACT.Abs)
            act.drain()
            A(e[2], e[2], ACT.Sin, scale=-TWO_PI, bias=cst[:, 1:2])
            act.drain().then_inc(s("disc_c"), 1)
            act.wait_ge(s("disc_done"), 1)
            act.dma_start(a["disc"], disc).then_inc(s("disc_saved"), 16)
            act.wait_ge(s("disc_saved"), 16)
            meet(act, met)
            A(lam_t[:, 0, :], V("lru_lambda"), ACT.Abs)
            act.drain()
            A(lam_t[:, 1, :], lam_t[:, 0, :], ACT.Exp, scale=-1.0)
            act.drain()
            A(lam_t[:, 2, :], lam_t[:, 1, :], ACT.Ln, bias=ones[:, 0:1]).then_inc(s("lam_ready"), 1)
            norm_bias(0, mod[:, 0:16])
            act.wait_ge(s("f_ready"), 1)
            A(fl[:, 1, :], fl[:, 0, :], ACT.Abs)
            act.drain()
            A(fl[:, 2, :], fl[:, 1, :], ACT.Exp, scale=-1.0)
            act.drain()
            A(fl[:, 3, :], fl[:, 2, :], ACT.Ln, bias=ones[0:8, 0:1]).then_inc(s("log1p_ready"), 1)
            with act.Fori(0, HEADS) as i:
                for g in range(3):
                    high("heads", i, g, g)
                high("heads", i, 3, 3, halves=(0,))
                product(act, "heads", i, 2)
                A(Qh, banks[0][:, 0:T], ACT.Copy, scale=SCALE)
                A(Kh, banks[0][:, T:2 * T], ACT.Copy).then_inc(bank_free[0], 1)
                act.drain().then_inc(s("qk_ready"), 1)
                high("heads", i, 3, 3, halves=(1,))
                act.wait_ge(s("gates_in_psum"), i + 2)
                A(rg, WC[:, 0:T], ACT.Sigmoid, bias=V("lru_b_a")[:, bass.ds(i, 1)])
                A(ig, WC[:, T:2 * T], ACT.Sigmoid, bias=V("lru_b_x")[:, bass.ds(i, 1)])
                act.drain()
                A(ut, rg, ACT.Tanh, scale=sp8[:, 0, bass.ds(i, 1)])
                A(at_, rg, ACT.Exp, scale=sp8[:, 1, bass.ds(i, 1)])
                act.drain().then_inc(s("lru_u_ready"), 1)
                high("heads", i, 4, 4, halves=(0,))
                act.wait_ge(s("negmax_ready"), i + 1)
                A(Pr[:, 0, :], WA[:, 0:P], ACT.Exp, bias=rowmax[:, 0:1], accum_out=rowsum[:, 0:1])
                A(Pr[:, 1:3, :].rearrange("p a b -> p (a b)"), WA[:, P:3 * P], ACT.Exp, bias=rowmax[:, 1:2],
                  accum_out=rowsum[:, 1:2])
                act.drain().then_inc(s("exps_ready"), 1)
                product(act, "heads", i, 3)
                A(VTh, banks[1][:, 0:T], ACT.Copy)
                act.drain().then_inc(s("vt_ready"), 1)
                high("heads", i, 4, 4, halves=(1,))
                act.wait_ge(s("vrows_in_psum"), i + 1)
                A(Vr.rearrange("p a b -> p (a b)"), banks[1][:, T:2 * T], ACT.Copy).then_inc(s("vrows_ready"), 1)
                act.drain().then_inc(bank_free[1], 1)
                act.wait_ge(s("pt_in_psum"), i + 1)
                A(PT.rearrange("p a b -> p (a b)"), WB[:, 0:3 * P], ACT.Copy).then_inc(s("pt_ready"), 1)
                act.wait_ge(s("lru_t_ready"), i + 1)
                A(t2, t1, ACT.Sqrt, scale=2.0).then_inc(s("lru_sq_ready"), 1)
                product(act, "heads", i, 4)
                act.wait_ge(s("lru_done"), i + 1)
                A(LY, banks[3][:, 0:T], ACT.Gelu_apprx_tanh).then_inc(bank_free[3], 1)
                act.drain().then_inc(s("ly_ready"), 1)
                act.wait_ge(s("attn_in_psum"), i + 1)
                A(M[:, bass.ds(i, 1), :], WA[:, 0:T], ACT.Copy).then_inc(s("attn_ready"), 1)
            meet(act, met)
            act.sem_inc(s("norm_src"), 1)
            norm_squares("merged", M)
            norm_sqrt("merged")
            with act.Fori(0, 2) as i:
                for g in range(8):
                    high("w_out", i, g, 5 * (g // 2) + 2 * (g % 2))
            meet(act, met)
            act.sem_inc(s("norm_src"), 1)
            act.dma_start(k12, a["k12"]).then_inc(s("k_loaded"), 16)
            norm_squares("ffn", x)
            norm_sqrt("ffn")
            norm_bias(1, mod[:, 48:64])
            with act.Fori(0, 4) as i:
                for h in range(2):
                    n = 2 * i + h
                    for half in range(2):
                        high("topk", i, 2 * h + half, 4 * h + half)
                    act.wait_ge(s("s_in_psum"), n + 1)
                    for half in range(2):
                        product(act, "topk", i, 2 * h + half)
                        A(Qp[:, half, :], banks[half][:, 0:T], ACT.Copy).then_inc(bank_free[half], 1)
                    act.drain().then_inc(s("peerq_ready"), 1)
                    for k in range(2):
                        for half in range(2):
                            vec_sum("topk", i, 4 * h + 2 + k, 2 * h + k, 80 + 4 * i + 2 * h + k, half)
            act.wait_ge(s("vs_ready"), 1)
            A(picked[:, 2], picked[:, 2], ACT.Exp).then_inc(s("vs_exp"), 1)
            act.wait_ge(s("cols_in_psum"), 1)
            for w in range(3):
                A((cols[:, 0, :], cols[:, 1, :], weight)[w], (WA, WB, WC)[w][:, 0:T], ACT.Copy)
            meet(act, met)
            act.dma_start(cond[:], a["c2"].broadcast_to([P, D])).then_inc(s("cond_loaded"), 16)
            act.sem_inc(s("wd_copied"), 2)
            act.wait_ge(s("cond_loaded"), 32)
            A(cond[:], cond[:], ACT.Silu).then_inc(s("cond_ready"), 1)

            def copy_unit(unit, bank, buf, tok):
                act.wait_ge(s("hot_used"), 2 * unit + 4)
                A(Wd[:, buf, :, bass.ds(tok, 16)],
                  bank[:].rearrange("p (t i) -> p i t", i=QW), ACT.Copy).then_inc(s("wd_copied"), 1)

            with act.Fori(0, 4) as i:
                for u in range(4):
                    copy_unit(4 * i + u, (WB, WC)[u % 2], 0, 64 * i + 16 * u)
            with act.Fori(0, 2) as o:
                for par in range(2):
                    act.wait_ge(s("g_ready"), 64 * o + 32 * par + 1)
                    with act.Fori(0, 4) as q:
                        g = 8 * o + 4 * par + q

                        def hidden(n):
                            product(act, "peer", g, n)
                            act.wait_ge(s("gelu_free"), 8 * g + n + 1)
                            A(GL[:, n % 2, :], banks[n % 4][:, 0:T], ACT.Gelu_apprx_tanh).then_inc(bank_free[n % 4], 1)
                            act.drain().then_inc(s("gelu_ready"), 1)

                        for c in range(16):
                            def work(half):
                                if c == 8 and half == 0:
                                    hidden(7)
                                if c % 4 == 2:
                                    n = c // 2 - 1
                                    vec_sum("peer", g, 3 * n + 2, c // 4, 96 + 8 * g + n, half)

                            high("peer", g, c, 12 * (c // 8) + 3 * (c % 8 // 2) + c % 2, c >= 8, work)
                            if 0 < c < 8:
                                hidden(c - 1)
                            if c % 4 == 3:
                                copy_unit(4 * g + 16 + c // 4, (WB, WC)[c // 4 % 2], 1 - par, 64 * q + 16 * (c // 4))
            meet(act, met)
            act.dma_start(disc, a["disc"]).then_inc(s("disc_loaded"), 16)
            act.dma_start(CC, a["ssm_c"]).then_inc(s("disc_loaded"), 16)
            act.sem_inc(s("norm_src"), 1)
            norm_squares("final", x)
            norm_sqrt("final")
            norm_squares("l0", x)
            norm_sqrt("l0")
            norm_bias(2, mod[:, 96:112])
            act.wait_ge(s("disc_loaded"), 32)
            meet(act, met)

            def table(duo, col, n, free):
                for k in range(2):
                    A(ph[:, k, :], iota_t[:], ACT.Copy, scale=theta[:, bass.ds(col + k, 1)])
                act.drain()
                A(rn[:], ph[:], ACT.Copy, bias=MAGIC)
                act.drain()
                A(rn[:], rn[:], ACT.Copy, bias=-MAGIC).then_inc(s("phase_ready"), 1)
                act.wait_ge(s("frac_ready"), n + 1)
                if free is not None:
                    act.wait_ge(s("q_ready"), free)
                A(tab[:, duo, 1], ph[:], ACT.Sin, scale=TWO_PI)
                A(rn[:], ph[:], ACT.Abs)
                act.drain()
                A(tab[:, duo, 0], rn[:], ACT.Sin, scale=-TWO_PI, bias=cst[:, 1:2])
                act.drain().then_inc(s("table_ready"), 1)

            def u_out(i, t):
                product(act, "ssm", i, 2 * t)
                act.wait_ge(s("y_read"), 2 * i + t + 1)
                A(Us[:, t % 2, :], banks[2 * t % 4][:, 0:T], ACT.Copy).then_inc(bank_free[2 * t % 4], 1)
                act.drain().then_inc(s("u_ready"), 1)

            def ssm_tile(i, t, last=False):
                tile = 2 * i + t
                if not last:
                    high("ssm", i, 2 * t + 2, 2 * t + 2)
                product(act, "ssm", i, 2 * t + 1)
                b = (2 * t + 1) % 4
                A(SZ[:, bass.ds(tile, 1), :], banks[b][:, 0:T], ACT.Silu).then_inc(bank_free[b], 1)
                if not last:
                    table(0, 4 * tile + 4, 2 * tile + 2, 4 + 4 * tile + 2)
                    u_out(i, t + 1)
                    high("ssm", i, 2 * t + 3, 2 * t + 3)
                    table(1, 4 * tile + 6, 2 * tile + 3, 4 + 4 * tile + 4)

            high("ssm", 0, 0, 0)
            for duo in range(2):
                table(duo, 2 * duo, duo, None)
            u_out(0, 0)
            high("ssm", 0, 1, 1)
            ssm_tile(0, 0)
            with act.Fori(0, 7) as i:
                for t in (1, 2):
                    ssm_tile(i, t)
            ssm_tile(7, 1, last=True)
            act.wait_ge(s("y_read"), KT + 2)
            for j in range(4):
                A(Y[:, 4 * j:4 * j + 4, :], Y[:, 4 * j:4 * j + 4, :], ACT.Gelu_apprx_tanh).then_inc(s("y_gelu"), 1)
            with act.Fori(0, 2) as i:
                for g in range(9):
                    if g < 8:
                        high("glu", i, g, g)
                    if g > 0:
                        m = 8 * i + g - 1
                        product(act, "glu", i, g - 1)
                        act.wait_ge(s("glu_free"), m + 1)
                        A(glt[:, (g - 1) % 2, :], banks[(g - 1) % 4][:, 0:T], ACT.Sigmoid,
                          bias=V("b_glu")[:, bass.ds(m, 1)]).then_inc(bank_free[(g - 1) % 4], 1)
                        act.drain().then_inc(s("sig_ready"), 1)
            with act.Fori(0, 2) as i:
                for g in range(8):
                    high("ssm_out", i, g, g)
            meet(act, met)
            for dst, name in ((W1, "cmp_w1"), (W2, "cmp_w2"), (wg, "w_gate")):
                act.dma_start(dst, a[name][:, 0] if name == "cmp_w1" else a[name]).then_inc(s("w1_loaded"), 16)
            act.sem_inc(s("norm_src"), 1)
            norm_squares("l1", x)
            norm_sqrt("l1")
            norm_bias(3, mod[:, 192:208])
            with act.Fori(0, 3) as i:
                for g in range(9):
                    if g < 8:
                        high("kv", i, g, g)
                    if g > 0:
                        product(act, "kv", i, g - 1)
                        A(KVT[:, bass.ds(8 * i + g - 1, 1), :], banks[(g - 1) % 4][:, 0:T], ACT.Copy)\
                            .then_inc(bank_free[(g - 1) % 4], 1)
                        act.drain().then_inc(s("kv_ready"), 1)
            for g in range(KV):
                act.wait_ge(s("vr_in_psum"), g + 1)
                A(VR[:, g].rearrange("p a b c -> p (a b c)"), (WA, WB)[g % 2][:], ACT.Copy).then_inc(s("vr_ready"), 1)
            act.wait_ge(s("w1b_used"), 1)
            act.dma_start(W1, a["cmp_w1"][:, 1]).then_inc(s("w1_loaded"), 16)
            for b in range(2):
                act.wait_ge(s("b1e_ready"), 1)
                A(GC, WC[:, 64 * b:64 * b + KV * NCMP], ACT.Gelu_apprx_tanh, bias=b1e[:, b:b + 1])\
                    .then_inc(s("cmp_gelu"), 1)
                act.wait_ge(s("cmp2_in_psum"), b + 1)
                A((KC, VCt)[b].rearrange("p a b -> p (a b)"), WC[:, 192 + 64 * b:192 + 64 * b + KV * NCMP],
                  ACT.Identity, bias=V("cmp_b2")[:, b:b + 1])
                act.drain().then_inc(s("kc_ready"), 1)
            act.wait_ge(s("vc_in_psum"), 1)
            A(VCr[0:NCMP].rearrange("p a b -> p (a b)"), WA[0:NCMP, :], ACT.Copy)
            norm_bias(4, mod[:, 144:160])
            act.wait_ge(s("gt_in_psum"), 1)
            A(GT, WB[:, 0:128].rearrange("p (a b) -> p a b", a=2)[:, :, 0:48], ACT.Sigmoid)
            meet(act, met)
            with act.Fori(0, KV) as g:
                def q_out(hh):
                    product(act, "nsa", g, hh)
                    A(Qg[:, hh, :], banks[hh][:, 0:T], ACT.Copy, scale=SCALE).then_inc(bank_free[hh], 1)
                    act.drain().then_inc(s("q_ready2"), 1)

                def z_silu(hh, br):
                    c = 4 + 3 * hh + br
                    product(act, "nsa", g, c)
                    A(SZn[:, hh % 2, br, :], banks[c % 4][:, 0:T], ACT.Silu).then_inc(bank_free[c % 4], 1)
                    act.drain().then_inc(s("sz_ready"), 1)

                high("nsa", g, 0, 0)
                for hh in range(1, HPG):
                    high("nsa", g, hh, hh)
                    q_out(hh - 1)
                def z_high(z, half):
                    high("nsa", g, 4 + z, 4 + z, halves=(half,))

                z_high(0, 0)
                q_out(HPG - 1)
                z_high(0, 1)
                for hh in range(HPG):
                    n = 4 * g + hh
                    z_high(3 * hh + 1, 0)
                    act.wait_ge(s("negmax2"), n + 1)
                    for br in range(2):
                        w = (WA, WB)[br]
                        A(Pn[:, br, 0, :], w[:, 0:P], ACT.Exp, bias=mx[:, 2 * br:2 * br + 1],
                          accum_out=sm[:, 2 * br:2 * br + 1])
                        A(Pn[:, br, 1:3, :].rearrange("p a b -> p (a b)"), w[:, P:3 * P], ACT.Exp,
                          bias=mx[:, 2 * br + 1:2 * br + 2], accum_out=sm[:, 2 * br + 1:2 * br + 2])
                    for qt in range(2):
                        A(Pc[:, qt, :], WC[:, 16 * qt:16 * qt + NCMP], ACT.Exp, bias=mx[:, 4 + qt:5 + qt],
                          accum_out=sm[:, 4 + qt:5 + qt])
                    act.drain().then_inc(s("exps2"), 1)
                    z_high(3 * hh + 1, 1)
                    z_silu(hh, 0)
                    z_high(3 * hh + 2, 0)
                    z_high(3 * hh + 2, 1)
                    z_silu(hh, 1)
                    act.wait_ge(s("ptn_in_psum"), n + 1)
                    for br in range(2):
                        A(PTn[:, br].rearrange("p a b -> p (a b)"), (WA, WB)[br][:, 0:3 * P], ACT.Copy)
                    A(PTc[0:NCMP].rearrange("p a b -> p (a b)"), WC[0:NCMP, 0:T], ACT.Copy)
                    act.drain().then_inc(s("ptn_ready"), 1)
                    if hh < HPG - 1:
                        z_high(3 * hh + 3, 0)
                    z_silu(hh, 2)
                    if hh < HPG - 1:
                        z_high(3 * hh + 3, 1)
            meet(act, met)
            with act.Fori(0, 2) as i:
                for g in range(8):
                    high("w_o", i, g, g)
            meet(act, met)
            act.sem_inc(s("norm_src"), 1)
            norm_squares("final2", x)
            norm_sqrt("final2")

        @block.vector
        def _(dve):
            v = nc.vector
            met = [0]

            def low(stage, i, g, pos, by_column=False, work=None, tiles=DVE_K, halves=(0, 1)):
                for half in halves:
                    n = half_of(stage, i, g, half)
                    dve.wait_ge(s("hi_ready"), n + 1)
                    v.tensor_tensor(wlo[:, half, 0:tiles], half_chunk(pos, half, by_column)[:, 0:tiles],
                                    whi[:, half, 0:tiles].bitcast(F32), ALU.subtract).then_inc(s("lo_dve"), 1)
                    if tiles == 8:
                        dve.drain().then_inc(s("lo_pool"), 1)
                    if half == 1:
                        dve.drain().then_inc(slot_free[pos % R], 2 if tiles == 8 else 1)
                    if work is not None:
                        work(half)

            def vec_sum(stage, i, pos, col, half):
                if half == 0:
                    loaded(dve, stage, i, pos)
                w = ring[:, pos % R, 8 * half:8 * half + 8, :].rearrange("p k n -> p (k n)")
                v.tensor_tensor_reduce(w, w, cond[:, D // 2 * half:D // 2 * half + D // 2], 1.0, 0.0, ALU.mult, ALU.add,
                                       accum_out=sums[:, pos % R, half:half + 1])
                if half == 1:
                    dve.drain().then_inc(slot_free[pos % R], 2)
                    v.tensor_copy(mod_ab[:, :, bass.ds(col, 1)], sums[:, pos % R, :].unsqueeze(2))

            def whole_vec(stage, i, pos, col):
                for half in range(2):
                    vec_sum(stage, i, pos, col, half)

            def split(name, src, waits=None):
                for j in range(4):
                    if waits is not None:
                        dve.wait_ge(s(waits[0]), waits[1] + (j + 1) * waits[2])
                    v.tensor_copy(Hhi[:, 4 * j:4 * j + 4, :], src[:, 4 * j:4 * j + 4, :]).then_inc(s("hhi_ready"), 1)
                    if j >= 2:
                        dve.drain()
                        v.tensor_tensor(Hlo[:, 4 * j:4 * j + 4, :], src[:, 4 * j:4 * j + 4, :],
                                        Hhi[:, 4 * j:4 * j + 4, :].bitcast(F32), ALU.subtract)\
                            .then_inc(s("h_ready"), 1)

            def norm_rstd(name, width):
                n = NORMS[name]
                groups = 2 if name == "merged" else 1
                dve.wait_ge(s("sums_ready"), n + 1)
                v.tensor_scalar(var[:, 0:groups], WA[:, 0:groups * T].rearrange("p (a b) -> p a b", b=T),
                                1.0 / width, EPS, ALU.mult, ALU.add)
                if groups == 1:
                    v.tensor_scalar(var[:, 1], WA[:, 0:T], 1.0 / width, EPS, ALU.mult, ALU.add)
                dve.drain().then_inc(s("var_ready"), 1)
                dve.wait_ge(s("sd_ready"), n + 1)
                v.reciprocal(rstd[:], sd[:])
                dve.drain()

            def norm_scale(dst, src, g, signal=None):
                for k in range(KT):
                    ins = v.scalar_tensor_tensor(dst[:, k, :], src[:, k, :], g[:, k:k + 1], rstd[:, k // 8, :],
                                                 ALU.mult, ALU.mult)
                    if signal:
                        ins.then_inc(s(signal), 1)
                dve.drain()

            def modulated_gain(n, g, scale):
                v.tensor_scalar(gain[:, n, :], scale, 1.0, None, ALU.add)
                dve.drain()
                v.tensor_tensor(gain[:, n, :], gain[:, n, :], g, ALU.mult)
                dve.drain()

            def take_mod(lo, hi):
                dve.drain()
                v.tensor_tensor(mod[:, lo:hi], mod[:, lo:hi], mod_ab[:, 1, lo:hi], ALU.add)
                dve.drain()
                v.tensor_tensor(mod[:, lo:hi], mod[:, lo:hi],
                                vec[:, VOFF["b_ada"] + lo:VOFF["b_ada"] + hi], ALU.add)
                dve.drain()

            def residual(stage, i, g, gate):
                product(dve, stage, i, g)
                m = 8 * i + g
                v.scalar_tensor_tensor(x[:, bass.ds(m, 1), :], banks[g % 4][:, 0:T], gate[:, bass.ds(m, 1)],
                                       x[:, bass.ds(m, 1), :], ALU.mult, ALU.add).then_inc(bank_free[g % 4], 1)

            def plain_residual(stage, gate):
                with dve.Fori(0, 2) as i:
                    for g in range(9):
                        if g < 8:
                            low(stage, i, g, g)
                        if g > 0:
                            residual(stage, i, g - 1, gate)

            for name in GRANTED["dve"]:
                dve.sem_inc(s(name), 1)
            v.memset(cst[:, 0:1], -MAGIC)
            v.memset(cst[:, 1:2], HALF_PI)
            norm_rstd("mix", D)
            dve.wait_ge(s("disc_e"), 1)
            v.reciprocal(e[4], e[4]).then_inc(s("disc_f"), 1)
            dve.wait_ge(s("cond_ready"), 1)
            with dve.Fori(0, 8) as i:
                for pos in range(4):
                    whole_vec("shift_scale", i, pos, 4 * i + pos)
            take_mod(0, 32)
            modulated_gain(0, V("g_mix"), mod[:, 16:32])
            meet(dve, met)
            norm_scale(SQ, x, gain[:, 0, :], "scaled_ready")
            split("mix", SQ, ("biased", 0, 4))
            v.memset(LX[:, 0:3], 0.0)
            v.tensor_scalar(sp8[:, 0, :], V("lru_lambda"), -1.0, 0.0, ALU.mult, ALU.max)
            dve.wait_ge(s("lam_ready"), 1)
            dve.drain()
            v.tensor_tensor(sp8[:, 0, :], sp8[:, 0, :], lam_t[:, 2, :], ALU.add)
            dve.drain()
            v.tensor_scalar(sp8[:, 0, :], sp8[:, 0, :], LRU_C, None, ALU.mult)
            dve.drain()
            v.tensor_scalar(sp8[:, 1, :], sp8[:, 0, :], -1.0, None, ALU.mult)
            dve.wait_ge(s("f_in_psum"), 1)
            v.tensor_scalar(fl[:, 0, :], WB[0:8, 0:T], b_f[:, 0:1], None, ALU.add).then_inc(s("f_ready"), 1)
            dve.drain()
            v.tensor_scalar(fl[:, 4, :], fl[:, 0, :], 0.0, None, ALU.min)
            dve.wait_ge(s("log1p_ready"), 1)
            dve.drain()
            v.tensor_tensor(fl[:, 4, :], fl[:, 4, :], fl[:, 3, :], ALU.subtract)
            dve.drain()
            v.tensor_tensor_scan(fl[:, 5, :], ones[0:8, :], fl[:, 4, :], 0.0, ALU.mult, ALU.add)
            dve.drain().then_inc(s("cum_ready"), 1)
            conv_w = V("conv_w").rearrange("p (a b) -> p a b", b=4)
            with dve.Fori(0, HEADS) as i:
                v.tensor_scalar(cm[:, 0, :], fl[:, 5, :], ident[0:8, bass.ds(i, 1)], None, ALU.mult)
                dve.drain()
                v.tensor_scalar(cm[:, 1, :], cm[:, 0, :], -1.0, None, ALU.mult).then_inc(s("cm_ready"), 1)
                low("heads", i, 0, 0)
                low("heads", i, 1, 1, halves=(0,))
                product(dve, "heads", i, 0)
                v.tensor_copy(LX[:, 3:3 + T], banks[2][:, 0:T]).then_inc(bank_free[2], 1)
                dve.drain()
                v.tensor_scalar(xc, LX[:, 0:T], conv_w[:, bass.ds(i, 1), 0], V("conv_b")[:, bass.ds(i, 1)],
                                ALU.mult, ALU.add)
                for w in range(1, 4):
                    dve.drain()
                    v.scalar_tensor_tensor(xc, LX[:, w:w + T], conv_w[:, bass.ds(i, 1), w], xc, ALU.mult, ALU.add)
                dve.drain().then_inc(s("xc_ready"), 1)
                low("heads", i, 1, 1, halves=(1,))
                low("heads", i, 2, 2)
                whole_vec("heads", i, 5, 32 + 3 * i)
                low("heads", i, 3, 3, halves=(0,))
                dve.wait_ge(s("scores_ready"), i + 1)
                v.tensor_reduce(rowmax[:, 0:1], WA[:, 0:P], AX, ALU.max)
                v.tensor_reduce(rowmax[:, 1:2], WA[:, P:3 * P], AX, ALU.max)
                dve.drain()
                v.tensor_scalar(rowmax, rowmax, -1.0, None, ALU.mult).then_inc(s("negmax_ready"), 1)
                low("heads", i, 3, 3, halves=(1,))
                dve.wait_ge(s("lru_u_ready"), i + 2)
                v.tensor_tensor(gx, ig, xc, ALU.mult)
                v.tensor_scalar(t1, ut, 1.0, None, ALU.add)
                dve.drain()
                v.reciprocal(t1, t1)
                dve.drain()
                v.tensor_tensor(t1, t1, ut, ALU.mult).then_inc(s("lru_t_ready"), 1)
                low("heads", i, 4, 4, halves=(0,))
                dve.wait_ge(s("exps_ready"), i + 1)
                v.reciprocal(rowrec, rowsum)
                dve.drain()
                v.tensor_scalar(Pr[:, 0, :], Pr[:, 0, :], rowrec[:, 0:1], None, ALU.mult)
                v.tensor_scalar(Pr[:, 1:3, :], Pr[:, 1:3, :], rowrec[:, 1:2], None, ALU.mult)
                dve.drain().then_inc(s("probs_ready"), 1)
                low("heads", i, 4, 4, halves=(1,))
                whole_vec("heads", i, 6, 33 + 3 * i)
                dve.wait_ge(s("lru_sq_ready"), i + 1)
                v.tensor_tensor(gx, gx, t2, ALU.mult)
                dve.drain()
                v.tensor_tensor_scan(t1, at_, gx, 0.0, ALU.mult, ALU.add)
                dve.drain()
                dve.wait_ge(s("ly_ready"), i + 1)
                v.tensor_tensor(M[:, bass.ds(HEADS + i, 1), :], t1, LY, ALU.mult).then_inc(s("lru_done"), 1)
                whole_vec("heads", i, 7, 34 + 3 * i)
            meet(dve, met)
            take_mod(32, 56)
            norm_rstd("merged", D // 2)
            norm_scale(SQ, M, V("g_merge"))
            split("merged", SQ)
            with dve.Fori(0, 2) as i:
                for g in range(8):
                    m = g // 2
                    low("w_out", i, g, 5 * m + 2 * (g % 2))
                    if g > 0:
                        residual("w_out", i, g - 1, mod[:, 32:48])
                    if g % 2 == 0:
                        whole_vec("w_out", i, 5 * m + 1, 56 + 12 * i + 3 * m)
                    else:
                        whole_vec("w_out", i, 5 * m + 3, 57 + 12 * i + 3 * m)
                        whole_vec("w_out", i, 5 * m + 4, 58 + 12 * i + 3 * m)
                residual("w_out", i, 7, mod[:, 32:48])
            meet(dve, met)
            take_mod(56, 80)
            modulated_gain(1, V("g_ffn"), mod[:, 64:80])
            norm_rstd("ffn", D)
            norm_scale(SQ, x, gain[:, 1, :], "scaled_ready")
            split("ffn", SQ, ("biased", KT, 4))

            def top16(vals, idx, src):
                v.max(vals[:, 0:8], src)
                dve.drain()
                v.max_index(idx[:, 0:8], vals[:, 0:8], src)
                dve.drain()
                v.match_replace(src, vals[:, 0:8], src, LOW)
                dve.drain()
                v.max(vals[:, 8:16], src)
                dve.drain()
                v.max_index(idx[:, 8:16], vals[:, 8:16], src)

            iota_k = iota_t[:, 0:TOPK].unsqueeze(1).broadcast_to([P, TOPK, TOPK])
            with dve.Fori(0, HEADS) as i:
                dve.wait_ge(s("s_in_psum"), i + 2)
                v.tensor_copy(S4.rearrange("p a b -> p (a b)"), WA[:]).then_inc(s("s_ready"), 1)
                dve.drain()
                for tt in range(2):
                    top16(v1f, i1u, S4[:, 2 * tt, :])
                    top16(v2f, i2u, S4[:, 2 * tt + 1, :])
                    dve.drain()
                    v.tensor_copy(i1f, i1u)
                    v.tensor_copy(i2f, i2u)
                    v.tensor_tensor(cand, v1f.unsqueeze(2).broadcast_to([P, TOPK, TOPK]),
                                    v2f.unsqueeze(1).broadcast_to([P, TOPK, TOPK]), ALU.add)
                    dve.drain()
                    top16(vs, ic, cand.rearrange("p a b -> p (a b)"))
                    dve.drain()
                    v.tensor_scalar(ich, ic, 4, None, ALU.logical_shift_right)
                    v.tensor_scalar(icl, ic, 15, None, ALU.bitwise_and)
                    dve.drain()
                    v.tensor_copy(chf, ich)
                    v.tensor_copy(clf, icl)
                    dve.drain()
                    for cf, hot, idx in ((chf, hot1, i1f), (clf, hot2, i2f)):
                        v.tensor_tensor(hot, cf.unsqueeze(2).broadcast_to([P, TOPK, TOPK]), iota_k, ALU.is_equal)
                    dve.drain()
                    for cf, hot, idx in ((chf, hot1, i1f), (clf, hot2, i2f)):
                        v.tensor_tensor(hot, hot, idx.unsqueeze(1).broadcast_to([P, TOPK, TOPK]), ALU.mult)
                    dve.drain()
                    for w, hot in enumerate((hot1, hot2)):
                        v.tensor_reduce(picked[:, w, tt, bass.ds(i, 1), :].rearrange("p a b -> p (a b)"), hot, AX, ALU.add)
                    v.tensor_copy(picked[:, 2, tt, bass.ds(i, 1), :].rearrange("p a b -> p (a b)"), vs)
                    dve.drain()
            v.tensor_copy(pmax, picked[:, 2, :, :, 0])
            dve.drain()
            for tt in range(2):
                v.tensor_tensor(picked[:, 2, tt], picked[:, 2, tt],
                                pmax[:, tt].unsqueeze(2).broadcast_to([P, HEADS, TOPK]), ALU.subtract)
            dve.drain().then_inc(s("vs_ready"), 1)
            dve.wait_ge(s("vs_exp"), 1)
            v.tensor_reduce(psum_, picked[:, 2], AX, ALU.add)
            dve.drain()
            v.reciprocal(prec, psum_)
            dve.drain()
            for tt in range(2):
                v.tensor_tensor(picked[:, 2, tt], picked[:, 2, tt],
                                prec[:, tt].unsqueeze(2).broadcast_to([P, HEADS, TOPK]), ALU.mult)
            dve.drain().then_inc(s("picked_ready"), 1)
            meet(dve, met)
            take_mod(80, 96)
            dve.wait_ge(s("cond_ready"), 2)
            whole = var[:, 1]
            for k in range(3):
                v.tensor_copy(parts[:, k, :], weight)
                dve.drain()
                if k < 2:
                    v.tensor_copy(whole, parts[:, k, :])
                    dve.drain()
                    v.tensor_tensor(weight, weight, whole, ALU.subtract)
                    dve.drain()

            def first_hots(unit, h, tok):
                dve.wait_ge(s("hot_used"), 2 * unit + h + 1)
                for j in range(8):
                    v.tensor_scalar(hotA[h][:, j, :], iota16b[:], cols[:, 0, bass.ds(tok + j, 1)], None, ALU.is_equal)

            def equal_second(h, tok):
                v.tensor_tensor(eqB[h], iota_t[:, 0:QW].unsqueeze(1).broadcast_to([P, 8, QW]),
                                cols[:, 1, bass.ds(tok, 8)].unsqueeze(2).broadcast_to([P, 8, QW]), ALU.is_equal)

            def second_hots(unit, h, tok):
                equal_second(h, tok)
                dve.drain()
                for k in range(3):
                    v.tensor_tensor(hotB[:, h, :, k, :], eqB[h],
                                    parts[:, k, bass.ds(tok, 8)].unsqueeze(2).broadcast_to([P, 8, QW]), ALU.mult)
                dve.drain().then_inc(s("hot_ready"), 1)

            with dve.Fori(0, 4) as i:
                for u in range(4):
                    for h in range(2):
                        first_hots(4 * i + u, h, 64 * i + 16 * u + 8 * h)
                        equal_second(h, 64 * i + 16 * u + 8 * h)
                        dve.drain().then_inc(s("hot_equal"), 1)
            with dve.Fori(0, 2) as o:
                for par in range(2):
                    dve.wait_ge(s("wd_copied"), 2 + 16 + 32 * o + 16 * par)
                    v.tensor_scalar(cols[:, 1, :], cols[:, 1, :], float(QW), None, ALU.subtract)
                    dve.drain()
                    with dve.Fori(0, 4) as q:
                        g = 8 * o + 4 * par + q

                        def weigh(n):
                            b = GL[:, n % 2, :]
                            dve.wait_ge(s("gelu_ready"), 8 * g + n + 1)
                            v.tensor_tensor(b, b, Wd[:, par, bass.ds(8 * q + n, 1), :], ALU.mult)
                            dve.drain()
                            v.tensor_copy(Ghi[:, n, :], b)
                            dve.drain()
                            v.tensor_tensor(Glo[:, n, :], b, Ghi[:, n, :].bitcast(F32), ALU.subtract)\
                                .then_inc(s("g_ready"), 1)
                            dve.drain().then_inc(s("gelu_free"), 1)

                        def result(n):
                            product(dve, "peer", g, 8 + n)
                            for dd in range(2):
                                m = 2 * n + dd
                                last = v.scalar_tensor_tensor(x[:, m, :], banks[n % 4][:, T * dd:T * dd + T],
                                                              mod[:, 80 + m:81 + m], x[:, m, :], ALU.mult, ALU.add)
                            last.then_inc(bank_free[n % 4], 1)

                        for c in range(16):
                            def work(half):
                                if c % 4 < 2:
                                    u = 2 * (c // 4) + c % 4
                                    (first_hots, second_hots)[half](4 * g + 16 + u // 2, u % 2, 64 * q + 8 * u)
                                if c % 4 == 3:
                                    n = c // 2
                                    vec_sum("peer", g, 3 * n + 2, 96 + 8 * g + n, half)
                                if half == 0 and 2 <= c <= 8:
                                    weigh(c - 2)
                                if half == 0 and c == 8:
                                    weigh(7)
                                if half == 1 and c > 8:
                                    result(c - 9)

                            low("peer", g, c, 12 * (c // 8) + 3 * (c % 8 // 2) + c % 2, c >= 8, work)
                        result(7)
            meet(dve, met)
            take_mod(96, 224)
            norm_rstd("final", D)
            norm_scale(x, x, V("g_final"))
            dve.drain().then_inc(s("norm_src"), 1)
            modulated_gain(2, V("g_l0"), mod[:, 112:128])
            norm_rstd("l0", D)
            norm_scale(SQ, x, gain[:, 2, :], "scaled_ready")
            split("l0", SQ, ("biased", 2 * KT, 4))
            meet(dve, met)
            def fraction(n):
                dve.wait_ge(s("phase_ready"), n + 1)
                v.tensor_tensor(ph[:], ph[:], rn[:], ALU.subtract)
                dve.drain().then_inc(s("frac_ready"), 1)

            def y_out(i, t):
                tile = 2 * i + t
                dve.wait_ge(s("y_pair"), 4 * tile + 9)
                v.scalar_tensor_tensor(Y[:, bass.ds(tile, 1), :], Us[:, t % 2, :], V("ssm_d")[:, bass.ds(tile, 1)],
                                       WC[:, 0:T], ALU.mult, ALU.add)
                dve.drain().then_inc(s("y_read"), 1)

            def ssm_tile(i, t, first=False, last=False):
                tile = 2 * i + t
                for j in range(4):
                    duo, k = j // 2, j % 2
                    bu = (WA, WB)[j % 2][:].rearrange("p (a b) -> p a b", a=2)
                    dve.wait_ge(s("table_ready"), 2 * tile + duo + 1)
                    dve.wait_ge(s("bu_in_psum"), 4 * tile + j + 1)
                    v.tensor_tensor(P1, bu, tab[:, duo, 0, k:k + 1, :].broadcast_to([P, 2, T]), ALU.mult)
                    v.tensor_tensor(P2, bu, tab[:, duo, 1, k:k + 1, :].broadcast_to([P, 2, T]), ALU.mult)
                    dve.drain().then_inc(s("bu_read"), 1)
                    v.tensor_tensor(Wr[:, 0, :], P1[:, 0, :], P2[:, 1, :], ALU.add)
                    v.tensor_tensor(Wr[:, 1, :], P1[:, 1, :], P2[:, 0, :], ALU.subtract)
                    dve.drain()
                    dve.wait_ge(s("q_ready"), 4 + 4 * tile + j - 1)
                    m = mag[:, bass.ds(4 * tile + j, 1)].broadcast_to([P, T])
                    for ri in range(2):
                        v.tensor_tensor_scan(Z[:, j % 2, ri, :], m, Wr[:, ri, :], 0.0, ALU.mult, ALU.add)
                    dve.drain().then_inc(s("z_ready"), 1)
                    if j == 0 and not first:
                        y_out(i, t - 1)
                    if j in (1, 2) and not last:
                        low("ssm", i, 2 * t + 2, 2 * t + 2, tiles=8, halves=(j - 1,))
                    if j == 2 and not last:
                        fraction(2 * tile + 2)
                if not last:
                    low("ssm", i, 2 * t + 3, 2 * t + 3, tiles=8)
                    fraction(2 * tile + 3)

            low("ssm", 0, 0, 0, tiles=8)
            fraction(0)
            fraction(1)
            low("ssm", 0, 1, 1, tiles=8)
            ssm_tile(0, 0, first=True)
            with dve.Fori(0, 7) as i:
                for t in (1, 2):
                    ssm_tile(i, t)
            ssm_tile(7, 1, last=True)
            y_out(7, 1)
            split("y", Y, ("y_gelu", 0, 1))
            dve.sem_inc(s("glu_free"), 2)
            with dve.Fori(0, 2) as i:
                for g in range(9):
                    if g < 8:
                        low("glu", i, g, g)
                    if g > 0:
                        m = 8 * i + g - 1
                        dve.wait_ge(s("sig_ready"), m + 1)
                        v.tensor_tensor(Y[:, bass.ds(m, 1), :], glt[:, (g - 1) % 2, :], Y[:, bass.ds(m, 1), :], ALU.mult)
                        dve.drain().then_inc(s("glu_free"), 1)
                        v.tensor_tensor(SZ[:, bass.ds(m, 1), :], Y[:, bass.ds(m, 1), :], SZ[:, bass.ds(m, 1), :], ALU.mult)
            dve.drain()
            product(dve, "glu", 1, 7)
            split("glu", SZ)
            plain_residual("ssm_out", mod[:, 128:144])
            meet(dve, met)
            modulated_gain(3, V("g_kv"), mod[:, 208:224])
            modulated_gain(4, V("g_l1"), mod[:, 160:176])
            norm_rstd("l1", D)
            norm_scale(SQ, x, gain[:, 3, :], "scaled_ready")
            split("kv", SQ, ("biased", 3 * KT, 4))
            with dve.Fori(0, 3) as i:
                for g in range(8):
                    low("kv", i, g, g)
            dve.wait_ge(s("w1b_used"), 2)
            v.tensor_tensor(b1e, WC[:, 128:130], V("cmp_b1"), ALU.add).then_inc(s("b1e_ready"), 1)
            norm_scale(SQ, x, gain[:, 4, :], "scaled_ready")
            split("l1", SQ, ("biased", 4 * KT, 4))
            meet(dve, met)
            gates = GT.rearrange("p t (b n) -> p t b n", b=3)
            with dve.Fori(0, KV) as g:
                for hh in range(HPG):
                    low("nsa", g, hh, hh)

                def z_low(z, half):
                    low("nsa", g, 4 + z, 4 + z, halves=(half,))

                z_low(0, 0)
                z_low(0, 1)
                for hh in range(HPG):
                    n = 4 * g + hh
                    z_low(3 * hh + 1, 0)
                    dve.wait_ge(s("sn_in_psum"), n + 1)
                    for br in range(2):
                        w = (WA, WB)[br]
                        v.tensor_reduce(mx[:, 2 * br:2 * br + 1], w[:, 0:P], AX, ALU.max)
                        v.tensor_reduce(mx[:, 2 * br + 1:2 * br + 2], w[:, P:3 * P], AX, ALU.max)
                    v.tensor_reduce(mx[:, 4:6], WC[:, 0:32].rearrange("p (a b) -> p a b", a=2)[:, :, 0:NCMP], AX, ALU.max)
                    dve.drain()
                    v.tensor_scalar(mx, mx, -1.0, None, ALU.mult).then_inc(s("negmax2"), 1)
                    z_low(3 * hh + 1, 1)
                    dve.wait_ge(s("exps2"), n + 1)
                    v.reciprocal(rc, sm)
                    dve.drain()
                    for k, br in enumerate((1, 2, 0)):
                        v.tensor_tensor(rc[:, 2 * k:2 * k + 2], rc[:, 2 * k:2 * k + 2],
                                        gates[:, :, br, bass.ds(n, 1)].rearrange("p a b -> p (a b)"), ALU.mult)
                    dve.drain()
                    for br in range(2):
                        v.tensor_scalar(Pn[:, br, 0, :], Pn[:, br, 0, :], rc[:, 2 * br:2 * br + 1], None, ALU.mult)
                        v.tensor_scalar(Pn[:, br, 1:3, :], Pn[:, br, 1:3, :], rc[:, 2 * br + 1:2 * br + 2], None, ALU.mult)
                    for qt in range(2):
                        v.scalar_tensor_tensor(Pc[:, qt, :], Pc[:, qt, :], rc[:, 4 + qt:5 + qt], cmp_one[:, qt, :],
                                               ALU.mult, ALU.mult)
                    dve.drain().then_inc(s("probs2"), 1)
                    z_low(3 * hh + 2, 0)
                    z_low(3 * hh + 2, 1)
                    if hh < HPG - 1:
                        z_low(3 * hh + 3, 0)
                    dve.wait_ge(s("sz_ready"), 3 * n + 3)
                    dve.wait_ge(s("on_in_psum"), n + 2)
                    v.tensor_tensor(ot[:, 0, :], WA[:, 0:T], SZn[:, hh % 2, 1, :], ALU.mult)
                    v.tensor_tensor(ot[:, 1, :], WB[:, 0:T], SZn[:, hh % 2, 2, :], ALU.mult)
                    v.tensor_tensor(ot[:, 2, :], WC[:, 0:T], SZn[:, hh % 2, 0, :], ALU.mult)
                    dve.drain().then_inc(s("combined"), 1)
                    v.tensor_tensor(ot[:, 0, :], ot[:, 0, :], ot[:, 1, :], ALU.add)
                    dve.drain()
                    v.tensor_tensor(O[:, bass.ds(n, 1), :], ot[:, 0, :], ot[:, 2, :], ALU.add)
                    dve.drain()
                    if hh < HPG - 1:
                        z_low(3 * hh + 3, 1)
            meet(dve, met)
            split("o", O)
            plain_residual("w_o", mod[:, 176:192])
            meet(dve, met)
            norm_rstd("final2", D)
            norm_scale(SQ, x, V("g_final2"))
            dve.drain().then_inc(s("out_ready"), 1)

        @block.gpsimd
        def _(pool):
            gp = nc.gpsimd
            met = [0]

            def low(stage, i, g, pos, by_column=False, first=DVE_K, between=None):
                for half in range(2):
                    n = half_of(stage, i, g, half)
                    pool.wait_ge(s("hi_ready"), n + 1)
                    gp.tensor_tensor(wlo[:, half, first:8], half_chunk(pos, half, by_column)[:, first:8],
                                     whi[:, half, first:8].bitcast(F32), ALU.subtract).then_inc(s("lo_pool"), 1)
                    if first == 0:
                        pool.drain().then_inc(s("lo_dve"), 1)
                    if half == 1:
                        pool.drain().then_inc(slot_free[pos % R], 2 if first == 0 else 1)
                    if between is not None:
                        between(half)

            def vec_times(stage, i, pos, half):
                if half == 0:
                    loaded(pool, stage, i, pos)
                w = ring[:, pos % R, 8 * half:8 * half + 8, :].rearrange("p k n -> p (k n)")
                gp.tensor_tensor(w, w, cond[:, D // 2 * half:D // 2 * half + D // 2], ALU.mult)\
                    .then_inc(s("prod_ready"), 1)

            def split(name, src):
                for j in range(2):
                    pool.wait_ge(s("hhi_ready"), 4 * SPLITS[name] + j + 1)
                    gp.tensor_tensor(Hlo[:, 4 * j:4 * j + 4, :], src[:, 4 * j:4 * j + 4, :],
                                     Hhi[:, 4 * j:4 * j + 4, :].bitcast(F32), ALU.subtract).then_inc(s("h_ready"), 1)

            def plain(stage):
                body, n = STAGES[stage][0:2]
                with pool.Fori(0, n) as i:
                    for g in range(body):
                        low(stage, i, g, g)

            gp.memset(ones[:], 1.0)
            gp.iota(itmp, [[1, T]], base=0, channel_multiplier=0)
            pool.drain()
            gp.tensor_copy(iota_t[:], itmp)
            gp.tensor_copy(iota16b[:], itmp[:, 0:P])

            def select(out, src, base, pattern, cm_, op, fill):
                pool.drain()
                gp.affine_select(out=out, in_=src, compare_op=op, fill=fill, base=base, pattern=pattern,
                                 channel_multiplier=cm_)

            select(ident[:], ones[:, 0:P], 0, [[-1, P]], 1, ALU.is_equal, 0.0)
            gp.memset(causal16[:], 0.0)
            select(causal16[:], causal16[:], 0, [[-1, P]], 1, ALU.is_ge, NEG)
            gp.tensor_copy(ident16[:], ident[:])
            gp.memset(cmp_neg[:], 0.0)
            select(cmp_neg[:], cmp_neg[:], -31, [[P, 2], [-16, NCMP]], 1, ALU.is_ge, NEG)
            gp.memset(cmp_one[:], 1.0)
            select(cmp_one[:], cmp_one[:], -31, [[P, 2], [-16, NCMP]], 1, ALU.is_ge, 0.0)
            select(in16[:], ones[:, 0:8], 0, [[-16, 8]], 1, ALU.is_ge, 0.0)
            select(in16[:], in16[:], 15, [[16, 8]], -1, ALU.is_ge, 0.0)
            select(in64[:], ones[:, 0:2], 0, [[-64, 2]], 1, ALU.is_ge, 0.0)
            select(in64[:], in64[:], 63, [[64, 2]], -1, ALU.is_ge, 0.0)
            pool.drain()
            i16 = in16[:].rearrange("p (a b) -> p b a", b=2)
            gp.tensor_tensor(par16[:], i16[:, :, 0], i16[:, :, 1], ALU.add)
            gp.tensor_scalar(neg64[:], in64[:], -1.0, None, ALU.mult)
            for k in (2, 3):
                pool.drain()
                gp.tensor_tensor(par16[:], par16[:], i16[:, :, k], ALU.add)
            pool.drain().then_inc(s("consts_ready"), 1)

            def tt(out, a_, b_, op):
                gp.tensor_tensor(out, a_, b_, op)

            pool.wait_ge(s("disc_a"), 1)
            lr, li = bl[:, 0], bl[:, 1]
            dt = bst_.unsqueeze(2).broadcast_to([P, KT, 64])
            tt(e[0], lr, dt, ALU.mult)
            tt(e[1], li, dt, ALU.mult)
            tt(pe_[0], V("lam_re"), pst, ALU.mult)
            tt(pe_[1], V("lam_im"), pst, ALU.mult)
            tt(e[4], lr, lr, ALU.mult)
            tt(e[5], li, li, ALU.mult)
            pool.drain()
            tt(e[4], e[4], e[5], ALU.add)
            pool.drain().then_inc(s("disc_e"), 1)
            for ang, tmp in ((e[1], e[2]), (pe_[1], pe_[2])):
                gp.tensor_scalar(ang, ang, 1.0 / (2 * np.pi), None, ALU.mult)
                pool.drain()
                gp.tensor_scalar(tmp, ang, MAGIC, None, ALU.add)
                pool.drain()
                gp.tensor_scalar(tmp, tmp, MAGIC, None, ALU.subtract)
                pool.drain()
                tt(ang, ang, tmp, ALU.subtract)
                pool.drain()
            gp.tensor_copy(theta[:, 0:PAIRS], pe_[1])
            gp.memset(theta[:, PAIRS:PAIRS + 4], 0.0)
            pool.drain().then_inc(s("disc_b"), 1)
            pool.wait_ge(s("disc_c"), 1)
            tt(e[2], e[0], e[2], ALU.mult)
            tt(e[3], e[0], e[3], ALU.mult)
            pool.drain()
            gp.tensor_scalar(e[2], e[2], 1.0, None, ALU.subtract)
            pool.drain()
            tt(e[0], e[2], lr, ALU.mult)
            tt(e[1], e[3], li, ALU.mult)
            tt(e[5], e[3], lr, ALU.mult)
            tt(e[6], e[2], li, ALU.mult)
            pool.drain()
            tt(e[0], e[0], e[1], ALU.add)
            tt(e[5], e[5], e[6], ALU.subtract)
            pool.wait_ge(s("disc_f"), 1)
            pool.drain()
            tt(e[0], e[0], e[4], ALU.mult)
            tt(e[5], e[5], e[4], ALU.mult)
            pool.drain()
            tt(BB[:, 0], e[0], br_[:, 0], ALU.mult)
            tt(e[1], e[5], br_[:, 1], ALU.mult)
            tt(BB[:, 1], e[0], br_[:, 1], ALU.mult)
            tt(e[2], e[5], br_[:, 0], ALU.mult)
            pool.drain()
            tt(BB[:, 0], BB[:, 0], e[1], ALU.subtract)
            tt(BB[:, 1], BB[:, 1], e[2], ALU.add)
            pool.drain().then_inc(s("disc_done"), 1)
            meet(pool, met)
            split("mix", SQ)
            with pool.Fori(0, HEADS) as i:
                for g in range(5):
                    low("heads", i, g, g)
            meet(pool, met)
            split("merged", SQ)
            with pool.Fori(0, 2) as i:
                for g in range(8):
                    low("w_out", i, g, 5 * (g // 2) + 2 * (g % 2))
            meet(pool, met)
            split("ffn", SQ)
            with pool.Fori(0, 4) as i:
                for h in range(2):
                    for half in range(2):
                        low("topk", i, 2 * h + half, 4 * h + half, first=0)
                    for k in range(2):
                        for half in range(2):
                            vec_times("topk", i, 4 * h + 2 + k, half)
            pool.sem_inc(s("gelu_free"), 2)
            meet(pool, met)
            with pool.Fori(0, 4) as i:
                for u in range(4):
                    for h in range(2):
                        pool.wait_ge(s("hot_equal"), 2 * (4 * i + u) + h + 1)
                        for k in range(3):
                            gp.tensor_tensor(hotB[:, h, :, k, :], eqB[h],
                                             parts[:, k, bass.ds(64 * i + 16 * u + 8 * h, 8)].unsqueeze(2)
                                             .broadcast_to([P, 8, QW]), ALU.mult)
                        pool.drain().then_inc(s("hot_ready"), 1)
            pool.wait_ge(s("cond_ready"), 2)
            with pool.Fori(0, 16) as g:
                for c in range(16):
                    def after(half):
                        if c % 4 == 1:
                            vec_times("peer", g, 3 * (c // 2) + 2, half)

                    low("peer", g, c, 12 * (c // 8) + 3 * (c % 8 // 2) + c % 2, c >= 8, between=after)
            meet(pool, met)
            split("l0", SQ)
            pool.sem_inc(s("q_ready"), 4)
            pool.sem_inc(s("y_pair"), 5)
            pool.sem_inc(s("y_read"), 2)
            meet(pool, met)

            def masks(i, t):
                tile = 2 * i + t
                pool.wait_ge(s("y_pair"), 4 * tile + 1)
                for ri in range(2):
                    gp.tensor_tensor(Bst[:, t % 2, ri], BB[:, ri, bass.ds(tile, 1), :].broadcast_to([P, 2, 64]),
                                     par16[:].unsqueeze(2).broadcast_to([P, 2, 64]), ALU.mult)
                for ri in range(2):
                    gp.tensor_tensor(Cst[:, t % 2, ri],
                                     CC[:, ri, bass.ds(4 * tile, 4), :].unsqueeze(2).broadcast_to([P, 4, 2, 16]),
                                     (in64, neg64)[ri][:].unsqueeze(1).unsqueeze(3).broadcast_to([P, 4, 2, 16]),
                                     ALU.mult)
                pool.drain().then_inc(s("masks_built"), 1)

            def ssm_tile(i, t, last=False):
                tile = 2 * i + t
                for j in range(4):
                    duo, k = j // 2, j % 2
                    pool.wait_ge(s("z_ready"), 4 * tile + j + 1)
                    gp.tensor_tensor(Q1, Z[:, j % 2], tab[:, duo, 0, k:k + 1, :].broadcast_to([P, 2, T]), ALU.mult)
                    gp.tensor_tensor(Q2, Z[:, j % 2], tab[:, duo, 1, k:k + 1, :].broadcast_to([P, 2, T]), ALU.mult)
                    pool.drain()
                    pool.wait_ge(s("y_pair"), 4 * tile + j + 4)
                    gp.tensor_tensor(X[:, j % 2, 0, :], Q1[:, 0, :], Q2[:, 1, :], ALU.subtract)
                    gp.tensor_tensor(X[:, j % 2, 1, :], Q2[:, 0, :], Q1[:, 1, :], ALU.add)
                    pool.drain().then_inc(s("q_ready"), 1)
                    if j == 1 and not last:
                        masks(i, t + 1)

            masks(0, 0)
            ssm_tile(0, 0)
            with pool.Fori(0, 7) as i:
                for t in (1, 2):
                    ssm_tile(i, t)
            ssm_tile(7, 1, last=True)
            split("y", Y)
            plain("glu")
            split("glu", SZ)
            plain("ssm_out")
            meet(pool, met)
            split("kv", SQ)
            plain("kv")
            split("l1", SQ)
            meet(pool, met)
            with pool.Fori(0, KV) as g:
                pool.wait_ge(s("on_in_psum"), 4 * g + 1)
                gp.tensor_copy(Vg, VR[:, bass.ds(g, 1)].rearrange("p g a b c -> p (g a) b c"))
                gp.tensor_copy(VCg[0:NCMP], VCr[0:NCMP, bass.ds(g, 1), :].rearrange("p a b -> p (a b)"))
                pool.drain().then_inc(s("vg_ready"), 1)
                for c in range(16):
                    low("nsa", g, c, c)
            meet(pool, met)
            split("o", O)
            plain("w_o")
            meet(pool, met)


def _tiles(w):
    return np.ascontiguousarray(w.reshape(KT, P, w.shape[1] // P, P).transpose(2, 1, 0, 3))


def _turned(w):
    return np.ascontiguousarray(w.T).reshape(w.shape[1] // P, P, KT, P)


def _cols(v):
    return v.reshape(-1, P).T


def kernel(**inputs):
    import concourse.bacc as bacc
    from concourse.bass_utils import run_bass_kernel_spmd
    i = {k: np.asarray(v) for k, v in inputs.items()}
    w_in = i["w_in"][0]
    heads = [w_in[:, off + P * h:off + P * (h + 1)] for h in range(HEADS) for off in (3080, 0, 1024, 2048, 4104)]
    qg = i["nsa_w_qg_2"][0]
    qz = []
    for g in range(KV):
        qz += [qg[:, P * (HPG * g + h):P * (HPG * g + h + 1)] for h in range(HPG)]
        qz += [qg[:, 2096 + P * (16 * b + HPG * g + h):2096 + P * (16 * b + HPG * g + h + 1)]
               for h in range(HPG) for b in range(3)]
    vecs = dict(
        b_ada=_cols(i["b_ada"]),
        b_mod2=np.concatenate([_cols(i["mod_b_2"]), _cols(i["kv_mod_b_2"])], axis=1),
        g_mix=_cols(i["g_mix"]), g_ffn=_cols(i["g_ffn"]), g_final=_cols(i["g_final"]),
        g_merge=np.concatenate([_cols(i["g_attn_out"]), _cols(i["g_lru_out"])], axis=1),
        g_l0=_cols(i["norm_g_2"][0]), g_l1=_cols(i["norm_g_2"][1]), g_kv=_cols(i["kv_norm_g_2"]),
        g_final2=_cols(i["final_norm_g_2"]),
        conv_w=i["conv_w"][0].reshape(4, HEADS, P).transpose(2, 1, 0).reshape(P, 32),
        conv_b=_cols(i["conv_b"]), lru_b_a=_cols(i["lru_b_a"]), lru_b_x=_cols(i["lru_b_x"]),
        lru_lambda=_cols(i["lru_lambda"]), ssm_d=_cols(i["ssm_d_2"]), b_glu=_cols(i["ssm_b_glu_2"]),
        cmp_b1=_cols(i["cmp_b1_2"]), cmp_b2=_cols(i["cmp_b2_2"]), cmp_pe=_cols(i["cmp_pe_2"]),
        lam_re=i["ssm_lam_re_2"].reshape(PAIRS, P).T, lam_im=i["ssm_lam_im_2"].reshape(PAIRS, P).T)
    arrays = dict(
        x=i["x"][0].reshape(T, KT, P).transpose(2, 1, 0),
        vec=np.concatenate([vecs[n] for n, _ in VEC], axis=1),
        w_f=w_in[:, 3072:3080].reshape(KT, P, 8).transpose(1, 0, 2),
        b_f=i["b_f"].reshape(8, 1),
        w_ada=_turned(i["w_ada"][0]),
        w_in=_tiles(np.concatenate(heads, axis=1)),
        gate_w=np.stack([i["lru_w_a"][0], i["lru_w_x"][0]], axis=2).reshape(HEADS, P, 2, P),
        w_out=_tiles(i["w_out"][0]),
        w_q=_tiles(i["peer_w_q"][0]),
        k12=np.stack([i["peer_k1"][0], i["peer_k2"][0]]).transpose(3, 0, 1, 2),
        c=i["c"], c2=i["c_2"],
        w_mod2=_turned(np.concatenate([i["mod_w_2"][0], i["mod_w_2"][1], i["kv_mod_w_2"]], axis=1)),
        peer_u=i["peer_u"][0].reshape(P, P, KT, P).transpose(1, 3, 2, 0),
        peer_v=i["peer_v"][0].reshape(P, 16, 8, 8, 2 * P).transpose(1, 3, 0, 2, 4).reshape(P, P, KT, P),
        ssm_in=_tiles(i["ssm_w_in_2"][0]),
        step_pair=i["ssm_log_step_2"].reshape(PAIRS, 2).T,
        step_tile=i["ssm_log_step_2"].reshape(KT, 8).T,
        lam_tile=np.stack([i["ssm_lam_re_2"].reshape(KT, 8, 64), i["ssm_lam_im_2"].reshape(KT, 8, 64)]).transpose(2, 0, 1, 3),
        ssm_b=np.stack([i["ssm_b_re_2"], i["ssm_b_im_2"]]).reshape(2, KT, 8, 64, 16).transpose(2, 4, 0, 1, 3).reshape(P, 2, KT, 64),
        ssm_c=np.stack([i["ssm_c_re_2"], i["ssm_c_im_2"]]).reshape(2, PAIRS, 2, 16, 64).transpose(2, 4, 0, 1, 3).reshape(P, 2, PAIRS, 16),
        w_glu=_tiles(i["ssm_w_glu_2"][0]), ssm_out=_tiles(i["ssm_w_out_2"][0]),
        w_kv=_tiles(i["w_kv_2"]),
        cmp_w1=i["cmp_w1_2"].reshape(2, CMP_L, P, P).transpose(2, 0, 1, 3),
        cmp_w2=i["cmp_w2_2"].transpose(1, 0, 2),
        w_gate=qg[:, 2048:2096].reshape(KT, P, 48).transpose(1, 0, 2),
        w_qz=_tiles(np.concatenate(qz, axis=1)), w_o=_tiles(i["nsa_w_o_2"][0]))
    nc = bacc.Bacc("TRN2", target_bir_lowering=False, num_devices=1)
    feed, aps = {}, {}
    for name, value in arrays.items():
        feed["in_" + name] = np.ascontiguousarray(value)
        aps[name] = nc.dram_tensor("in_" + name, value.shape, mybir.dt.from_np(value.dtype), kind="ExternalInput").ap()
    aps["disc"] = nc.dram_tensor("discretised", (P, 2 * KT * 64 + 2 * PAIRS + 4), F32, kind="Internal").ap()
    aps["out"] = nc.dram_tensor("out_0", (P, KT, T), F32, kind="ExternalOutput").ap()
    build(nc, aps)
    res = run_bass_kernel_spmd(nc, [feed], core_ids=[0])
    return np.ascontiguousarray(res.results[0]["out_0"].transpose(2, 1, 0)).reshape(1, T, D)
```
